# Optimizing a Trainium2 kernel written in Bass

```python
import math
import jax, jax.numpy as jnp
from jax import lax
import numpy as np

D_MODEL = 1024
BATCH = 1
SEQ = 1024
DEPTH = 2

GRID_W = 64
HEAD_DIM = D_MODEL // 16
GROUP_W = 4 * HEAD_DIM
MIX_WIDTH = 4 * GROUP_W
N_HEADS_A = 4
N_KV_A = 2
GQA_GROUP = N_HEADS_A // N_KV_A
N_HEADS_B = 4
MLA_Q_RANK = 3 * HEAD_DIM
MLA_KV_RANK = 2 * HEAD_DIM
MLA_NOPE = HEAD_DIM
MLA_ROPE = HEAD_DIM // 2
MLA_V = HEAD_DIM
N_HEADS_C = 4
DIFF_QK = HEAD_DIM // 2
DIFF_V = HEAD_DIM
N_HEADS_D = 4
NA_ROWS_MAX = 8
NA_COLS = 16
D_FF = 4 * D_MODEL
Q_BLOCK = 128
ROPE_BASE = 10000.0
EPS = 1e-6

A_COLS = (N_HEADS_A + 2 * N_KV_A) * HEAD_DIM
B_COLS = MLA_Q_RANK + MLA_KV_RANK + MLA_ROPE
C_COLS = 3 * GROUP_W
D_COLS = 3 * GROUP_W
IN_COLS = A_COLS + B_COLS + C_COLS + D_COLS
SPLITS = (A_COLS, A_COLS + B_COLS, A_COLS + B_COLS + C_COLS)

kernel_name = 'hybrid_parallel_heads_encoder'

def rms_norm(x, g):
    xf = x.astype(jnp.float32)
    y = xf * lax.rsqrt(jnp.mean(xf * xf, axis=-1, keepdims=True) + EPS)
    return (y * g.astype(jnp.float32)).astype(x.dtype)

def rope_angles(pos, dim):
    inv = ROPE_BASE ** (-jnp.arange(0, dim, 2, dtype=jnp.float32) / dim)
    return pos.astype(jnp.float32)[:, None] * inv[None, :]

def apply_rope(x, ang):
    x1, x2 = jnp.split(x, 2, axis=-1)
    cos = jnp.cos(ang).astype(x.dtype)
    sin = jnp.sin(ang).astype(x.dtype)
    return jnp.concatenate([x1 * cos - x2 * sin, x1 * sin + x2 * cos], axis=-1)

def axial_rope(x, ang_row, ang_col):
    xr, xc = jnp.split(x, 2, axis=-1)
    return jnp.concatenate([apply_rope(xr, ang_row), apply_rope(xc, ang_col)], axis=-1)

def alibi_slopes(n_heads):
    return jnp.exp2(-8.0 * jnp.arange(1, n_heads + 1, dtype=jnp.float32) / n_heads)

def neighbourhood_index(n_tokens):
    rows = n_tokens // GRID_W
    kr = min(NA_ROWS_MAX, rows)
    kc = min(NA_COLS, GRID_W)
    t = jnp.arange(n_tokens, dtype=jnp.int32)
    r, c = t // GRID_W, t % GRID_W
    r0 = jnp.clip(r - kr // 2, 0, rows - kr)
    c0 = jnp.clip(c - kc // 2, 0, GRID_W - kc)
    key_r = r0[:, None, None] + jnp.arange(kr, dtype=jnp.int32)[None, :, None]
    key_c = c0[:, None, None] + jnp.arange(kc, dtype=jnp.int32)[None, None, :]
    idx = (key_r * GRID_W + key_c).reshape(n_tokens, kr * kc)
    dr = key_r - r[:, None, None] + (NA_ROWS_MAX - 1)
    dc = key_c - c[:, None, None] + (NA_COLS - 1)
    rel = (dr * (2 * NA_COLS - 1) + dc).reshape(n_tokens, kr * kc)
    return idx, rel

def sweep_query_blocks(block_fn, n_tokens):
    out = lax.map(block_fn, jnp.arange(n_tokens // Q_BLOCK))
    return jnp.moveaxis(out, 0, 1).reshape(out.shape[1], n_tokens, out.shape[-1])

def gqa_axial(u, q_gain, k_gain, ang_row, ang_col):
    b, s, _ = u.shape
    q, k, v = jnp.split(u, [N_HEADS_A * HEAD_DIM, (N_HEADS_A + N_KV_A) * HEAD_DIM], axis=-1)
    q = q.reshape(b, s, N_KV_A, GQA_GROUP, HEAD_DIM).transpose(0, 2, 3, 1, 4)
    k = k.reshape(b, s, N_KV_A, HEAD_DIM).transpose(0, 2, 1, 3)
    v = v.reshape(b, s, N_KV_A, HEAD_DIM).transpose(0, 2, 1, 3)
    q = axial_rope(rms_norm(q, q_gain), ang_row, ang_col)
    k = axial_rope(rms_norm(k, k_gain), ang_row, ang_col)
    scale = HEAD_DIM ** -0.5

    def block(i):
        qb = lax.dynamic_slice_in_dim(q, i * Q_BLOCK, Q_BLOCK, axis=3)
        sc = jnp.einsum('bkgqd,bksd->bkgqs', qb, k, preferred_element_type=jnp.float32) * scale
        p = jax.nn.softmax(sc, axis=-1).astype(v.dtype)
        o = jnp.einsum('bkgqs,bksd->bqkgd', p, v)
        return o.reshape(b, Q_BLOCK, N_HEADS_A * HEAD_DIM)

    return sweep_query_blocks(block, s)

def mla(u, cq_gain, ckv_gain, w_uq, w_ukv, ang_seq):
    b, s, _ = u.shape
    c_q, c_kv, k_rope = jnp.split(u, [MLA_Q_RANK, MLA_Q_RANK + MLA_KV_RANK], axis=-1)
    q = (rms_norm(c_q, cq_gain) @ w_uq).reshape(b, s, N_HEADS_B, MLA_NOPE + MLA_ROPE).transpose(0, 2, 1, 3)
    kv = (rms_norm(c_kv, ckv_gain) @ w_ukv).reshape(b, s, N_HEADS_B, MLA_NOPE + MLA_V).transpose(0, 2, 1, 3)
    q_nope, q_rope = jnp.split(q, [MLA_NOPE], axis=-1)
    k_nope, v = jnp.split(kv, [MLA_NOPE], axis=-1)
    q_rope = apply_rope(q_rope, ang_seq)
    k_rope = apply_rope(k_rope, ang_seq)
    scale = (MLA_NOPE + MLA_ROPE) ** -0.5

    def block(i):
        qn = lax.dynamic_slice_in_dim(q_nope, i * Q_BLOCK, Q_BLOCK, axis=2)
        qr = lax.dynamic_slice_in_dim(q_rope, i * Q_BLOCK, Q_BLOCK, axis=2)
        sc = (jnp.einsum('bhqd,bhsd->bhqs', qn, k_nope, preferred_element_type=jnp.float32)
              + jnp.einsum('bhqr,bsr->bhqs', qr, k_rope, preferred_element_type=jnp.float32)) * scale
        p = jax.nn.softmax(sc, axis=-1).astype(v.dtype)
        o = jnp.einsum('bhqs,bhsd->bqhd', p, v)
        return o.reshape(b, Q_BLOCK, N_HEADS_B * MLA_V)

    return sweep_query_blocks(block, s)

def diff_attention(u, lq1, lk1, lq2, lk2, g_head, slopes, lambda_init):
    b, s, _ = u.shape
    q, k, v = jnp.split(u, [GROUP_W, 2 * GROUP_W], axis=-1)
    q = q.reshape(b, s, N_HEADS_C, 2, DIFF_QK).transpose(0, 2, 3, 1, 4)
    k = k.reshape(b, s, N_HEADS_C, 2, DIFF_QK).transpose(0, 2, 3, 1, 4)
    v = v.reshape(b, s, N_HEADS_C, DIFF_V).transpose(0, 2, 1, 3)
    f32 = jnp.float32
    lam = (jnp.exp(jnp.sum(lq1.astype(f32) * lk1.astype(f32)))
           - jnp.exp(jnp.sum(lq2.astype(f32) * lk2.astype(f32))) + lambda_init)
    t = jnp.arange(s, dtype=jnp.int32)
    scale = DIFF_QK ** -0.5

    def block(i):
        qb = lax.dynamic_slice_in_dim(q, i * Q_BLOCK, Q_BLOCK, axis=3)
        qpos = i * Q_BLOCK + jnp.arange(Q_BLOCK, dtype=jnp.int32)
        dist = jnp.abs(qpos[:, None] - t[None, :]).astype(f32)
        bias = -slopes[:, None, None, None] * dist
        sc = jnp.einsum('bhmqd,bhmsd->bhmqs', qb, k, preferred_element_type=f32) * scale + bias
        p = jax.nn.softmax(sc, axis=-1)
        a = (p[:, :, 0] - lam * p[:, :, 1]).astype(v.dtype)
        o = jnp.einsum('bhqs,bhsd->bqhd', a, v)
        o = rms_norm(o, g_head) * (1.0 - lambda_init)
        return o.reshape(b, Q_BLOCK, N_HEADS_C * DIFF_V)

    return sweep_query_blocks(block, s)

def neighbourhood_attention(u, rel_bias, na_idx, na_rel):
    b, s, _ = u.shape
    q, k, v = jnp.split(u, [GROUP_W, 2 * GROUP_W], axis=-1)
    q = q.reshape(b, s, N_HEADS_D, HEAD_DIM)
    k = k.reshape(b, s, N_HEADS_D, HEAD_DIM)
    v = v.reshape(b, s, N_HEADS_D, HEAD_DIM)
    bias_flat = rel_bias.reshape(N_HEADS_D, -1).astype(jnp.float32)
    scale = HEAD_DIM ** -0.5

    def block(i):
        qb = lax.dynamic_slice_in_dim(q, i * Q_BLOCK, Q_BLOCK, axis=1)
        idx = lax.dynamic_slice_in_dim(na_idx, i * Q_BLOCK, Q_BLOCK, axis=0)
        rel = lax.dynamic_slice_in_dim(na_rel, i * Q_BLOCK, Q_BLOCK, axis=0)
        kb = jnp.take(k, idx, axis=1)
        vb = jnp.take(v, idx, axis=1)
        sc = (jnp.einsum('bqhd,bqnhd->bhqn', qb, kb, preferred_element_type=jnp.float32) * scale
              + jnp.take(bias_flat, rel, axis=1))
        p = jax.nn.softmax(sc, axis=-1).astype(v.dtype)
        o = jnp.einsum('bhqn,bqnhd->bqhd', p, vb)
        return o.reshape(b, Q_BLOCK, N_HEADS_D * HEAD_DIM)

    return sweep_query_blocks(block, s)

def setup_inputs(seed: int = 0) -> dict:
    key = jax.random.key(seed)
    ks = jax.random.split(key, 26)
    L = DEPTH

    def dense(k, fan_in, fan_out):
        return jax.random.normal(k, (L, fan_in, fan_out), jnp.float32) * fan_in ** -0.5

    def gain(k, dim):
        return 1.0 + 0.02 * jax.random.normal(k, (L, dim), jnp.float32)

    def small(k, shape, sc):
        return sc * jax.random.normal(k, shape, jnp.float32)

    return {
        'x': jax.random.normal(ks[0], (BATCH, SEQ, D_MODEL), jnp.float32),
        'norm_mix_pre': gain(ks[1], D_MODEL),
        'norm_mix_post': gain(ks[2], D_MODEL),
        'norm_mlp_pre': gain(ks[3], D_MODEL),
        'norm_mlp_post': gain(ks[4], D_MODEL),
        'w_in': dense(ks[5], D_MODEL, IN_COLS),
        'a_q_norm': gain(ks[6], HEAD_DIM),
        'a_k_norm': gain(ks[7], HEAD_DIM),
        'b_cq_norm': gain(ks[8], MLA_Q_RANK),
        'b_ckv_norm': gain(ks[9], MLA_KV_RANK),
        'b_w_uq': dense(ks[10], MLA_Q_RANK, N_HEADS_B * (MLA_NOPE + MLA_ROPE)),
        'b_w_ukv': dense(ks[11], MLA_KV_RANK, N_HEADS_B * (MLA_NOPE + MLA_V)),
        'c_lambda_q1': small(ks[12], (L, DIFF_QK), 0.1),
        'c_lambda_k1': small(ks[13], (L, DIFF_QK), 0.1),
        'c_lambda_q2': small(ks[14], (L, DIFF_QK), 0.1),
        'c_lambda_k2': small(ks[15], (L, DIFF_QK), 0.1),
        'd_rel_bias': small(ks[16], (L, N_HEADS_D, 2 * NA_ROWS_MAX - 1, 2 * NA_COLS - 1), 0.1),
        'g_out_a': gain(ks[17], GROUP_W),
        'g_out_b': gain(ks[18], GROUP_W),
        'g_out_c': gain(ks[19], DIFF_V),
        'g_out_d': gain(ks[20], GROUP_W),
        'w_out': dense(ks[21], MIX_WIDTH, D_MODEL),
        'w_up': dense(ks[22], D_MODEL, D_FF),
        'w_down': dense(ks[23], D_FF, D_MODEL),
    }

def reference(x, norm_mix_pre, norm_mix_post, norm_mlp_pre, norm_mlp_post, w_in,
              a_q_norm, a_k_norm, b_cq_norm, b_ckv_norm, b_w_uq, b_w_ukv,
              c_lambda_q1, c_lambda_k1, c_lambda_q2, c_lambda_k2, d_rel_bias,
              g_out_a, g_out_b, g_out_c, g_out_d, w_out, w_up, w_down):
    n_tokens = x.shape[1]
    t = jnp.arange(n_tokens, dtype=jnp.int32)
    ang_row = rope_angles(t // GRID_W, HEAD_DIM // 2)
    ang_col = rope_angles(t % GRID_W, HEAD_DIM // 2)
    ang_seq = rope_angles(t, MLA_ROPE)
    slopes = alibi_slopes(N_HEADS_C)
    na_idx, na_rel = neighbourhood_index(n_tokens)

    for l in range(DEPTH):
        h = rms_norm(x, norm_mix_pre[l])
        u = h @ w_in[l]
        ua, ub, uc, ud = jnp.split(u, SPLITS, axis=-1)
        oa = rms_norm(gqa_axial(ua, a_q_norm[l], a_k_norm[l], ang_row, ang_col), g_out_a[l])
        ob = rms_norm(mla(ub, b_cq_norm[l], b_ckv_norm[l], b_w_uq[l], b_w_ukv[l], ang_seq), g_out_b[l])
        lambda_init = 0.8 - 0.6 * math.exp(-0.3 * l)
        oc = diff_attention(uc, c_lambda_q1[l], c_lambda_k1[l], c_lambda_q2[l], c_lambda_k2[l],
                            g_out_c[l], slopes, lambda_init)
        od = rms_norm(neighbourhood_attention(ud, d_rel_bias[l], na_idx, na_rel), g_out_d[l])
        mix = jnp.concatenate([oa, ob, oc, od], axis=-1) @ w_out[l]
        x = x + rms_norm(mix, norm_mix_post[l])
        h = rms_norm(x, norm_mlp_pre[l])
        f = jnp.square(jax.nn.relu(h @ w_up[l])) @ w_down[l]
        x = x + rms_norm(f, norm_mlp_post[l])
    return x


_drawn_inputs = setup_inputs


def setup_inputs(seed=0):
    import zlib

    import numpy as np

    out = dict(_drawn_inputs(seed))
    spreads = {}
    factors = {'norm_mix_post': 2.98,
     'norm_mlp_pre': 3.546,
     'norm_mlp_post': 3.646,
     'a_q_norm': 7.639,
     'a_k_norm': 7.103,
     'b_cq_norm': 8.0,
     'b_ckv_norm': 3.879,
     'c_lambda_q2': 3.657,
     'c_lambda_k2': 2.975,
     'g_out_a': 5.992,
     'g_out_b': 6.314,
     'g_out_c': 8.0,
     'g_out_d': 6.119}
    for name, (base, spread) in spreads.items():
        noise = np.random.default_rng([zlib.crc32(name.encode()), seed]).standard_normal(out[name].shape)
        drawn = base * np.exp(spread * noise) if base else spread * noise
        out[name] = __import__('jax').numpy.asarray(drawn.astype(out[name].dtype))
    for name, factor in factors.items():
        out[name] = (out[name] * factor).astype(out[name].dtype)
    return out
```

```python
from contextlib import ExitStack
import math

import numpy as np
import concourse.bass as bass
from concourse import mybir

ALU = mybir.AluOpType
ACT = mybir.ActivationFunctionType
AX_X = mybir.AxisListType.X
F32 = mybir.dt.float32
F32R = mybir.dt.float32r

P = 128
SEQ, D, DEPTH = 1024, 1024, 2
NT = SEQ // P
KT = D // P
HALF = 512
HD = 64
GRID_W = 64
NHEAD = 4
B_Q, B_KV, B_ROPE = 3 * HD, 2 * HD, HD // 2
A0 = 0
B0 = A0 + 8 * HD
C0 = B0 + B_Q + B_KV + B_ROPE
D0 = C0 + 12 * HD
FF = 4 * D
FF_CHUNK = 1024
NA_R, NA_C = 8, 16
REL_C = 2 * NA_C - 1
REL_R = 2 * NA_R - 1
REL_N = NHEAD * REL_R * REL_C
EPS = 1e-6
NEG = -1e30
NEG_START = -3.0e38
REL_PAD = 64
REL_ROW = REL_N + 2 * REL_PAD
SKEW = 2 * GRID_W - 1


def shape_constants():
    t = np.arange(SEQ)

    def angles(pos, dim):
        inv = np.float32(10000.0) ** (-np.arange(0, dim, 2, dtype=np.float32) / np.float32(dim))
        return pos.astype(np.float32)[:, None] * inv[None, :].astype(np.float32)

    def both(ang):
        c, s = np.cos(ang), np.sin(ang)
        return np.concatenate([c, c], 1), np.concatenate([-s, s], 1)

    cr, sr = both(angles(t // GRID_W, HD // 2))
    cc, sc = both(angles(t % GRID_W, HD // 2))
    cb, sb = both(angles(t, B_ROPE))
    col = np.arange(GRID_W)
    first = np.clip(col - NA_C // 2, 0, GRID_W - NA_C)
    seen = (col[None, :] >= first[:, None]) & (col[None, :] < first[:, None] + NA_C)
    col_mask = np.where(seen, 0.0, NEG)
    row_mask = np.zeros((2, 10))
    row_mask[0, 8:] = NEG
    row_mask[1, 0] = NEG
    row_mask[1, 9] = NEG
    p, m = np.arange(P)[:, None], np.arange(2 * SEQ - P)[None, :]
    li = [0.8 - 0.6 * math.exp(-0.3 * l) for l in range(DEPTH)]
    tables = {
        "cos_a": np.concatenate([cr, cc], 1), "sin_a": np.concatenate([sr, sc], 1),
        "cos_sin_b": np.concatenate([cb.T, sb.T], 0),
        "col_mask": np.concatenate([col_mask, col_mask], 0),
        "row_mask": np.repeat(row_mask, GRID_W, 0),
        "neg_dist": -np.abs(p + (SEQ - P) - m),
        "slopes": np.array([[2.0 ** (-8.0 * (h + 1) / NHEAD) for h in range(NHEAD)]]),
        "lambda_init": np.array([[v, 1.0 - v] for v in li]),
    }
    return {k: np.ascontiguousarray(v, dtype=np.float32) for k, v in tables.items()}


SEMS = """w_landed0 w_landed1 w_hi w_lo gemm_done gemm_out tt_done tt_hi tt_lo
 x_landed0 x_landed1 gain_landed x_stored square_done norm_done gain_done hi_done lo_done tr_done ytr_done
 ysq_done ynorm_done xadd_done zero_done ft_free dve_step act_step pool_step pe_step const_landed
 scores_done max_done exp_done ptr_done pt_hi pt_lo pv_done ot_done o_done map_done
 stack_landed root_done yroot_done relu_done sq_done up_hi up_lo acc_done copy_landed prep_done prep2_done mix_sq""".split()


class Sems:

    def __init__(self, ctx, nc):
        handles = [ctx.enter_context(nc.semaphore(n)) for n in SEMS]
        self.by_name = dict(zip(SEMS, handles))
        nums = [h.num for h in handles]
        self.range = range(min(nums), max(nums) + 1)

    def __getitem__(self, name):
        return self.by_name[name]


def build(nc, a, out):
    with ExitStack() as ctx:
        S = Sems(ctx, nc)
        x_copied = ctx.enter_context(nc.semaphore("x_copied"))
        skew_landed = ctx.enter_context(nc.semaphore("skew_landed"))

        def sb(c, name, shape, dt=F32):
            return c.enter_context(nc.sbuf_tensor(name, shape, dt))

        def ps(c, name, shape, dt=F32):
            return c.enter_context(nc.psum_tensor(name, shape, dt))

        def end_stage():
            nc.all_engine_barrier(sems_to_clear=S.range)

        ident = sb(ctx, "ident", [P, P])
        fold = sb(ctx, "fold", [P, HD])
        ones = sb(ctx, "ones", [P, P])
        h_hi = sb(ctx, "h_hi", [P, KT, SEQ], F32R)
        h_lo = sb(ctx, "h_lo", [P, KT, SEQ], F32R)
        eps_col = sb(ctx, "eps_col", [P, 1])
        rel_scratch = nc.dram_tensor("rel_scratch", (DEPTH, REL_ROW), F32).ap()
        skew = nc.dram_tensor("skew", (DEPTH, NHEAD * REL_R, GRID_W, SKEW), F32).ap()

        with ExitStack() as c, nc.Block() as block:
            zero = sb(c, "zero", [DEPTH, REL_PAD])

            @block.sync
            def _(sp):
                sp.dma_start(out, a["x"]).then_inc(x_copied, 16)

            @block.scalar
            def _(act):
                act.wait_ge(S["const_landed"], 1)
                for at in (0, REL_PAD + REL_N):
                    act.dma_start(rel_scratch[:, at:at + REL_PAD], zero[:, :]).then_inc(S["copy_landed"], 16)
                act.dma_start(rel_scratch[:, REL_PAD:REL_PAD + REL_N], a["d_rel_bias"]).then_inc(S["copy_landed"], 16)
                act.wait_ge(S["copy_landed"], 48)
                for l in range(DEPTH):
                    src = bass.AP(rel_scratch.tensor, l * REL_ROW + REL_PAD + NA_C - GRID_W,
                                  [[REL_C, NHEAD * REL_R], [0, GRID_W], [1, SKEW]])
                    act.dma_start(skew[l], src).then_inc(skew_landed, 16)

            @block.vector
            def _(dve):
                nc.vector.memset(zero[:, :], 0.0).then_inc(S["const_landed"], 1)
                nc.vector.memset(ones[:, :], 1.0)
                nc.vector.memset(eps_col[:, :], EPS)

            @block.gpsimd
            def _(pool):
                nc.gpsimd.memset(ident[:, :], 0.0).then_inc(S["pool_step"], 1)
                nc.gpsimd.memset(fold[:, :], 0.0).then_inc(S["pool_step"], 1)
                pool.wait_ge(S["pool_step"], 2)
                nc.gpsimd.affine_select(out=ident[:, :], in_=ident[:, :], compare_op=ALU.not_equal, fill=1.0,
                                        base=0, pattern=[[-1, P]], channel_multiplier=1)
                nc.gpsimd.affine_select(out=fold[:, :], in_=fold[:, :], compare_op=ALU.not_equal, fill=1.0,
                                        base=0, pattern=[[-1, HD]], channel_multiplier=1).then_inc(S["pool_step"], 1)
                pool.wait_ge(S["pool_step"], 3)
                nc.gpsimd.affine_select(out=fold[:, :], in_=fold[:, :], compare_op=ALU.not_equal, fill=1.0,
                                        base=-HD, pattern=[[-1, HD]], channel_multiplier=1)
        end_stage()

        def weight_ring(c, tag):
            return (sb(c, f"w_raw_{tag}", [P, 2, KT, P]), sb(c, f"w_h_{tag}", [P, 2, KT, P], F32R),
                    sb(c, f"w_l_{tag}", [P, 2, KT, P], F32R))

        def load_weights(sp, ring, units, base=0, looped=False):
            raw = ring[0]
            for u, (pieces, _) in enumerate(units):
                if u >= 2 or looped:
                    sp.wait_ge(S["w_lo"], base + (u - 1))
                for dst, src in pieces:
                    sp.dma_start(dst(raw[:, u % 2]), src).then_inc(S[f"w_landed{u % 2}"], 16)

        def landed(units, u):
            return 16 * sum(len(units[v][0]) for v in range(u % 2, u + 1, 2))

        def split_hi(act, ring, units, u, base=0, looped=False, landed_base=0):
            raw, hi, _ = ring
            act.wait_ge(S[f"w_landed{u % 2}"], landed_base + landed(units, u))
            if u >= 2 or looped:
                act.wait_ge(S["gemm_done"], base + (u - 1))
            for i, (rows, cols) in enumerate(units[u][1]):
                last = nc.scalar.activation(hi[0:rows, u % 2, cols, :], raw[0:rows, u % 2, cols, :], ACT.Copy)
            last.then_inc(S["w_hi"], 1)

        def split_lo(pool, ring, units, u, units_before=0):
            raw, hi, lo = ring
            pool.wait_ge(S["w_hi"], units_before + (u + 1))
            for rows, cols in units[u][1]:
                last = nc.gpsimd.tensor_tensor(lo[0:rows, u % 2, cols, :], raw[0:rows, u % 2, cols, :],
                                               hi[0:rows, u % 2, cols, :], ALU.subtract)
            last.then_inc(S["w_lo"], 1)

        def products(pe, dst, ring, units, u, x_hi, x_lo, base=0, before_last=None):
            _, hi, lo = ring
            pe.wait_ge(S["w_lo"], base + (u + 1))
            rows_of = [rows for rows, cols in units[u][1] for _ in range(cols.start, cols.stop)]
            for k, rows in enumerate(rows_of):
                if before_last and k == len(rows_of) - 1:
                    before_last()
                wh, wl = hi[0:rows, u % 2, k, :], lo[0:rows, u % 2, k, :]
                for n in range(2):
                    o = dst[:, n * HALF:(n + 1) * HALF]
                    tok = slice(n * HALF, (n + 1) * HALF)
                    nc.tensor.matmul(o, wh, x_hi[0:rows, k, tok], start=(k == 0), stop=False)
                    nc.tensor.matmul(o, wh, x_lo[0:rows, k, tok], start=False, stop=False)
                for n in range(2):
                    last = nc.tensor.matmul(dst[:, n * HALF:(n + 1) * HALF], wl,
                                            x_hi[0:rows, k, n * HALF:(n + 1) * HALF],
                                            start=False, stop=(k == len(rows_of) - 1))
            last.then_inc(S["gemm_done"], 1)

        FULL = [(P, slice(0, KT))]

        def full_unit(src):
            return ([(lambda w: w, src.rearrange("(k p) n -> p k n", p=P))], FULL)

        def transposes(pe, dst, src_of, n=8):
            for i in range(n):
                last = nc.tensor.transpose(dst[:, i * P:(i + 1) * P], src_of(i), ident[:, :])
            return last

        def row_vector(src):
            return src.partition_broadcast(P)

        def root(act, ss, width):
            return nc.scalar.activation(ss, ss, ACT.Sqrt, scale=1.0 / width, bias=eps_col[:, 0:1])

        def rstd(dve, ss, step):
            nc.vector.reciprocal(ss, ss).then_inc(S["dve_step"], 1)
            dve.wait_ge(S["dve_step"], step + 1)
            return step + 1

        def norm_stage(tag, ft, post_gain, pre_gain):
            post, pre = ft is not None, pre_gain is not None
            with ExitStack() as c, nc.Block() as block:
                x = sb(c, f"x_{tag}", [P, 2, D])
                junk = sb(c, f"junk_{tag}", [P, D])
                stat = sb(c, f"stat_{tag}", [P, 2, NT])
                if post:
                    g_post = sb(c, f"g_post_{tag}", [P, D])
                    y = sb(c, f"y_{tag}", [P, 2, D])
                    y_ps = ps(c, f"y_ps_{tag}", [P, 2, D])
                if pre:
                    g_pre = sb(c, f"g_pre_{tag}", [P, D])
                    hn = sb(c, f"hn_{tag}", [P, 2, D])
                    h_ps = ps(c, f"h_ps_{tag}", [P, 2, D])
                gains = 16 * (post + pre)

                @block.sync
                def _(sp):
                    if post:
                        sp.dma_start(g_post[:, :], row_vector(post_gain)).then_inc(S["gain_landed"], 16)
                    if pre:
                        sp.dma_start(g_pre[:, :], row_vector(pre_gain)).then_inc(S["gain_landed"], 16)
                    sp.wait_ge(x_copied, 16)

                    def load(t):
                        if t >= 2:
                            if post:
                                sp.wait_ge(S["x_stored"], 16 * (t - 1))
                            if pre:
                                sp.wait_ge(S["norm_done"], t - 1)
                        sp.dma_start(x[:, t % 2, :], out[t * P:(t + 1) * P, :]).then_inc(S[f"x_landed{t % 2}"], 16)

                    for t in range(NT + 1):
                        if t >= 1 and post:
                            if t < NT:
                                load(t)
                            sp.wait_ge(S["xadd_done"], t)
                            sp.dma_start(out[(t - 1) * P:t * P, :], x[:, (t - 1) % 2, :]).then_inc(S["x_stored"], 16)
                        elif t < NT:
                            load(t)
                    if post:
                        sp.wait_ge(S["x_stored"], 16 * NT)

                @block.gpsimd
                def _(pool):
                    if post:
                        for t in range(NT):
                            pool.wait_ge(S[f"x_landed{t % 2}"], 16 * (t // 2 + 1))
                            pool.wait_ge(S["ynorm_done"], t + 1)
                            nc.gpsimd.tensor_tensor(x[:, t % 2, :], x[:, t % 2, :], y[:, t % 2, :],
                                                    ALU.add).then_inc(S["xadd_done"], 1)

                @block.tensor
                def _(pe):
                    for t in range(NT + 1):
                        if post and t < NT:
                            if t >= 2:
                                pe.wait_ge(S["ynorm_done"], t - 1)
                            transposes(pe, y_ps[:, t % 2, :], lambda m, t=t: ft[:, m, t * P:(t + 1) * P]) \
                                .then_inc(S["ytr_done"], 1)
                        if pre and t >= 1:
                            pe.wait_ge(S["norm_done"], t)
                            if t >= 3:
                                pe.wait_ge(S["lo_done"], t - 2)
                            transposes(pe, h_ps[:, (t - 1) % 2, :],
                                       lambda k, t=t: hn[:, (t - 1) % 2, k * P:(k + 1) * P]) \
                                .then_inc(S["tr_done"], 1)

                @block.scalar
                def _(act):
                    for t in range(NT + 2):
                        if post and t < NT:
                            act.wait_ge(S["ytr_done"], t + 1)
                            nc.scalar.activation(junk[:, :], y_ps[:, t % 2, :], ACT.Square,
                                                 accum_out=stat[:, 0, t:t + 1]).then_inc(S["ysq_done"], 1)
                            act.wait_ge(S["ysq_done"], t + 1)
                            root(act, stat[:, 0, t:t + 1], D).then_inc(S["yroot_done"], 1)
                        if pre and 1 <= t <= NT:
                            if post:
                                act.wait_ge(S["xadd_done"], t)
                            else:
                                act.wait_ge(S[f"x_landed{(t - 1) % 2}"], 16 * ((t - 1) // 2 + 1))
                            nc.scalar.activation(junk[:, :], x[:, (t - 1) % 2, :], ACT.Square,
                                                 accum_out=stat[:, 1, t - 1:t]).then_inc(S["square_done"], 1)
                            act.wait_ge(S["square_done"], t)
                            root(act, stat[:, 1, t - 1:t], D).then_inc(S["root_done"], 1)
                        if pre and t >= 2:
                            act.wait_ge(S["tr_done"], t - 1)
                            nc.scalar.activation(h_hi[:, :, (t - 2) * P:(t - 1) * P],
                                                 h_ps[:, (t - 2) % 2, :].rearrange("p (k n) -> p k n", k=KT),
                                                 ACT.Copy).then_inc(S["hi_done"], 1)

                @block.vector
                def _(dve):
                    step = 0
                    dve.wait_ge(S["gain_landed"], gains)
                    for t in range(NT + 2):
                        if post and t < NT:
                            dve.wait_ge(S["yroot_done"], t + 1)
                            step = rstd(dve, stat[:, 0, t:t + 1], step)
                            if t >= 2:
                                dve.wait_ge(S["xadd_done"], t - 1)
                            nc.vector.scalar_tensor_tensor(out=y[:, t % 2, :], in0=y_ps[:, t % 2, :],
                                                           scalar=stat[:, 0, t:t + 1], in1=g_post[:, :],
                                                           op0=ALU.mult, op1=ALU.mult).then_inc(S["ynorm_done"], 1)
                        if pre and 1 <= t <= NT:
                            s = t - 1
                            dve.wait_ge(S["root_done"], t)
                            step = rstd(dve, stat[:, 1, s:t], step)
                            if t >= 3:
                                dve.wait_ge(S["tr_done"], t - 2)
                            nc.vector.scalar_tensor_tensor(out=hn[:, s % 2, :], in0=x[:, s % 2, :],
                                                           scalar=stat[:, 1, s:t], in1=g_pre[:, :],
                                                           op0=ALU.mult, op1=ALU.mult).then_inc(S["norm_done"], 1)
                        if pre and t >= 2:
                            s = t - 2
                            dve.wait_ge(S["hi_done"], s + 1)
                            nc.vector.tensor_tensor(h_lo[:, :, s * P:(s + 1) * P],
                                                    h_ps[:, s % 2, :].rearrange("p (k n) -> p k n", k=KT),
                                                    h_hi[:, :, s * P:(s + 1) * P], ALU.subtract) \
                                .then_inc(S["lo_done"], 1)
            end_stage()

        def attention_stage(tag, maps, tiles, group, mix_cols, mix, combine=None):
            n_all = len(maps) * NT
            kmax = max(t[1] for t in tiles)
            with ExitStack() as c, nc.Block() as block:
                prob = sb(c, f"prob_{tag}", [P, 2, kmax * P])
                pt_h = sb(c, f"pt_h_{tag}", [P, 2, kmax, group * P], F32R)
                pt_l = sb(c, f"pt_l_{tag}", [P, 2, kmax, group * P], F32R)
                ot = sb(c, f"ot_{tag}", [P, 2, group * P])
                nmax = sb(c, f"nmax_{tag}", [P, n_all])
                rmax = sb(c, f"rmax_{tag}", [P, n_all])
                z = sb(c, f"z_{tag}", [P, n_all])
                part = sb(c, f"part_{tag}", [P, 2, NT, HD])
                s_ps = ps(c, f"s_ps_{tag}", [P, 2, 2 * HALF])
                t_ps = ps(c, f"t_ps_{tag}", [P, 2, HALF])
                ot_ps = ps(c, f"ot_ps_{tag}", [P, HALF])
                o_ps = ps(c, f"o_ps_{tag}", [P, NT, HD])

                def seq(n):
                    return n // NT, n % NT

                piece_end = [0]
                for n in range(n_all):
                    piece_end.append(piece_end[-1] + -(-tiles[n % NT][1] // 4))

                def pieces(n):
                    cnt = tiles[n % NT][1]
                    return [(piece_end[n] + b, 4 * b, min(cnt, 4 * b + 4)) for b in range(-(-cnt // 4))]

                def turned(p, k0, k1):
                    return t_ps[:, p % 2, 0:(k1 - k0) * P].rearrange("p (k n) -> p k n", k=k1 - k0)

                @block.tensor
                def _(pe):
                    def scores(n):
                        m, i = seq(n)
                        first, cnt = tiles[i][0:2]
                        if n >= 2:
                            pe.wait_ge(S["exp_done"], n - 1)
                        q_of, k_of = maps[m][0], maps[m][1]
                        for at in range(0, cnt * P, HALF):
                            w = min(HALF, cnt * P - at)
                            for j, (q, k) in enumerate(zip(q_of, k_of)):
                                last = nc.tensor.matmul(s_ps[:, n % 2, at:at + w], q(i),
                                                        k(first * P + at, first * P + at + w),
                                                        start=(j == 0), stop=(j == len(q_of) - 1))
                        last.then_inc(S["scores_done"], 1)

                    def turn(n):
                        m, i = seq(n)
                        pe.wait_ge(S["exp_done"], n + 1)
                        for p, k0, k1 in pieces(n):
                            if p >= 2:
                                pe.wait_ge(S["pt_lo"], p - 1)
                            transposes(pe, t_ps[:, p % 2, :],
                                       lambda k: prob[:, n % 2, (k0 + k) * P:(k0 + k + 1) * P], k1 - k0) \
                                .then_inc(S["ptr_done"], 1)

                    def values(g):
                        m, i = seq(g * group)
                        first, cnt = tiles[i][0:2]
                        pe.wait_ge(S["pt_lo"], piece_end[(g + 1) * group])
                        if g >= 1:
                            pe.wait_ge(S["ot_done"], g)
                        v = maps[m][2]
                        for k in range(cnt):
                            for j, pt in enumerate((pt_h, pt_l)):
                                last = nc.tensor.matmul(ot_ps[:, 0:group * P], v[:, first + k, :],
                                                        pt[:, g % 2, k, :], start=(k == 0 and j == 0),
                                                        stop=(k == cnt - 1 and j == 1))
                        last.then_inc(S["pv_done"], 1)

                    def finish(g):
                        m, i = seq(g * group)
                        pe.wait_ge(S["ot_done"], g + 1)
                        if m >= 1 and i == 0:
                            pe.wait_ge(S["map_done"], m)
                        for j in range(group):
                            last = nc.tensor.matmul(o_ps[:, i + j, :], ot[:, g % 2, j * P:(j + 1) * P],
                                                    fold[:, :], start=True, stop=True)
                        last.then_inc(S["o_done"], 1)

                    scores(0)
                    scores(1)
                    for n in range(n_all + 2 * group):
                        if n + 2 < n_all:
                            scores(n + 2)
                        if n < n_all:
                            turn(n)
                        if n >= group and n % group == 0 and n // group <= n_all // group:
                            values(n // group - 1)
                        if n >= 2 * group and n % group == 0:
                            finish(n // group - 2)

                @block.scalar
                def _(act):
                    def split(n):
                        m, i = seq(n)
                        g, j = n // group, n % group
                        if j == 0 and g >= 2:
                            act.wait_ge(S["pv_done"], g - 1)
                        for p, k0, k1 in pieces(n):
                            act.wait_ge(S["ptr_done"], p + 1)
                            nc.scalar.activation(pt_h[:, g % 2, k0:k1, j * P:(j + 1) * P], turned(p, k0, k1),
                                                 ACT.Copy).then_inc(S["pt_hi"], 1)

                    def lift(g):
                        act.wait_ge(S["pv_done"], g + 1)
                        if g >= 2:
                            act.wait_ge(S["o_done"], g - 1)
                        nc.scalar.activation(ot[:, g % 2, :], ot_ps[:, 0:group * P], ACT.Copy) \
                            .then_inc(S["ot_done"], 1)

                    def exponential(n):
                        cnt = tiles[n % NT][1]
                        act.wait_ge(S["max_done"], n + 1)
                        if n >= 2:
                            act.wait_ge(S["ptr_done"], piece_end[n - 1])
                        nc.scalar.activation(prob[:, n % 2, 0:cnt * P], s_ps[:, n % 2, 0:cnt * P], ACT.Exp,
                                             bias=nmax[:, n:n + 1], accum_out=z[:, n:n + 1]) \
                            .then_inc(S["exp_done"], 1)

                    exponential(0)
                    for n in range(n_all + 2 * group):
                        if n + 1 < n_all:
                            exponential(n + 1)
                        if n < n_all:
                            split(n)
                        if n >= 2 * group - 1 and (n + 1) % group == 0 and (n + 1) // group - 2 < n_all // group:
                            lift((n + 1) // group - 2)

                @block.vector
                def _(dve):
                    step = [0]

                    def after(ins):
                        step[0] += 1
                        ins.then_inc(S["dve_step"], 1)
                        dve.wait_ge(S["dve_step"], step[0])

                    def maximum(n):
                        m, i = seq(n)
                        first, cnt, bias = tiles[i]
                        dve.wait_ge(S["scores_done"], n + 1)
                        s = s_ps[:, n % 2, 0:cnt * P]
                        if bias is None:
                            nc.vector.tensor_reduce(nmax[:, n:n + 1], s, AX_X, ALU.max, negate=True) \
                                .then_inc(S["max_done"], 1)
                        else:
                            after(nc.vector.tensor_tensor_reduce(out=s, in0=s, in1=bias(m), scale=1.0,
                                                                 scalar=NEG_START, op0=ALU.add, op1=ALU.max,
                                                                 accum_out=rmax[:, n:n + 1]))
                            nc.vector.tensor_scalar(nmax[:, n:n + 1], rmax[:, n:n + 1], -1.0, None, ALU.mult) \
                                .then_inc(S["max_done"], 1)

                    def split(n):
                        m, i = seq(n)
                        g, j = n // group, n % group
                        for p, k0, k1 in pieces(n):
                            dve.wait_ge(S["pt_hi"], p + 1)
                            nc.vector.tensor_tensor(pt_l[:, g % 2, k0:k1, j * P:(j + 1) * P], turned(p, k0, k1),
                                                    pt_h[:, g % 2, k0:k1, j * P:(j + 1) * P], ALU.subtract) \
                                .then_inc(S["pt_lo"], 1)

                    def divide(m):
                        zm = z[:, m * NT:(m + 1) * NT]
                        after(nc.vector.reciprocal(zm, zm))
                        dve.wait_ge(S["o_done"], (m + 1) * NT // group)
                        zb = zm.unsqueeze(2).to_broadcast([P, NT, HD])
                        if combine is None:
                            nc.vector.tensor_tensor(mix[:, :, mix_cols(m)], o_ps[:, :, :], zb, ALU.mult) \
                                .then_inc(S["map_done"], 1)
                        else:
                            after(nc.vector.tensor_tensor(part[:, m % 2], o_ps[:, :, :], zb, ALU.mult))
                            if m % 2:
                                nc.vector.scalar_tensor_tensor(out=mix[:, :, mix_cols(m // 2)], in0=part[:, 1],
                                                               scalar=combine, in1=part[:, 0],
                                                               op0=ALU.mult, op1=ALU.add) \
                                    .then_inc(S["map_done"], 1)
                            else:
                                nc.vector.tensor_copy(rmax[:, 0:1], rmax[:, 0:1]).then_inc(S["map_done"], 1)

                    lag = 2 * group + 1
                    maximum(0)
                    maximum(1)
                    for n in range(n_all + lag + 1):
                        if n + 2 < n_all:
                            maximum(n + 2)
                        if n < n_all:
                            split(n)
                        if n >= NT - 1 + lag and (n - lag + 1) % NT == 0:
                            divide((n - lag + 1) // NT - 1)
            end_stage()

        def turn_values(pe, t_ps, u_sb, slot):
            return transposes(pe, t_ps[:, slot, :], lambda t: u_sb[:, slot, t * P:(t + 1) * P])

        with nc.Fori(0, DEPTH) as layer:
            def vec(name, lo=None, hi=None):
                v = a[name][bass.ds(layer, 1), :]
                return v if lo is None else v[:, lo:hi]

            norm_stage("mix_pre", None, None, vec("norm_mix_pre"))
            with ExitStack() as cm:
                mix = sb(cm, "mix", [P, NT, D])

                with nc.Fori(0, 2) as kv, ExitStack() as ca:
                    q_h = sb(ca, "a_q_h", [P, 2, SEQ], F32R)
                    q_l = sb(ca, "a_q_l", [P, 2, SEQ], F32R)
                    k_s = sb(ca, "a_k_s", [P, SEQ], F32R)
                    v_s = sb(ca, "a_v_s", [P, NT, P], F32R)
                    with ExitStack() as c, nc.Block() as block:
                        ring = weight_ring(c, "a")
                        u_sb = sb(c, "a_u", [P, 2, SEQ])
                        tok = sb(c, "a_tok", [P, NT, 3, HD])
                        sq = sb(c, "a_sq", [P, NT, 3, HD])
                        rot = sb(c, "a_rot", [P, NT, 3, HD])
                        dup = sb(c, "a_dup", [P, NT, 3, 2, HD])
                        ss = sb(c, "a_ss", [P, NT * 3])
                        gain = sb(c, "a_gain", [P, 3, HD])
                        cos = sb(c, "a_cos", [P, NT, HD])
                        sin = sb(c, "a_sin", [P, NT, HD])
                        u_ps = ps(c, "a_u_ps", [P, 2, SEQ])
                        t_ps = ps(c, "a_t_ps", [P, 2, SEQ])
                        w = a["w_in"][layer]
                        units = [full_unit(w[:, bass.ds(kv * P + A0, P)]),
                                 ([(lambda w_, j=j: w_[:, :, j * HD:(j + 1) * HD],
                                    w[:, bass.ds(kv * HD + (A0 + (4 + 2 * j) * HD), HD)]
                                    .rearrange("(k p) n -> p k n", p=P)) for j in range(2)], FULL)]

                        @block.sync
                        def _(sp):
                            load_weights(sp, ring, units)
                            for dst, name in ((cos, "cos_a"), (sin, "sin_a")):
                                sp.dma_start(dst[:, :, :], a[name].rearrange("(t p) d -> p t d", p=P)) \
                                    .then_inc(S["const_landed"], 16)
                            for h in range(3):
                                sp.dma_start(gain[:, h, :], row_vector(vec("a_k_norm" if h == 2 else "a_q_norm"))) \
                                    .then_inc(S["const_landed"], 16)

                        @block.gpsimd
                        def _(pool):
                            for u in range(2):
                                split_lo(pool, ring, units, u)

                        @block.tensor
                        def _(pe):
                            for u in range(2):
                                products(pe, u_ps[:, u, :], ring, units, u, h_hi, h_lo)
                            for u in range(2):
                                pe.wait_ge(S["gemm_out"], u + 1)
                                turn_values(pe, t_ps, u_sb, u).then_inc(S["tt_done"], 1)
                            pe.wait_ge(S["prep_done"], 1)
                            for h in range(3):
                                dst = u_ps[:, h, :] if h < 2 else t_ps[:, 0, :]
                                transposes(pe, dst, lambda t, h=h: dup[:, t, h].rearrange("p a d -> p (a d)")) \
                                    .then_inc(S["ptr_done"], 1)

                        @block.scalar
                        def _(act):
                            for u in range(2):
                                split_hi(act, ring, units, u)
                            for u in range(2):
                                act.wait_ge(S["gemm_done"], u + 1)
                                nc.scalar.activation(u_sb[:, u, :], u_ps[:, u, :], ACT.Copy).then_inc(S["gemm_out"], 1)
                            act.wait_ge(S["tt_done"], 2)
                            nc.scalar.activation(v_s[:, :, 0:HD],
                                                 t_ps[:, 1, :].rearrange("p (t d) -> p t d", t=NT)[:, :, HD:P],
                                                 ACT.Copy).then_inc(S["tt_hi"], 1)
                            act.wait_ge(S["dve_step"], 4)
                            root(act, ss[:, :], HD).then_inc(S["root_done"], 1)
                            for h in range(3):
                                act.wait_ge(S["ptr_done"], h + 1)
                                dst = q_h[:, h, :] if h < 2 else k_s[:, :]
                                src = u_ps[:, h, :] if h < 2 else t_ps[:, 0, :]
                                nc.scalar.activation(dst, src, ACT.Copy, scale=HD ** -0.5 if h < 2 else 1.0) \
                                    .then_inc(S["hi_done"], 1)

                        @block.vector
                        def _(dve):
                            step = [0]

                            def after(ins):
                                step[0] += 1
                                ins.then_inc(S["dve_step"], 1)
                                dve.wait_ge(S["dve_step"], step[0])

                            dve.wait_ge(S["tt_done"], 1)
                            nc.vector.tensor_copy(tok[:, :, 0:2, :].rearrange("p t h d -> p t (h d)"),
                                                  t_ps[:, 0, :].rearrange("p (t d) -> p t d", t=NT)) \
                                .then_inc(S["dve_step"], 1)
                            dve.wait_ge(S["tt_hi"], 1)
                            nc.vector.tensor_copy(tok[:, :, 2, :],
                                                  t_ps[:, 1, :].rearrange("p (t d) -> p t d", t=NT)[:, :, 0:HD]) \
                                .then_inc(S["dve_step"], 1)
                            nc.vector.tensor_tensor(v_s[:, :, HD:P],
                                                    t_ps[:, 1, :].rearrange("p (t d) -> p t d", t=NT)[:, :, HD:P],
                                                    v_s[:, :, 0:HD], ALU.subtract).then_inc(S["tt_lo"], 1)
                            step[0] = 2
                            dve.wait_ge(S["dve_step"], 2)
                            flat = tok[:, :, :, :].rearrange("p t h d -> p (t h) d")
                            after(nc.vector.tensor_tensor(sq[:, :, :, :].rearrange("p t h d -> p (t h) d"),
                                                          flat, flat, ALU.mult))
                            after(nc.vector.tensor_reduce(ss[:, :], sq[:, :, :, :].rearrange("p t h d -> p (t h) d"),
                                                          AX_X, ALU.add))
                            dve.wait_ge(S["root_done"], 1)
                            step[0] = rstd(dve, ss[:, :], step[0])
                            after(nc.vector.tensor_tensor(flat, flat,
                                                          ss[:, :].unsqueeze(2).to_broadcast([P, NT * 3, HD]), ALU.mult))
                            dve.wait_ge(S["const_landed"], 80)
                            gb = gain[:, :, :].rearrange("p h d -> p (h d)").unsqueeze(1).to_broadcast([P, NT, 3 * HD])
                            after(nc.vector.tensor_tensor(tok[:, :, :, :].rearrange("p t h d -> p t (h d)"),
                                                          tok[:, :, :, :].rearrange("p t h d -> p t (h d)"), gb, ALU.mult))
                            q4 = HD // 4
                            for d0 in range(0, HD, 2 * q4):
                                for f, g in ((d0, d0 + q4), (d0 + q4, d0)):
                                    nc.vector.tensor_tensor(
                                        rot[:, :, :, f:f + q4], tok[:, :, :, g:g + q4],
                                        sin[:, :, f:f + q4].unsqueeze(2).to_broadcast([P, NT, 3, q4]), ALU.mult) \
                                        .then_inc(S["dve_step"], 1)
                                    step[0] += 1
                            dve.wait_ge(S["dve_step"], step[0])
                            after(nc.vector.tensor_tensor(tok[:, :, :, :], tok[:, :, :, :],
                                                          cos[:, :, :].unsqueeze(2).to_broadcast([P, NT, 3, HD]), ALU.mult))
                            for j in range(2):
                                last = nc.vector.tensor_tensor(
                                    dup[:, :, :, j, :].rearrange("p t h d -> p (t h) d"), flat,
                                    rot[:, :, :, :].rearrange("p t h d -> p (t h) d"), ALU.add)
                                last.then_inc(S["prep_done" if j else "prep2_done"], 1)
                            for h in range(2):
                                dve.wait_ge(S["hi_done"], h + 1)
                                nc.vector.scalar_tensor_tensor(out=q_l[:, h, :], in0=u_ps[:, h, :], scalar=HD ** -0.5,
                                                               in1=q_h[:, h, :], op0=ALU.mult, op1=ALU.subtract)
                            dve.wait_ge(S["hi_done"], 3)
                            nc.vector.tensor_tensor(k_s[HD:P, :], t_ps[HD:P, 0, :], k_s[HD:P, :], ALU.subtract)
                    end_stage()
                    maps = [([lambda i, h=h: q_h[:, h, i * P:(i + 1) * P], lambda i, h=h: q_l[:, h, i * P:(i + 1) * P]],
                             [lambda x0, x1: k_s[:, x0:x1]] * 2, v_s) for h in range(2)]
                    attention_stage("a", maps, [(0, NT, None)] * NT, 2,
                                    lambda m: bass.ds(kv * P + m * HD, HD), mix)

                with ExitStack() as cb:
                    cq_h = sb(cb, "cq_h", [P, 2, SEQ], F32R)
                    cq_l = sb(cb, "cq_l", [P, 2, SEQ], F32R)
                    ckv_h = sb(cb, "ckv_h", [P, 1, SEQ], F32R)
                    ckv_l = sb(cb, "ckv_l", [P, 1, SEQ], F32R)
                    k_rope = sb(cb, "k_rope", [P, SEQ])
                    cs = sb(cb, "cos_sin", [P, SEQ])
                    R0, R1 = HD, HD + B_ROPE
                    with ExitStack() as c, nc.Block() as block:
                        ring = weight_ring(c, "b")
                        u_sb = sb(c, "b_u", [P, 3, SEQ])
                        sq = sb(c, "b_sq", [P, 3, SEQ])
                        r_sb = sb(c, "b_r", [P, 2, SEQ])
                        g_col = sb(c, "b_g", [P, 3])
                        rt = sb(c, "b_rt", [P, SEQ])
                        u_ps = ps(c, "b_u_ps", [P, 2, SEQ])
                        r_ps = ps(c, "b_r_ps", [P, 2, SEQ])
                        w = a["w_in"][layer]

                        def cols(c0, n):
                            return w[:, c0:c0 + n].rearrange("(k p) n -> p k n", p=P)

                        half = B_ROPE // 2
                        kr = B0 + B_Q + B_KV
                        units = [full_unit(w[:, B0:B0 + P]),
                                 ([(lambda w_: w_[:, :, 0:HD], cols(B0 + P, HD)),
                                   (lambda w_: w_[:, :, R0:R1], cols(kr, B_ROPE)),
                                   (lambda w_: w_[:, :, R1:R1 + half], cols(kr + half, half)),
                                   (lambda w_: w_[:, :, R1 + half:P], cols(kr, half))], FULL),
                                 full_unit(w[:, B0 + B_Q:B0 + B_Q + P])]

                        @block.sync
                        def _(sp):
                            load_weights(sp, ring, units)
                            sp.dma_start(cs[HD:P, :], a["cos_sin_b"]).then_inc(S["const_landed"], 16)
                            col = lambda v: v.rearrange("a p -> p a")
                            sp.dma_start(g_col[:, 0:1], col(vec("b_cq_norm", 0, P))).then_inc(S["const_landed"], 16)
                            sp.dma_start(g_col[0:HD, 1:2], col(vec("b_cq_norm", P, B_Q))).then_inc(S["const_landed"], 16)
                            sp.dma_start(g_col[:, 2:3], col(vec("b_ckv_norm"))).then_inc(S["const_landed"], 16)

                        @block.gpsimd
                        def _(pool):
                            for u in range(3):
                                split_lo(pool, ring, units, u)

                        @block.tensor
                        def _(pe):
                            for u in range(3):
                                if u == 2:
                                    pe.wait_ge(S["gemm_out"], 1)
                                    pe.wait_ge(S["square_done"], 1)
                                products(pe, u_ps[:, u % 2, :], ring, units, u, h_hi, h_lo)
                            for r, parts in enumerate((((0, P), (1, HD)), ((2, P),))):
                                pe.wait_ge(S["square_done"], 2 + r)
                                for n in range(2):
                                    for j, (u, rows) in enumerate(parts):
                                        last = nc.tensor.matmul(r_ps[:, r, n * HALF:(n + 1) * HALF], ones[0:rows, :],
                                                                sq[0:rows, u, n * HALF:(n + 1) * HALF],
                                                                start=(j == 0), stop=(j == len(parts) - 1))
                                last.then_inc(S["pe_step"], 1)

                        @block.scalar
                        def _(act):
                            split_hi(act, ring, units, 0)
                            split_hi(act, ring, units, 1)
                            for u in range(3):
                                act.wait_ge(S["gemm_done"], u + 1)
                                nc.scalar.activation(u_sb[:, u, :], u_ps[:, u % 2, :], ACT.Copy).then_inc(S["gemm_out"], 1)
                                nc.scalar.activation(sq[:, u, :], u_ps[:, u % 2, :], ACT.Square) \
                                    .then_inc(S["square_done"], 1)
                                if u == 0:
                                    split_hi(act, ring, units, 2)
                            for r, width in enumerate((B_Q, B_KV)):
                                act.wait_ge(S["pe_step"], r + 1)
                                nc.scalar.activation(r_sb[:, r, :], r_ps[:, r, :], ACT.Sqrt, scale=1.0 / width,
                                                     bias=eps_col[:, 0:1]).then_inc(S["root_done"], 1)
                            for j, dst in enumerate((cq_h[:, 0, :], cq_h[0:HD, 1, :], ckv_h[:, 0, :])):
                                act.wait_ge(S["norm_done"], j + 1)
                                nc.scalar.activation(dst, u_sb[0:dst.shape[0], j, :], ACT.Copy).then_inc(S["hi_done"], 1)

                        @block.vector
                        def _(dve):
                            step = 0
                            dve.wait_ge(S["const_landed"], 64)
                            dve.wait_ge(S["gemm_out"], 2)
                            nc.vector.tensor_tensor(k_rope[R0:R1, :], u_sb[R0:R1, 1, :], cs[R0:R1, :],
                                                    ALU.mult).then_inc(S["prep_done"], 1)
                            nc.vector.tensor_tensor(rt[R0:R1, :], u_sb[R1:P, 1, :], cs[R1:P, :],
                                                    ALU.mult).then_inc(S["prep_done"], 1)
                            dve.wait_ge(S["prep_done"], 2)
                            nc.vector.tensor_tensor(k_rope[R0:R1, :], k_rope[R0:R1, :], rt[R0:R1, :], ALU.add)
                            for r in range(2):
                                dve.wait_ge(S["root_done"], r + 1)
                                step = rstd(dve, r_sb[:, r, :], step)
                                for u, rows in (((0, P), (1, HD)) if r == 0 else ((2, P),)):
                                    nc.vector.scalar_tensor_tensor(out=u_sb[0:rows, u, :], in0=u_sb[0:rows, u, :],
                                                                   scalar=g_col[0:rows, u:u + 1], in1=r_sb[0:rows, r, :],
                                                                   op0=ALU.mult, op1=ALU.mult) \
                                        .then_inc(S["norm_done"], 1)
                            for j, (hi, lo) in enumerate(((cq_h[:, 0, :], cq_l[:, 0, :]),
                                                          (cq_h[0:HD, 1, :], cq_l[0:HD, 1, :]),
                                                          (ckv_h[:, 0, :], ckv_l[:, 0, :]))):
                                dve.wait_ge(S["hi_done"], j + 1)
                                nc.vector.tensor_tensor(lo, u_sb[0:hi.shape[0], j, :], hi, ALU.subtract)
                    end_stage()

                    with nc.Fori(0, NHEAD) as h, ExitStack() as ch:
                        q_h = sb(ch, "b_q_h", [P, SEQ], F32R)
                        q_l = sb(ch, "b_q_l", [P, SEQ], F32R)
                        k_h = sb(ch, "b_k_h", [P, SEQ], F32R)
                        k_l = sb(ch, "b_k_l", [P, SEQ], F32R)
                        v_s = sb(ch, "b_v_s", [P, NT, P], F32R)
                        QK = HD + B_ROPE
                        with ExitStack() as c, nc.Block() as block:
                            ring = weight_ring(c, "bh")
                            u_sb = sb(c, "bh_u", [P, 2, SEQ])
                            rt = sb(c, "bh_rt", [P, SEQ])
                            u_ps = ps(c, "bh_u_ps", [P, 2, SEQ])
                            t_ps = ps(c, "bh_t_ps", [P, 2, SEQ])
                            wq, wkv = a["b_w_uq"][layer], a["b_w_ukv"][layer]
                            half = B_ROPE // 2
                            rope0 = HD

                            def q_piece(k, rows, d0, d1, c0):
                                return (lambda w_: w_[0:rows, k, d0:d1],
                                        wq[k * P:k * P + rows, bass.ds(h * QK + c0, d1 - d0)])

                            q_pieces = [q_piece(k, rows, d0, d1, c0) for k, rows in ((0, P), (1, HD))
                                        for d0, d1, c0 in ((0, QK, 0), (QK, QK + half, rope0 + half),
                                                           (QK + half, P, rope0))]
                            units = [(q_pieces, [(P, slice(0, 1)), (HD, slice(1, 2))]),
                                     ([(lambda w_: w_[:, 0, :], wkv[:, bass.ds(h * P, P)])], [(P, slice(0, 1))])]

                            @block.sync
                            def _(sp):
                                load_weights(sp, ring, units)

                            @block.gpsimd
                            def _(pool):
                                for u in range(2):
                                    split_lo(pool, ring, units, u)

                            @block.tensor
                            def _(pe):
                                products(pe, u_ps[:, 0, :], ring, units, 0, cq_h, cq_l)
                                products(pe, u_ps[:, 1, :], ring, units, 1, ckv_h, ckv_l)
                                pe.wait_ge(S["gemm_out"], 2)
                                turn_values(pe, t_ps, u_sb, 1).then_inc(S["tt_done"], 1)

                            @block.scalar
                            def _(act):
                                for u in range(2):
                                    split_hi(act, ring, units, u)
                                act.wait_ge(S["gemm_done"], 1)
                                nc.scalar.activation(u_sb[:, 0, :], u_ps[:, 0, :], ACT.Copy, scale=QK ** -0.5) \
                                    .then_inc(S["gemm_out"], 1)
                                act.wait_ge(S["gemm_done"], 2)
                                nc.scalar.activation(u_sb[:, 1, :], u_ps[:, 1, :], ACT.Copy).then_inc(S["gemm_out"], 1)
                                nc.scalar.activation(k_h[0:HD, :], u_ps[0:HD, 1, :], ACT.Copy)
                                nc.scalar.activation(k_h[R0:R1, :], k_rope[R0:R1, :], ACT.Copy) \
                                    .then_inc(S["hi_done"], 1)
                                act.wait_ge(S["tt_done"], 1)
                                nc.scalar.activation(v_s[:, :, 0:HD],
                                                     t_ps[:, 1, :].rearrange("p (t d) -> p t d", t=NT)[:, :, HD:P],
                                                     ACT.Copy).then_inc(S["tt_hi"], 1)
                                act.wait_ge(S["prep_done"], 1)
                                nc.scalar.activation(q_h[0:QK, :], u_sb[0:QK, 0, :], ACT.Copy) \
                                    .then_inc(S["hi_done"], 1)

                            @block.vector
                            def _(dve):
                                dve.wait_ge(S["gemm_out"], 1)
                                nc.vector.tensor_tensor(rt[R0:R1, :], u_sb[R1:P, 0, :], cs[R1:P, :],
                                                        ALU.mult).then_inc(S["dve_step"], 1)
                                nc.vector.tensor_tensor(u_sb[R0:R1, 0, :], u_sb[R0:R1, 0, :], cs[R0:R1, :],
                                                        ALU.mult).then_inc(S["dve_step"], 1)
                                dve.wait_ge(S["dve_step"], 2)
                                nc.vector.tensor_tensor(u_sb[R0:R1, 0, :], u_sb[R0:R1, 0, :], rt[R0:R1, :],
                                                        ALU.add).then_inc(S["prep_done"], 1)
                                dve.wait_ge(S["hi_done"], 1)
                                nc.vector.tensor_tensor(k_l[0:HD, :], u_ps[0:HD, 1, :], k_h[0:HD, :], ALU.subtract)
                                nc.vector.tensor_tensor(k_l[R0:R1, :], k_rope[R0:R1, :], k_h[R0:R1, :], ALU.subtract)
                                dve.wait_ge(S["tt_hi"], 1)
                                nc.vector.tensor_tensor(v_s[:, :, HD:P],
                                                        t_ps[:, 1, :].rearrange("p (t d) -> p t d", t=NT)[:, :, HD:P],
                                                        v_s[:, :, 0:HD], ALU.subtract)
                                dve.wait_ge(S["hi_done"], 2)
                                nc.vector.tensor_tensor(q_l[0:QK, :], u_sb[0:QK, 0, :], q_h[0:QK, :], ALU.subtract)
                        end_stage()
                        qh = lambda i: q_h[0:QK, i * P:(i + 1) * P]
                        ql = lambda i: q_l[0:QK, i * P:(i + 1) * P]
                        kh = lambda x0, x1: k_h[0:QK, x0:x1]
                        kl = lambda x0, x1: k_l[0:QK, x0:x1]
                        attention_stage("b", [([qh, qh, ql], [kh, kl, kh], v_s)], [(0, NT, None)] * NT, 2,
                                        lambda m: bass.ds(h * HD + 4 * HD, HD), mix)

                def pair_stage(tag, c0, pair, scale, stack, v_s, extra_dma, extra_act, extra_dve):
                    with ExitStack() as c, nc.Block() as block:
                        ring = weight_ring(c, tag)
                        p_h = sb(c, f"{tag}_p_h", [P, 2, SEQ], F32R)
                        p_l = sb(c, f"{tag}_p_l", [P, 2, SEQ], F32R)
                        u_sb = sb(c, f"{tag}_u", [P, 1, SEQ])
                        u_ps = ps(c, f"{tag}_u_ps", [P, 3, SEQ])
                        t_ps = ps(c, f"{tag}_t_ps", [P, 1, SEQ])
                        w = a["w_in"][layer]
                        units = [full_unit(w[:, bass.ds(pair * P + (c0 + j * 4 * HD), P)]) for j in range(3)]

                        @block.sync
                        def _(sp):
                            load_weights(sp, ring, units)
                            extra_dma(sp)
                            sent = 0
                            for j in range(2):
                                sp.wait_ge(S["hi_done"], j + 1)
                                sp.wait_ge(S["lo_done"], j + 1)
                                copies = stack(p_h[:, j], p_l[:, j], j == 1)
                                sent += len(copies)
                                for dst, src in copies:
                                    sp.dma_start(dst.bitcast(F32), src.bitcast(F32)).then_inc(S["stack_landed"], 16)
                            sp.wait_ge(S["stack_landed"], 16 * sent)

                        @block.gpsimd
                        def _(pool):
                            for u in range(3):
                                split_lo(pool, ring, units, u)

                        @block.tensor
                        def _(pe):
                            for u in range(3):
                                products(pe, u_ps[:, u, :], ring, units, u, h_hi, h_lo)
                            pe.wait_ge(S["gemm_out"], 1)
                            turn_values(pe, t_ps, u_sb, 0).then_inc(S["tt_done"], 1)

                        @block.scalar
                        def _(act):
                            split_hi(act, ring, units, 0)
                            split_hi(act, ring, units, 1)
                            extra_act(act)
                            act.wait_ge(S["gemm_done"], 1)
                            nc.scalar.activation(p_h[:, 0, :], u_ps[:, 0, :], ACT.Copy, scale=scale) \
                                .then_inc(S["hi_done"], 1)
                            split_hi(act, ring, units, 2)
                            act.wait_ge(S["gemm_done"], 2)
                            nc.scalar.activation(p_h[:, 1, :], u_ps[:, 1, :], ACT.Copy).then_inc(S["hi_done"], 1)
                            act.wait_ge(S["gemm_done"], 3)
                            nc.scalar.activation(u_sb[:, 0, :], u_ps[:, 2, :], ACT.Copy).then_inc(S["gemm_out"], 1)
                            act.wait_ge(S["tt_done"], 1)
                            nc.scalar.activation(v_s[:, :, :, 0:HD],
                                                 t_ps[:, 0, :].rearrange("p (t h d) -> p t h d", t=NT, h=2),
                                                 ACT.Copy).then_inc(S["tt_hi"], 1)

                        @block.vector
                        def _(dve):
                            extra_dve[0](dve)
                            for j in range(2):
                                if j == 1:
                                    extra_dve[1](dve)
                                dve.wait_ge(S["hi_done"], j + 1)
                                nc.vector.scalar_tensor_tensor(out=p_l[:, j, :], in0=u_ps[:, j, :],
                                                               scalar=1.0 if j else scale, in1=p_h[:, j, :],
                                                               op0=ALU.mult, op1=ALU.subtract).then_inc(S["lo_done"], 1)
                            dve.wait_ge(S["tt_hi"], 1)
                            nc.vector.tensor_tensor(v_s[:, :, :, HD:P],
                                                    t_ps[:, 0, :].rearrange("p (t h d) -> p t h d", t=NT, h=2),
                                                    v_s[:, :, :, 0:HD], ALU.subtract)
                    end_stage()

                with ExitStack() as cc:
                    lam = sb(cc, "lam", [P, 1])
                    nd = sb(cc, "neg_dist", [P, 2 * SEQ - P])
                    lv = sb(cc, "lam_vec", [P, 4, HD // 2])
                    lj = sb(cc, "lam_junk", [P, HD // 2])
                    ls = sb(cc, "lam_sum", [P, 2])
                    li = sb(cc, "lam_init", [P, 2])

                    with nc.Fori(0, 2) as pair, ExitStack() as ch:
                        qs = sb(ch, "c_q_s", [P, 4, SEQ], F32R)
                        ks = sb(ch, "c_k_s", [P, 4, SEQ], F32R)
                        v_s = sb(ch, "c_v_s", [P, NT, 2, P], F32R)
                        alibi = sb(ch, "alibi", [P, 2, 2 * SEQ - P])
                        slope = sb(ch, "slope", [P, 2])
                        W = HD // 2

                        def stack(hi, lo, is_k):
                            order = (hi, lo, hi, lo) if is_k else (hi, hi, lo, lo)
                            dst = ks if is_k else qs
                            return [(dst[r * W:(r + 1) * W, m, :], src[m * W:(m + 1) * W, :])
                                    for m in range(4) for r, src in enumerate(order)]

                        def extra_dma(sp):
                            sp.dma_start(nd[:, :], a["neg_dist"]).then_inc(S["const_landed"], 16)
                            sp.dma_start(slope[:, :], row_vector(a["slopes"][:, bass.ds(pair * 2, 2)])) \
                                .then_inc(S["const_landed"], 16)
                            sp.dma_start(li[:, :], row_vector(vec("lambda_init"))).then_inc(S["gain_landed"], 16)
                            for j, name in enumerate(("c_lambda_q1", "c_lambda_k1", "c_lambda_q2", "c_lambda_k2")):
                                sp.dma_start(lv[:, j, :], row_vector(vec(name))).then_inc(S["gain_landed"], 16)

                        def biases(act):
                            act.wait_ge(S["const_landed"], 32)
                            for j in range(2):
                                nc.scalar.activation(alibi[:, j, :], nd[:, :], ACT.Copy, scale=slope[:, j:j + 1])
                            act.wait_ge(S["dve_step"], 2)
                            nc.scalar.activation(ls[:, :], ls[:, :], ACT.Exp).then_inc(S["exp_done"], 1)

                        def lambda_sums(dve):
                            dve.wait_ge(S["gain_landed"], 80)
                            for j in range(2):
                                nc.vector.tensor_tensor_reduce(out=lj[:, :], in0=lv[:, 2 * j, :], in1=lv[:, 2 * j + 1, :],
                                                               scale=1.0, scalar=0.0, op0=ALU.mult, op1=ALU.add,
                                                               accum_out=ls[:, j:j + 1]).then_inc(S["dve_step"], 1)
                                dve.wait_ge(S["dve_step"], j + 1)

                        def lambda_difference(dve):
                            dve.wait_ge(S["exp_done"], 1)
                            nc.vector.tensor_tensor(lam[:, :], ls[:, 1:2], ls[:, 0:1], ALU.subtract) \
                                .then_inc(S["dve_step"], 1)
                            dve.wait_ge(S["dve_step"], 3)
                            nc.vector.tensor_tensor(lam[:, :], lam[:, :], li[:, 0:1], ALU.subtract)

                        pair_stage("c", C0, pair, W ** -0.5, stack, v_s, extra_dma, biases,
                                   (lambda_sums, lambda_difference))
                        maps = [([lambda i, m=m: qs[:, m, i * P:(i + 1) * P]],
                                 [lambda x0, x1, m=m: ks[:, m, x0:x1]], v_s[:, :, m // 2, :]) for m in range(4)]
                        tiles = [(0, NT, lambda m, i=i: alibi[:, m // 2, (SEQ - P) - i * P:(SEQ - P) - i * P + SEQ])
                                 for i in range(NT)]
                        attention_stage("c", maps, tiles, 2, lambda j: bass.ds(pair * P + (8 * HD + j * HD), HD),
                                        mix, combine=lam[:, 0:1])

                with nc.Fori(0, 2) as pair, ExitStack() as ch:
                    if True:
                        qh = sb(ch, "d_q_h", [P, 2, SEQ], F32R)
                        ql = sb(ch, "d_q_l", [P, 2, SEQ], F32R)
                        ks = sb(ch, "d_k_s", [P, 2, SEQ], F32R)
                        v_s = sb(ch, "d_v_s", [P, NT, 2, P], F32R)
                        edge = sb(ch, "bias_edge", [P, 2, REL_R + 1, GRID_W])
                        inner = sb(ch, "bias_inner", [P, 2, 10, GRID_W])
                        cmask = sb(ch, "cmask", [P, GRID_W])
                        rmask = sb(ch, "rmask", [P, 10])

                        def load_bias(sp):
                            sp.dma_start(cmask[:, :], a["col_mask"]).then_inc(S["const_landed"], 16)
                            sp.dma_start(rmask[:, :], a["row_mask"]).then_inc(S["const_landed"], 16)
                            sp.wait_ge(skew_landed, 16 * DEPTH)
                            sp.wait_ge(S["dve_step"], 1)
                            for r in range(2):
                                for h in range(2):
                                    row = layer * (NHEAD * REL_R) + pair * (2 * REL_R) + h * REL_R
                                    src = bass.AP(skew.tensor, row * (GRID_W * SKEW) + (GRID_W - 1),
                                                  [[SKEW - 1, GRID_W], [GRID_W * SKEW, REL_R], [1, GRID_W]])
                                    sp.dma_start(edge[r * GRID_W:(r + 1) * GRID_W, h, r:r + REL_R, :], src) \
                                        .then_inc(S["copy_landed"], 16)

                        def clear_bias(dve):
                            nc.vector.memset(edge[:, :, :, :], NEG).then_inc(S["dve_step"], 1)

                        def mask_bias(dve):
                            dve.wait_ge(S["const_landed"], 32)
                            dve.wait_ge(S["copy_landed"], 16 * 4)
                            e = edge[:, :, :, :].rearrange("p h r k -> p (h r) k")
                            nc.vector.tensor_tensor(e, e, cmask[:, :].unsqueeze(1)
                                                    .to_broadcast([P, 2 * (REL_R + 1), GRID_W]),
                                                    ALU.add).then_inc(S["dve_step"], 1)
                            dve.wait_ge(S["dve_step"], 2)
                            for h in range(2):
                                nc.vector.tensor_tensor(inner[:, h], edge[:, h, 3:13, :],
                                                        rmask[:, :].unsqueeze(2).to_broadcast([P, 10, GRID_W]), ALU.add)

                        def stack(hi, lo, is_k):
                            out_ = []
                            for h in range(2):
                                s = slice(h * HD, (h + 1) * HD)
                                for r in range(2):
                                    d = slice(r * HD, (r + 1) * HD)
                                    if is_k:
                                        out_.append((ks[d, h, :], (lo if r else hi)[s, :]))
                                    else:
                                        out_ += [(qh[d, h, :], hi[s, :]), (ql[d, h, :], lo[s, :])]
                            return out_

                        pair_stage("d", D0, pair, HD ** -0.5, stack, v_s, load_bias, lambda act: None,
                                   (clear_bias, mask_bias))

                        maps = [([lambda i, h=h: qh[:, h, i * P:(i + 1) * P], lambda i, h=h: ql[:, h, i * P:(i + 1) * P]],
                                 [lambda x0, x1, h=h: ks[:, h, x0:x1]] * 2, v_s[:, :, h, :]) for h in range(2)]

                        def bias(i):
                            r = {0: 7, 1: 5, 6: 3, 7: 1}.get(i)
                            if r is None:
                                return lambda m: inner[:, m].rearrange("p r k -> p (r k)")
                            return lambda m: edge[:, m, r:r + NA_R, :].rearrange("p r k -> p (r k)")

                        tiles = [((0 if i < 2 else 4 if i > 5 else i - 2), (5 if 2 <= i <= 5 else 4), bias(i))
                                 for i in range(NT)]
                        attention_stage("d", maps, tiles, 1, lambda m: bass.ds(pair * P + (12 * HD + m * HD), HD), mix)

                with ExitStack() as c, nc.Block() as block:
                    sq = sb(c, "m_sq", [P, 2, D])
                    ss = sb(c, "m_ss", [P, NT, 4, 4])
                    sg = sb(c, "m_sg", [P, NT, 4])
                    hn = sb(c, "m_hn", [P, 2, D])
                    g = sb(c, "m_g", [P, D])
                    li = sb(c, "m_li", [P, 2])
                    h_ps = ps(c, "m_ps", [P, 2, D])
                    GW = 4 * HD

                    @block.sync
                    def _(sp):
                        for j, name in ((0, "g_out_a"), (1, "g_out_b"), (3, "g_out_d")):
                            sp.dma_start(g[:, j * GW:(j + 1) * GW], row_vector(vec(name))).then_inc(S["gain_landed"], 16)
                        for h in range(4):
                            sp.dma_start(g[:, 2 * GW + h * HD:2 * GW + (h + 1) * HD], row_vector(vec("g_out_c"))) \
                                .then_inc(S["gain_landed"], 16)
                        sp.dma_start(li[:, :], row_vector(vec("lambda_init"))).then_inc(S["gain_landed"], 16)

                    @block.scalar
                    def _(act):
                        for t in range(NT):
                            if t >= 2:
                                act.wait_ge(S["mix_sq"], t - 1)
                            nc.scalar.activation(sq[:, t % 2, :], mix[:, t, :], ACT.Square).then_inc(S["square_done"], 1)
                        act.wait_ge(S["dve_step"], 4)
                        root(act, ss[:, :, :, :].rearrange("p t m h -> p (t m h)"), HD).then_inc(S["root_done"], 1)
                        for t in range(NT):
                            act.wait_ge(S["tr_done"], t + 1)
                            nc.scalar.activation(h_hi[:, :, t * P:(t + 1) * P],
                                                 h_ps[:, t % 2, :].rearrange("p (k n) -> p k n", k=KT),
                                                 ACT.Copy).then_inc(S["hi_done"], 1)

                    @block.vector
                    def _(dve):
                        step = [0]

                        def after(ins):
                            step[0] += 1
                            ins.then_inc(S["dve_step"], 1)
                            dve.wait_ge(S["dve_step"], step[0])

                        for t in range(NT):
                            dve.wait_ge(S["square_done"], t + 1)
                            nc.vector.tensor_reduce(ss[:, t].rearrange("p m h -> p (m h)"),
                                                    sq[:, t % 2, :].rearrange("p (h d) -> p h d", d=HD),
                                                    AX_X, ALU.add).then_inc(S["mix_sq"], 1)
                        dve.wait_ge(S["mix_sq"], NT)
                        after(nc.vector.tensor_reduce(sg[:, :, :].rearrange("p t m -> p (t m)"),
                                                      ss[:, :, :, :].rearrange("p t m h -> p (t m) h"), AX_X, ALU.add))
                        for m in (0, 1, 3):
                            after(nc.vector.tensor_scalar(ss[:, :, m, :], sg[:, :, m].unsqueeze(2)
                                                          .to_broadcast([P, NT, 4]), 0.25, None, ALU.mult))
                        dve.wait_ge(S["root_done"], 1)
                        after(nc.vector.reciprocal(ss[:, :, :, :], ss[:, :, :, :]))
                        dve.wait_ge(S["gain_landed"], 16 * 8)
                        after(nc.vector.tensor_scalar(g[:, 2 * GW:3 * GW], g[:, 2 * GW:3 * GW], li[:, 1:2], None, ALU.mult))
                        for t in range(NT + 1):
                            if t < NT:
                                if t >= 2:
                                    dve.wait_ge(S["tr_done"], t - 1)
                                after(nc.vector.tensor_tensor(
                                    hn[:, t % 2, :].rearrange("p (h d) -> p h d", d=HD),
                                    mix[:, t, :].rearrange("p (h d) -> p h d", d=HD),
                                    ss[:, t].rearrange("p m h -> p (m h)").unsqueeze(2).to_broadcast([P, 16, HD]),
                                    ALU.mult))
                                nc.vector.tensor_tensor(hn[:, t % 2, :], hn[:, t % 2, :], g[:, :], ALU.mult) \
                                    .then_inc(S["norm_done"], 1)
                            if t >= 1:
                                s = t - 1
                                dve.wait_ge(S["hi_done"], s + 1)
                                nc.vector.tensor_tensor(h_lo[:, :, s * P:(s + 1) * P],
                                                        h_ps[:, s % 2, :].rearrange("p (k n) -> p k n", k=KT),
                                                        h_hi[:, :, s * P:(s + 1) * P], ALU.subtract) \
                                    .then_inc(S["lo_done"], 1)

                    @block.tensor
                    def _(pe):
                        for t in range(NT):
                            pe.wait_ge(S["norm_done"], t + 1)
                            if t >= 2:
                                pe.wait_ge(S["lo_done"], t - 1)
                            transposes(pe, h_ps[:, t % 2, :], lambda k: hn[:, t % 2, k * P:(k + 1) * P]) \
                                .then_inc(S["tr_done"], 1)
                end_stage()

            with ExitStack() as co:
                ft = sb(co, "mix_out_t", [P, KT, SEQ])
                with ExitStack() as c, nc.Block() as block:
                    ring = weight_ring(c, "o")
                    u_ps = ps(c, "o_ps", [P, 2, SEQ])
                    w = a["w_out"][layer]
                    units = [full_unit(w[:, m * P:(m + 1) * P]) for m in range(KT)]

                    @block.sync
                    def _(sp):
                        load_weights(sp, ring, units)

                    @block.gpsimd
                    def _(pool):
                        for u in range(KT):
                            split_lo(pool, ring, units, u)

                    @block.scalar
                    def _(act):
                        for u in range(KT):
                            split_hi(act, ring, units, u)

                    @block.tensor
                    def _(pe):
                        for u in range(KT):
                            if u >= 2:
                                pe.wait_ge(S["gemm_out"], u - 1)
                            products(pe, u_ps[:, u % 2, :], ring, units, u, h_hi, h_lo)

                    @block.vector
                    def _(dve):
                        for u in range(KT):
                            dve.wait_ge(S["gemm_done"], u + 1)
                            nc.vector.tensor_copy(ft[:, u, :], u_ps[:, u % 2, :]).then_inc(S["gemm_out"], 1)
                end_stage()
                norm_stage("mlp_pre", ft, vec("norm_mix_post"), vec("norm_mlp_pre"))

            with ExitStack() as co:
                ft = sb(co, "mlp_out_t", [P, KT, SEQ])
                with ExitStack() as c, nc.Block() as block:
                    ring = weight_ring(c, "m")
                    up_h = sb(c, "up_h", [P, KT, SEQ], F32R)
                    up_l = sb(c, "up_l", [P, KT, SEQ], F32R)
                    r_sb = sb(c, "m_relu", [P, SEQ])
                    s_sb = sb(c, "m_square", [P, SEQ])
                    u_ps = ps(c, "u_ps", [P, 2, SEQ])
                    NU = 2 * KT
                    CHUNKS = FF // FF_CHUNK

                    def chunk_units(chunk):
                        wu = a["w_up"][layer]
                        wd = a["w_down"][layer][bass.ds(chunk * FF_CHUNK, FF_CHUNK), :]
                        return [full_unit(wu[:, bass.ds(chunk * FF_CHUNK + j * P, P)]) for j in range(KT)] + \
                               [full_unit(wd[:, m * P:(m + 1) * P]) for m in range(KT)]

                    shapes = chunk_units(0)

                    @block.sync
                    def _(sp):
                        with sp.Fori(0, CHUNKS) as chunk:
                            load_weights(sp, ring, chunk_units(chunk), chunk * NU + 2, looped=True)

                    @block.gpsimd
                    def _(pool):
                        pool.sem_inc(S["w_lo"], 2)
                        with pool.Fori(0, CHUNKS) as chunk:
                            for u in range(NU):
                                split_lo(pool, ring, shapes, u, chunk * NU)

                    @block.tensor
                    def _(pe):
                        pe.sem_inc(S["gemm_done"], 2)
                        with pe.Fori(0, CHUNKS) as chunk:
                            for u in range(NU):
                                if 2 <= u < KT + 2:
                                    pe.wait_ge(S["relu_done"], chunk * KT + (u - 1))
                                else:
                                    pe.wait_ge(S["acc_done"], chunk * KT + (u + 1 if u < 2 else u + 1 - KT))
                                if u < KT:
                                    products(pe, u_ps[:, u % 2, :], ring, shapes, u, h_hi, h_lo, chunk * NU + 2)
                                else:
                                    if u == KT:
                                        pe.wait_ge(S["up_lo"], chunk * KT + (KT - 1))
                                    products(pe, u_ps[:, u % 2, :], ring, shapes, u, up_h, up_l, chunk * NU + 2,
                                             lambda: pe.wait_ge(S["up_lo"], chunk * KT + KT))

                    @block.scalar
                    def _(act):
                        with act.Fori(0, CHUNKS) as chunk:
                            def hi(u):
                                split_hi(act, ring, shapes, u, chunk * NU + 2, looped=True, landed_base=chunk * (16 * KT))

                            hi(0)
                            for u in range(NU):
                                if u + 1 < NU:
                                    hi(u + 1)
                                if u < KT:
                                    act.wait_ge(S["gemm_done"], chunk * NU + (u + 3))
                                    nc.scalar.activation(r_sb[:, :], u_ps[:, u % 2, :], ACT.Relu) \
                                        .then_inc(S["relu_done"], 1)
                                    act.wait_ge(S["sq_done"], chunk * KT + (u + 1))
                                    nc.scalar.activation(up_h[:, u, :], s_sb[:, :], ACT.Copy).then_inc(S["up_hi"], 1)

                    @block.vector
                    def _(dve):
                        dve.sem_inc(S["acc_done"], 2)
                        nc.vector.memset(ft[:, :, :], 0.0).then_inc(S["zero_done"], 1)
                        dve.wait_ge(S["zero_done"], 1)
                        with dve.Fori(0, CHUNKS) as chunk:
                            for u in range(NU):
                                if u < KT:
                                    dve.wait_ge(S["relu_done"], chunk * KT + (u + 1))
                                    nc.vector.tensor_tensor(s_sb[:, :], r_sb[:, :], r_sb[:, :], ALU.mult) \
                                        .then_inc(S["sq_done"], 1)
                                    dve.wait_ge(S["up_hi"], chunk * KT + (u + 1))
                                    nc.vector.tensor_tensor(up_l[:, u, :], s_sb[:, :], up_h[:, u, :], ALU.subtract) \
                                        .then_inc(S["up_lo"], 1)
                                    dve.wait_ge(S["up_lo"], chunk * KT + (u + 1))
                                else:
                                    m = u - KT
                                    dve.wait_ge(S["gemm_done"], chunk * NU + (u + 3))
                                    dve.wait_ge(S["acc_done"], chunk * KT + (m + 2))
                                    nc.vector.tensor_tensor(ft[:, m, :], ft[:, m, :], u_ps[:, u % 2, :], ALU.add) \
                                        .then_inc(S["acc_done"], 1)
                end_stage()
                norm_stage("mlp_post", ft, vec("norm_mlp_post"), None)


_INS = ["x", "norm_mix_pre", "norm_mix_post", "norm_mlp_pre", "norm_mlp_post", "w_in", "a_q_norm", "a_k_norm",
        "b_cq_norm", "b_ckv_norm", "b_w_uq", "b_w_ukv", "c_lambda_q1", "c_lambda_k1", "c_lambda_q2",
        "c_lambda_k2", "d_rel_bias", "g_out_a", "g_out_b", "g_out_c", "g_out_d", "w_out", "w_up", "w_down"]


def kernel(**inputs):
    import concourse.bacc as _bacc
    from concourse.bass_utils import run_bass_kernel_spmd as _run

    nc = _bacc.Bacc("TRN2", target_bir_lowering=False, num_devices=1)
    arrays = {}
    for name in _INS:
        v = np.ascontiguousarray(inputs[name])
        if name == "x":
            v = v.reshape(SEQ, D)
        if name == "d_rel_bias":
            v = v.reshape(DEPTH, REL_N)
        arrays[name] = v
    arrays.update(shape_constants())
    aps = {n: nc.dram_tensor(f"in_{n}", v.shape, F32, kind="ExternalInput").ap() for n, v in arrays.items()}
    out = nc.dram_tensor("out_x", (SEQ, D), F32, kind="ExternalOutput").ap()
    build(nc, aps, out)
    r = _run(nc, [{f"in_{n}": v for n, v in arrays.items()}], core_ids=[0])
    return r.results[0]["out_x"].reshape(1, SEQ, D)
```

```python
from contextlib import ExitStack
import math

import numpy as np
import concourse.bass as bass
from concourse import mybir

ALU = mybir.AluOpType
ACT = mybir.ActivationFunctionType
AX_X = mybir.AxisListType.X
F32 = mybir.dt.float32
F32R = mybir.dt.float32r

P = 128
SEQ, D, DEPTH = 1024, 1024, 2
NT = SEQ // P
KT = D // P
HALF = 512
HD = 64
GRID_W = 64
NHEAD = 4
B_Q, B_KV, B_ROPE = 3 * HD, 2 * HD, HD // 2
A0 = 0
B0 = A0 + 8 * HD
C0 = B0 + B_Q + B_KV + B_ROPE
D0 = C0 + 12 * HD
FF = 4 * D
FF_CHUNK = 1024
NA_R, NA_C = 8, 16
REL_C = 2 * NA_C - 1
REL_R = 2 * NA_R - 1
REL_N = NHEAD * REL_R * REL_C
EPS = 1e-6
NEG = -1e30
MIN_START = 3.0e38
REL_PAD = 64
REL_ROW = REL_N + 2 * REL_PAD
SKEW = 2 * GRID_W - 1


def shape_constants():
    t = np.arange(SEQ)

    def angles(pos, dim):
        inv = np.float32(10000.0) ** (-np.arange(0, dim, 2, dtype=np.float32) / np.float32(dim))
        return pos.astype(np.float32)[:, None] * inv[None, :].astype(np.float32)

    def both(ang):
        c, s = np.cos(ang), np.sin(ang)
        return np.concatenate([c, c], 1), np.concatenate([-s, s], 1)

    cr, sr = both(angles(t // GRID_W, HD // 2))
    cc, sc = both(angles(t % GRID_W, HD // 2))
    cb, sb = both(angles(t, B_ROPE))
    col = np.arange(GRID_W)
    first = np.clip(col - NA_C // 2, 0, GRID_W - NA_C)
    seen = (col[None, :] >= first[:, None]) & (col[None, :] < first[:, None] + NA_C)
    col_mask = np.where(seen, 0.0, -NEG)
    row_mask = np.zeros((2, 10))
    row_mask[0, 8:] = -NEG
    row_mask[1, 0] = -NEG
    row_mask[1, 9] = -NEG
    p, m = np.arange(P)[:, None], np.arange(2 * SEQ - P)[None, :]
    li = [0.8 - 0.6 * math.exp(-0.3 * l) for l in range(DEPTH)]
    tables = {
        "cos_a": np.concatenate([cr, cc], 1), "sin_a": np.concatenate([sr, sc], 1),
        "cos_sin_b": np.concatenate([cb.T, sb.T], 0),
        "col_mask": np.concatenate([col_mask, col_mask], 0),
        "row_mask": np.repeat(row_mask, GRID_W, 0),
        "distance": np.abs(p + (SEQ - P) - m),
        "slopes": np.array([[2.0 ** (-8.0 * (h + 1) / NHEAD) for h in range(NHEAD)]]),
        "lambda_init": np.array([[v, 1.0 - v] for v in li]),
    }
    return {k: np.ascontiguousarray(v, dtype=np.float32) for k, v in tables.items()}


SEMS = """w_landed_head w_landed0 w_landed1 w_hi w_lo gemm_done gemm_out tt_done tt_hi tt_lo
 x_landed0 x_landed1 x_landed2 x_landed3 x_landed4 x_landed5 x_landed6 x_landed7 gain_landed x_stored square_done norm_done gain_done hi_done lo_done tr_done ytr_done
 ysq_done ynorm_done xadd_done zero_done ft_free dve_step act_step pool_step pe_step const_landed
 scores_done max_done exp_done ptr_done pt_hi pt_lo pv_done ot_done o_done map_done
 stack_landed root_done yroot_done relu_done sq_done up_hi up_lo acc_done q_hi k_hi k_lo rope_done swap_done copy_landed prep_done prep2_done mix_sq""".split()


class Sems:

    def __init__(self, ctx, nc):
        handles = [ctx.enter_context(nc.semaphore(n)) for n in SEMS]
        self.by_name = dict(zip(SEMS, handles))
        nums = [h.num for h in handles]
        self.range = range(min(nums), max(nums) + 1)

    def __getitem__(self, name):
        return self.by_name[name]


def build(nc, a, out):
    with ExitStack() as ctx:
        S = Sems(ctx, nc)
        x_copied = ctx.enter_context(nc.semaphore("x_copied"))
        skew_landed = ctx.enter_context(nc.semaphore("skew_landed"))

        def sb(c, name, shape, dt=F32):
            return c.enter_context(nc.sbuf_tensor(name, shape, dt))

        def ps(c, name, shape, dt=F32):
            return c.enter_context(nc.psum_tensor(name, shape, dt))

        def end_stage():
            nc.all_engine_barrier(sems_to_clear=S.range)

        ident = sb(ctx, "ident", [P, P])
        fold = sb(ctx, "fold", [P, HD])
        ones = sb(ctx, "ones", [P, P])
        h_hi = sb(ctx, "h_hi", [P, KT, SEQ], F32R)
        h_lo = sb(ctx, "h_lo", [P, KT, SEQ], F32R)
        eps_col = sb(ctx, "eps_col", [P, 1])
        rel_scratch = nc.dram_tensor("rel_scratch", (DEPTH, REL_ROW), F32).ap()
        skew = nc.dram_tensor("skew", (DEPTH, NHEAD * REL_R, GRID_W, SKEW), F32).ap()

        with ExitStack() as c, nc.Block() as block:
            zero = sb(c, "zero", [DEPTH, REL_PAD])

            @block.sync
            def _(sp):
                sp.dma_start(out, a["x"]).then_inc(x_copied, 16)

            @block.scalar
            def _(act):
                act.wait_ge(S["const_landed"], 1)
                for at in (0, REL_PAD + REL_N):
                    act.dma_start(rel_scratch[:, at:at + REL_PAD], zero[:, :]).then_inc(S["copy_landed"], 16)
                act.dma_start(rel_scratch[:, REL_PAD:REL_PAD + REL_N], a["d_rel_bias"]).then_inc(S["copy_landed"], 16)
                act.wait_ge(S["copy_landed"], 48)
                for l in range(DEPTH):
                    src = bass.AP(rel_scratch.tensor, l * REL_ROW + REL_PAD + NA_C - GRID_W,
                                  [[REL_C, NHEAD * REL_R], [0, GRID_W], [1, SKEW]])
                    act.dma_start(skew[l], src).then_inc(skew_landed, 16)

            @block.vector
            def _(dve):
                nc.vector.memset(zero[:, :], 0.0).then_inc(S["const_landed"], 1)
                nc.vector.memset(ones[:, :], 1.0)
                nc.vector.memset(eps_col[:, :], EPS)

            @block.gpsimd
            def _(pool):
                nc.gpsimd.memset(ident[:, :], 0.0).then_inc(S["pool_step"], 1)
                nc.gpsimd.memset(fold[:, :], 0.0).then_inc(S["pool_step"], 1)
                pool.wait_ge(S["pool_step"], 2)
                nc.gpsimd.affine_select(out=ident[:, :], in_=ident[:, :], compare_op=ALU.not_equal, fill=1.0,
                                        base=0, pattern=[[-1, P]], channel_multiplier=1)
                nc.gpsimd.affine_select(out=fold[:, :], in_=fold[:, :], compare_op=ALU.not_equal, fill=1.0,
                                        base=0, pattern=[[-1, HD]], channel_multiplier=1).then_inc(S["pool_step"], 1)
                pool.wait_ge(S["pool_step"], 3)
                nc.gpsimd.affine_select(out=fold[:, :], in_=fold[:, :], compare_op=ALU.not_equal, fill=1.0,
                                        base=-HD, pattern=[[-1, HD]], channel_multiplier=1)
        end_stage()

        def weight_ring(c, tag, kt=KT):
            return (sb(c, f"w_raw_{tag}", [P, 2, kt, P]), sb(c, f"w_h_{tag}", [P, 2, kt, P], F32R),
                    sb(c, f"w_l_{tag}", [P, 2, kt, P], F32R))

        HEAD = 2

        def parts(units, u):
            shape = units[u][1]
            if u == 0 and shape == FULL:
                return [[(P, slice(0, HEAD))], [(P, slice(HEAD, KT))]]
            return [shape]

        def parts_done(units, n, rnd=None):
            count = sum(len(parts(units, u)) for u in range(n))
            return count if rnd is None else rnd * sum(len(parts(units, u)) for u in range(len(units))) + count

        def load_weights(sp, ring, units, rnd=None):
            raw = ring[0]
            for u, (pieces, _) in enumerate(units):
                if rnd is not None:
                    sp.wait_ge(S["w_lo"], parts_done(units, u - 1, rnd) + 2 if u >= 1
                               else rnd * parts_done(units, len(units)) + 1)
                elif u >= 2:
                    sp.wait_ge(S["w_lo"], parts_done(units, u - 1))
                for dst, src in pieces:
                    d = dst(raw[:, u % 2])
                    if len(parts(units, u)) > 1:
                        sp.dma_start(d[:, 0:HEAD], src[:, 0:HEAD]).then_inc(S["w_landed_head"], 16)
                        d, src = d[:, HEAD:], src[:, HEAD:]
                    sp.dma_start(d, src).then_inc(S[f"w_landed{u % 2}"], 16)

        def landed(units, u, rnd=None):
            count = 16 * sum(len(units[v][0]) for v in range(u % 2, u + 1, 2))
            return count if rnd is None else rnd * (16 * sum(len(units[v][0]) for v in range(u % 2, len(units), 2))) + count

        def split_hi(act, ring, units, u, rnd=None):
            raw, hi, _ = ring
            if rnd is not None:
                act.wait_ge(S["gemm_done"], rnd * len(units) + (u + 1))
            elif u >= 2:
                act.wait_ge(S["gemm_done"], u - 1)
            part_list = parts(units, u)
            for j, part in enumerate(part_list):
                if j < len(part_list) - 1:
                    act.wait_ge(S["w_landed_head"], 16 if rnd is None else rnd * 16 + 16)
                else:
                    act.wait_ge(S[f"w_landed{u % 2}"], landed(units, u, rnd))
                for rows, cols in part:
                    last = nc.scalar.activation(hi[0:rows, u % 2, cols, :], raw[0:rows, u % 2, cols, :], ACT.Copy)
                last.then_inc(S["w_hi"], 1)

        def split_lo(pool, ring, units, u, rnd=None):
            raw, hi, lo = ring
            for j, part in enumerate(parts(units, u)):
                pool.wait_ge(S["w_hi"], parts_done(units, u, rnd) + (j + 1))
                for rows, cols in part:
                    last = nc.gpsimd.tensor_tensor(lo[0:rows, u % 2, cols, :], raw[0:rows, u % 2, cols, :],
                                                   hi[0:rows, u % 2, cols, :], ALU.subtract)
                last.then_inc(S["w_lo"], 1)

        def products(pe, dst, ring, units, u, x_hi, x_lo, rnd=None, before={}):
            _, hi, lo = ring
            rows_of = [rows for rows, cols in units[u][1] for _ in range(cols.start, cols.stop)]
            starts = [part[0][1].start for part in parts(units, u)]
            for k, rows in enumerate(rows_of):
                if k in starts:
                    pe.wait_ge(S["w_lo"], parts_done(units, u, rnd) + (starts.index(k) + 1 + (0 if rnd is None else 2)))
                if k in before:
                    before[k]()
                wh, wl = hi[0:rows, u % 2, k, :], lo[0:rows, u % 2, k, :]
                for n in range(2):
                    o = dst[:, n * HALF:(n + 1) * HALF]
                    tok = slice(n * HALF, (n + 1) * HALF)
                    nc.tensor.matmul(o, wh, x_hi[0:rows, k, tok], start=(k == 0), stop=False)
                    nc.tensor.matmul(o, wh, x_lo[0:rows, k, tok], start=False, stop=False)
                for n in range(2):
                    last = nc.tensor.matmul(dst[:, n * HALF:(n + 1) * HALF], wl,
                                            x_hi[0:rows, k, n * HALF:(n + 1) * HALF],
                                            start=False, stop=(k == len(rows_of) - 1))
            last.then_inc(S["gemm_done"], 1)

        FULL = [(P, slice(0, KT))]

        def full_unit(src):
            return ([(lambda w: w, src.rearrange("(k p) n -> p k n", p=P))], FULL)

        def transposes(pe, dst, src_of, n=8):
            for i in range(n):
                last = nc.tensor.transpose(dst[:, i * P:(i + 1) * P], src_of(i), ident[:, :])
            return last

        def row_vector(src):
            return src.partition_broadcast(P)

        def root(act, ss, width):
            return nc.scalar.activation(ss, ss, ACT.Sqrt, scale=1.0 / width, bias=eps_col[:, 0:1])

        def rstd(dve, ss, step):
            nc.vector.reciprocal(ss, ss).then_inc(S["dve_step"], 1)
            dve.wait_ge(S["dve_step"], step + 1)
            return step + 1

        def norm_stage(tag, ft, post_gain, pre_gain):
            post, pre = ft is not None, pre_gain is not None
            lag = 2 if post else 0
            with ExitStack() as c, nc.Block() as block:
                x = sb(c, f"x_{tag}", [P, NT, D])
                junk = sb(c, f"junk_{tag}", [P, D])
                stat = sb(c, f"stat_{tag}", [P, 2, NT])
                if post:
                    g_post = sb(c, f"g_post_{tag}", [P, D])
                    y = sb(c, f"y_{tag}", [P, 2, D])
                    y_ps = ps(c, f"y_ps_{tag}", [P, 2, D])
                if pre:
                    g_pre = sb(c, f"g_pre_{tag}", [P, D])
                    hn = sb(c, f"hn_{tag}", [P, 2, D])
                    h_ps = ps(c, f"h_ps_{tag}", [P, 2, D])
                gains = 16 * (post + pre)
                rounds = NT + (lag + 1 if pre else 0)

                @block.sync
                def _(sp):
                    sp.wait_ge(x_copied, 16)
                    for t in range(NT):
                        sp.dma_start(x[:, t, :], out[t * P:(t + 1) * P, :]).then_inc(S[f"x_landed{t}"], 16)
                        if t == 0:
                            if post:
                                sp.dma_start(g_post[:, :], row_vector(post_gain)).then_inc(S["gain_landed"], 16)
                            if pre:
                                sp.dma_start(g_pre[:, :], row_vector(pre_gain)).then_inc(S["gain_landed"], 16)
                    if post:
                        for t in range(NT):
                            sp.wait_ge(S["xadd_done"], t + 1)
                            sp.dma_start(out[t * P:(t + 1) * P, :], x[:, t, :]).then_inc(S["x_stored"], 16)
                        sp.wait_ge(S["x_stored"], 16 * NT)

                @block.gpsimd
                def _(pool):
                    if post:
                        for t in range(NT):
                            pool.wait_ge(S[f"x_landed{t}"], 16)
                            pool.wait_ge(S["ynorm_done"], t + 1)
                            nc.gpsimd.tensor_tensor(x[:, t, :], x[:, t, :], y[:, t % 2, :],
                                                    ALU.add).then_inc(S["xadd_done"], 1)

                @block.tensor
                def _(pe):
                    for t in range(rounds):
                        if post and t < NT:
                            if t >= 2:
                                pe.wait_ge(S["ynorm_done"], t - 1)
                            transposes(pe, y_ps[:, t % 2, :], lambda m, t=t: ft[:, m, t * P:(t + 1) * P]) \
                                .then_inc(S["ytr_done"], 1)
                        s = t - lag - 1
                        if pre and s >= 0:
                            pe.wait_ge(S["norm_done"], s + 1)
                            if s >= 2:
                                pe.wait_ge(S["lo_done"], s - 1)
                            transposes(pe, h_ps[:, s % 2, :], lambda k, s=s: hn[:, s % 2, k * P:(k + 1) * P]) \
                                .then_inc(S["tr_done"], 1)

                @block.scalar
                def _(act):
                    for t in range(rounds):
                        if post and t < NT:
                            act.wait_ge(S["ytr_done"], t + 1)
                            nc.scalar.activation(junk[:, :], y_ps[:, t % 2, :], ACT.Square,
                                                 accum_out=stat[:, 0, t:t + 1]).then_inc(S["ysq_done"], 1)
                            act.wait_ge(S["ysq_done"], t + 1)
                            root(act, stat[:, 0, t:t + 1], D).then_inc(S["yroot_done"], 1)
                        s = t - lag
                        if pre and 0 <= s < NT:
                            act.wait_ge(*((S["xadd_done"], s + 1) if post else (S[f"x_landed{s}"], 16)))
                            nc.scalar.activation(junk[:, :], x[:, s, :], ACT.Square,
                                                 accum_out=stat[:, 1, s:s + 1]).then_inc(S["square_done"], 1)
                            act.wait_ge(S["square_done"], s + 1)
                            root(act, stat[:, 1, s:s + 1], D).then_inc(S["root_done"], 1)
                        s -= 1
                        if pre and s >= 0:
                            act.wait_ge(S["tr_done"], s + 1)
                            nc.scalar.activation(h_hi[:, :, s * P:(s + 1) * P],
                                                 h_ps[:, s % 2, :].rearrange("p (k n) -> p k n", k=KT),
                                                 ACT.Copy).then_inc(S["hi_done"], 1)

                @block.vector
                def _(dve):
                    step = 0
                    dve.wait_ge(S["gain_landed"], gains)
                    for t in range(rounds):
                        if post and t < NT:
                            dve.wait_ge(S["yroot_done"], t + 1)
                            step = rstd(dve, stat[:, 0, t:t + 1], step)
                            if t >= 2:
                                dve.wait_ge(S["xadd_done"], t - 1)
                            nc.vector.scalar_tensor_tensor(out=y[:, t % 2, :], in0=y_ps[:, t % 2, :],
                                                           scalar=stat[:, 0, t:t + 1], in1=g_post[:, :],
                                                           op0=ALU.mult, op1=ALU.mult).then_inc(S["ynorm_done"], 1)
                        s = t - lag
                        if pre and 0 <= s < NT:
                            dve.wait_ge(S["root_done"], s + 1)
                            step = rstd(dve, stat[:, 1, s:s + 1], step)
                            if s >= 2:
                                dve.wait_ge(S["tr_done"], s - 1)
                            nc.vector.scalar_tensor_tensor(out=hn[:, s % 2, :], in0=x[:, s, :],
                                                           scalar=stat[:, 1, s:s + 1], in1=g_pre[:, :],
                                                           op0=ALU.mult, op1=ALU.mult).then_inc(S["norm_done"], 1)
                        s -= 1
                        if pre and s >= 0:
                            dve.wait_ge(S["hi_done"], s + 1)
                            nc.vector.tensor_tensor(h_lo[:, :, s * P:(s + 1) * P],
                                                    h_ps[:, s % 2, :].rearrange("p (k n) -> p k n", k=KT),
                                                    h_hi[:, :, s * P:(s + 1) * P], ALU.subtract) \
                                .then_inc(S["lo_done"], 1)
            end_stage()

        def attention_stage(tag, maps, tiles, mix_cols, mix, combine=None):
            n_all = len(maps) * NT
            n_groups = n_all // 2
            kmax = max(t[1] for t in tiles)
            base_of = [min(tiles[i][0], tiles[i + 1][0]) for i in range(0, NT, 2)]
            value_steps = []
            for i in range(0, NT, 2):
                (f0, c0), (f1, c1) = tiles[i][0:2], tiles[i + 1][0:2]
                both = range(max(f0, f1), min(f0 + c0, f1 + c1))
                value_steps.append([(k, slice(0, 2 * P)) for k in both]
                                   + [(k, slice(0, P)) for k in range(f0, f0 + c0) if k not in both]
                                   + [(k, slice(P, 2 * P)) for k in range(f1, f1 + c1) if k not in both])
            kslots = max(k - b + 1 for b, steps in zip(base_of, value_steps) for k, _ in steps)
            with ExitStack() as c, nc.Block() as block:
                prob = sb(c, f"prob_{tag}", [P, 2, kmax * P])
                pt_h = sb(c, f"pt_h_{tag}", [P, 2, kslots, 2 * P], F32R)
                pt_l = sb(c, f"pt_l_{tag}", [P, 2, kslots, 2 * P], F32R)
                ot = sb(c, f"ot_{tag}", [P, 2, 2 * P])
                nmax = sb(c, f"nmax_{tag}", [P, n_all])
                z = sb(c, f"z_{tag}", [P, n_all])
                if combine is not None:
                    part = sb(c, f"part_{tag}", [P, 2, NT, HD])
                s_ps = ps(c, f"s_ps_{tag}", [P, 2, 2 * HALF])
                t_ps = ps(c, f"t_ps_{tag}", [P, 2, HALF])
                ot_ps = ps(c, f"ot_ps_{tag}", [P, HALF])
                o_ps = ps(c, f"o_ps_{tag}", [P, NT, HD])

                def seq(n):
                    return n // NT, n % NT

                piece_end = [0]
                for n in range(n_all):
                    piece_end.append(piece_end[-1] + -(-tiles[n % NT][1] // 4))

                def pieces(n):
                    cnt = tiles[n % NT][1]
                    return [(piece_end[n] + b, 4 * b, min(cnt, 4 * b + 4)) for b in range(-(-cnt // 4))]

                def turned(p, k0, k1):
                    return t_ps[:, p % 2, 0:(k1 - k0) * P].rearrange("p (k n) -> p k n", k=k1 - k0)

                @block.tensor
                def _(pe):
                    def scores(n):
                        m, i = seq(n)
                        first, cnt = tiles[i][0:2]
                        if n >= 2:
                            pe.wait_ge(S["exp_done"], n - 1)
                        q_of, k_of = maps[m][0], maps[m][1]
                        for at in range(0, cnt * P, HALF):
                            w = min(HALF, cnt * P - at)
                            for j, (q, k) in enumerate(zip(q_of, k_of)):
                                last = nc.tensor.matmul(s_ps[:, n % 2, at:at + w], q(i),
                                                        k(first * P + at, first * P + at + w),
                                                        start=(j == 0), stop=(j == len(q_of) - 1))
                        last.then_inc(S["scores_done"], 1)

                    def turn(n):
                        m, i = seq(n)
                        pe.wait_ge(S["exp_done"], n + 1)
                        for p, k0, k1 in pieces(n):
                            if p >= 2:
                                pe.wait_ge(S["pt_lo"], p - 1)
                            transposes(pe, t_ps[:, p % 2, :],
                                       lambda k: prob[:, n % 2, (k0 + k) * P:(k0 + k + 1) * P], k1 - k0) \
                                .then_inc(S["ptr_done"], 1)

                    def values(g, half):
                        m, i = seq(2 * g)
                        if half == 0:
                            pe.wait_ge(S["pt_lo"], piece_end[2 * g + 2])
                            if g >= 1:
                                pe.wait_ge(S["ot_done"], g)
                        v, steps = maps[m][2], value_steps[i // 2]
                        cut = (len(steps) + 1) // 2
                        for at in range(0, cut) if half == 0 else range(cut, len(steps)):
                            k, cols = steps[at]
                            for j, pt in enumerate((pt_h, pt_l)):
                                last = nc.tensor.matmul(ot_ps[:, cols], v[:, k, :],
                                                        pt[:, g % 2, k - base_of[i // 2], cols],
                                                        start=(at == 0 and j == 0),
                                                        stop=(at == len(steps) - 1 and j == 1))
                        if half == 1:
                            last.then_inc(S["pv_done"], 1)

                    def finish(g):
                        m, i = seq(2 * g)
                        pe.wait_ge(S["ot_done"], g + 1)
                        if m >= 1 and i == 0:
                            pe.wait_ge(S["map_done"], m)
                        for j in range(2):
                            last = nc.tensor.matmul(o_ps[:, i + j, :], ot[:, g % 2, j * P:(j + 1) * P],
                                                    fold[:, :], start=True, stop=True)
                        last.then_inc(S["o_done"], 1)

                    scores(0)
                    scores(1)
                    for n in range(n_all + 3):
                        if n + 2 < n_all:
                            scores(n + 2)
                        if n < n_all:
                            turn(n)
                        if 0 <= n // 2 - 1 < n_groups:
                            values(n // 2 - 1, n % 2)
                        if n >= 4 and n % 2 == 0:
                            finish(n // 2 - 2)

                @block.scalar
                def _(act):
                    def split(n):
                        m, i = seq(n)
                        g, j = n // 2, n % 2
                        off = tiles[i][0] - base_of[i // 2]
                        if j == 0 and g >= 2:
                            act.wait_ge(S["pv_done"], g - 1)
                        for p, k0, k1 in pieces(n):
                            act.wait_ge(S["ptr_done"], p + 1)
                            nc.scalar.activation(pt_h[:, g % 2, off + k0:off + k1, j * P:(j + 1) * P],
                                                 turned(p, k0, k1),
                                                 ACT.Copy).then_inc(S["pt_hi"], 1)

                    def lift(g):
                        act.wait_ge(S["pv_done"], g + 1)
                        if g >= 2:
                            act.wait_ge(S["o_done"], g - 1)
                        nc.scalar.activation(ot[:, g % 2, :], ot_ps[:, 0:2 * P], ACT.Copy) \
                            .then_inc(S["ot_done"], 1)

                    def exponential(n):
                        cnt = tiles[n % NT][1]
                        act.wait_ge(S["max_done"], n + 1)
                        if n >= 2:
                            act.wait_ge(S["ptr_done"], piece_end[n - 1])
                        nc.scalar.activation(prob[:, n % 2, 0:cnt * P], s_ps[:, n % 2, 0:cnt * P], ACT.Exp,
                                             scale=1.0 if tiles[n % NT][2] is None else -1.0, bias=nmax[:, n:n + 1], accum_out=z[:, n:n + 1]) \
                            .then_inc(S["exp_done"], 1)

                    exponential(0)
                    for n in range(n_all + 2):
                        if n + 1 < n_all:
                            exponential(n + 1)
                        if n < n_all:
                            split(n)
                        if n >= 3 and n % 2 == 1:
                            lift(n // 2 - 1)

                @block.vector
                def _(dve):
                    step = [0]

                    def after(ins):
                        step[0] += 1
                        ins.then_inc(S["dve_step"], 1)
                        dve.wait_ge(S["dve_step"], step[0])

                    def maximum(n):
                        m, i = seq(n)
                        first, cnt, bias = tiles[i]
                        dve.wait_ge(S["scores_done"], n + 1)
                        s = s_ps[:, n % 2, 0:cnt * P]
                        if bias is None:
                            nc.vector.tensor_reduce(nmax[:, n:n + 1], s, AX_X, ALU.max, negate=True) \
                                .then_inc(S["max_done"], 1)
                        else:
                            nc.vector.tensor_tensor_reduce(out=s, in0=s, in1=bias(m), scale=1.0,
                                                           scalar=MIN_START, op0=ALU.add, op1=ALU.min,
                                                           accum_out=nmax[:, n:n + 1]).then_inc(S["max_done"], 1)

                    def split(n):
                        m, i = seq(n)
                        g, j = n // 2, n % 2
                        off = tiles[i][0] - base_of[i // 2]
                        for p, k0, k1 in pieces(n):
                            dve.wait_ge(S["pt_hi"], p + 1)
                            at = (slice(None), g % 2, slice(off + k0, off + k1), slice(j * P, (j + 1) * P))
                            nc.vector.tensor_tensor(pt_l[at], turned(p, k0, k1), pt_h[at], ALU.subtract) \
                                .then_inc(S["pt_lo"], 1)

                    def divide(m):
                        zm = z[:, m * NT:(m + 1) * NT]
                        after(nc.vector.reciprocal(zm, zm))
                        dve.wait_ge(S["o_done"], (m + 1) * NT // 2)
                        zb = zm.unsqueeze(2).to_broadcast([P, NT, HD])
                        if combine is None:
                            nc.vector.tensor_tensor(mix[:, :, mix_cols(m)], o_ps[:, :, :], zb, ALU.mult) \
                                .then_inc(S["map_done"], 1)
                        else:
                            after(nc.vector.tensor_tensor(part[:, m % 2], o_ps[:, :, :], zb, ALU.mult))
                            if m % 2:
                                nc.vector.scalar_tensor_tensor(out=mix[:, :, mix_cols(m // 2)], in0=part[:, 1],
                                                               scalar=combine, in1=part[:, 0],
                                                               op0=ALU.mult, op1=ALU.add) \
                                    .then_inc(S["map_done"], 1)
                            else:
                                dve.sem_inc(S["map_done"], 1)

                    maximum(0)
                    maximum(1)
                    for n in range(n_all + 4):
                        if n + 2 < n_all:
                            maximum(n + 2)
                        if n < n_all:
                            split(n)
                        if n >= NT + 3 and (n - 3) % NT == 0:
                            divide((n - 3) // NT - 1)
            end_stage()

        def turn_values(pe, t_ps, u_sb, slot):
            return transposes(pe, t_ps[:, slot, :], lambda t: u_sb[:, slot, t * P:(t + 1) * P])

        with nc.Fori(0, DEPTH) as layer:
            def vec(name, lo=None, hi=None):
                v = a[name][bass.ds(layer, 1), :]
                return v if lo is None else v[:, lo:hi]

            norm_stage("mix_pre", None, None, vec("norm_mix_pre"))
            with ExitStack() as cm:
                mix = sb(cm, "mix", [P, NT, D])

                with ExitStack() as ca:
                    q_h = sb(ca, "a_q_h", [P, 4, SEQ], F32R)
                    q_l = sb(ca, "a_q_l", [P, 4, SEQ], F32R)
                    k_s = sb(ca, "a_k_s", [P, 2, SEQ], F32R)
                    v_s = sb(ca, "a_v_s", [P, 2, NT, P], F32R)
                    with ExitStack() as c, nc.Block() as block:
                        ring = weight_ring(c, "a")
                        u_sb = sb(c, "a_u", [P, 2, SEQ])
                        tok = sb(c, "a_tok", [P, NT, 3, HD])
                        sq = sb(c, "a_sq", [P, NT, 3, HD])
                        rot = sq
                        res = sb(c, "a_res", [P, NT, 3, 2, HD])
                        ss = sb(c, "a_ss", [P, 2, NT * 3])
                        gain = sb(c, "a_gain", [P, 3, HD])
                        cos = sb(c, "a_cos", [P, NT, HD])
                        sin = sb(c, "a_sin", [P, NT, HD])
                        u_ps = ps(c, "a_u_ps", [P, 2, SEQ])
                        t_ps = ps(c, "a_t_ps", [P, 2, SEQ])
                        w = a["w_in"][layer]
                        units = []
                        for kv in range(2):
                            units.append(full_unit(w[:, A0 + kv * P:A0 + (kv + 1) * P]))
                            units.append(([(lambda w_, j=j: w_[:, :, j * HD:(j + 1) * HD],
                                            w[:, A0 + (4 + 2 * j + kv) * HD:A0 + (5 + 2 * j + kv) * HD]
                                            .rearrange("(k p) n -> p k n", p=P)) for j in range(2)], FULL))
                        back = [[t_ps[:, 0, :], t_ps[:, 1, :], u_ps[:, 0, :]],
                                [u_ps[:, 0, :], u_ps[:, 1, :], t_ps[:, 0, :]]]

                        def dst_h(kv, h):
                            return q_h[:, 2 * kv + h, :] if h < 2 else k_s[:, kv, :]

                        def v_part(t):
                            return t.rearrange("p (t d) -> p t d", t=NT)

                        @block.sync
                        def _(sp):
                            load_weights(sp, ring, units)
                            for dst, name in ((cos, "cos_a"), (sin, "sin_a")):
                                sp.dma_start(dst[:, :, :], a[name].rearrange("(t p) d -> p t d", p=P)) \
                                    .then_inc(S["const_landed"], 16)
                            for h in range(3):
                                sp.dma_start(gain[:, h, :], row_vector(vec("a_k_norm" if h == 2 else "a_q_norm"))) \
                                    .then_inc(S["const_landed"], 16)

                        @block.gpsimd
                        def _(pool):
                            for u in range(4):
                                split_lo(pool, ring, units, u)

                        @block.tensor
                        def _(pe):
                            def turn(u):
                                pe.wait_ge(S["gemm_out"], u + 1)
                                if u >= 2:
                                    pe.wait_ge(S["lo_done"], u - 1)
                                turn_values(pe, t_ps, u_sb, u % 2).then_inc(S["tt_done"], 1)

                            def turn_back(kv):
                                pe.wait_ge(S["prep_done"], kv + 1)
                                pe.wait_ge(S["gemm_out"], 3 + kv)
                                if kv == 1:
                                    pe.wait_ge(S["lo_done"], 3)
                                for h in range(3):
                                    transposes(pe, back[kv][h], lambda t: res[:, t, h].rearrange("p a d -> p (a d)")) \
                                        .then_inc(S["ptr_done"], 1)

                            def product(u, before):
                                if u >= 2:
                                    pe.wait_ge(S["gemm_out"], u - 1)
                                products(pe, u_ps[:, u % 2, :], ring, units, u, h_hi, h_lo, before=before)

                            product(0, {})
                            product(1, {HEAD: lambda: turn(0)})
                            product(2, {HEAD: lambda: turn(1)})
                            product(3, {KT - 1: lambda: turn_back(0)})
                            turn(2)
                            turn(3)
                            turn_back(1)

                        @block.scalar
                        def _(act):
                            def unit_out(u):
                                act.wait_ge(S["gemm_done"], u + 1)
                                if u >= 2:
                                    act.wait_ge(S["tt_done"], u - 1)
                                nc.scalar.activation(u_sb[:, u % 2, :], u_ps[:, u % 2, :], ACT.Copy) \
                                    .then_inc(S["gemm_out"], 1)

                            def value_hi(kv):
                                act.wait_ge(S["tt_done"], 2 * kv + 2)
                                nc.scalar.activation(v_s[:, kv, :, 0:HD], v_part(t_ps[:, 1, :])[:, :, HD:P],
                                                     ACT.Copy).then_inc(S["tt_hi"], 1)

                            def mean_root(kv):
                                act.wait_ge(S["square_done"], kv + 1)
                                root(act, ss[:, kv, :], HD).then_inc(S["root_done"], 1)

                            def back_hi(kv):
                                for h in range(3):
                                    act.wait_ge(S["ptr_done"], 3 * kv + h + 1)
                                    nc.scalar.activation(dst_h(kv, h), back[kv][h], ACT.Copy,
                                                         scale=HD ** -0.5 if h < 2 else 1.0).then_inc(S["hi_done"], 1)

                            split_hi(act, ring, units, 0)
                            split_hi(act, ring, units, 1)
                            unit_out(0)
                            split_hi(act, ring, units, 2)
                            unit_out(1)
                            split_hi(act, ring, units, 3)
                            value_hi(0)
                            mean_root(0)
                            unit_out(2)
                            back_hi(0)
                            unit_out(3)
                            value_hi(1)
                            mean_root(1)
                            back_hi(1)

                        @block.vector
                        def _(dve):
                            step = [0]

                            def after(ins):
                                step[0] += 1
                                ins.then_inc(S["dve_step"], 1)
                                dve.wait_ge(S["dve_step"], step[0])

                            flat = tok[:, :, :, :].rearrange("p t h d -> p (t h) d")
                            by_token = tok[:, :, :, :].rearrange("p t h d -> p t (h d)")
                            sq_flat = sq[:, :, :, :].rearrange("p t h d -> p (t h) d")

                            for kv in range(2):
                                dve.wait_ge(S["tt_done"], 2 * kv + 1)
                                nc.vector.tensor_copy(tok[:, :, 0:2, :].rearrange("p t h d -> p t (h d)"),
                                                      v_part(t_ps[:, 0, :])).then_inc(S["dve_step"], 1)
                                dve.wait_ge(S["tt_hi"], kv + 1)
                                nc.vector.tensor_copy(tok[:, :, 2, :], v_part(t_ps[:, 1, :])[:, :, 0:HD]) \
                                    .then_inc(S["dve_step"], 1)
                                nc.vector.tensor_tensor(v_s[:, kv, :, HD:P], v_part(t_ps[:, 1, :])[:, :, HD:P],
                                                        v_s[:, kv, :, 0:HD], ALU.subtract)
                                step[0] += 2
                                dve.wait_ge(S["dve_step"], step[0])
                                after(nc.vector.tensor_tensor(sq_flat, flat, flat, ALU.mult))
                                nc.vector.tensor_reduce(ss[:, kv, :], sq_flat, AX_X, ALU.add).then_inc(S["square_done"], 1)
                                dve.wait_ge(S["square_done"], kv + 1)
                                dve.wait_ge(S["const_landed"], 80)
                                gb = gain[:, :, :].rearrange("p h d -> p (h d)").unsqueeze(1).to_broadcast([P, NT, 3 * HD])
                                after(nc.vector.tensor_tensor(by_token, by_token, gb, ALU.mult))
                                dve.wait_ge(S["root_done"], kv + 1)
                                step[0] = rstd(dve, ss[:, kv, :], step[0])
                                after(nc.vector.tensor_tensor(flat, flat, ss[:, kv, :].unsqueeze(2)
                                                              .to_broadcast([P, NT * 3, HD]), ALU.mult))
                                q4 = HD // 4
                                for d0 in range(0, HD, 2 * q4):
                                    for f, g in ((d0, d0 + q4), (d0 + q4, d0)):
                                        nc.vector.tensor_tensor(
                                            rot[:, :, :, f:f + q4], tok[:, :, :, g:g + q4],
                                            sin[:, :, f:f + q4].unsqueeze(2).to_broadcast([P, NT, 3, q4]), ALU.mult) \
                                            .then_inc(S["dve_step"], 1)
                                        step[0] += 1
                                dve.wait_ge(S["dve_step"], step[0])
                                after(nc.vector.tensor_tensor(tok[:, :, :, :], tok[:, :, :, :],
                                                              cos[:, :, :].unsqueeze(2).to_broadcast([P, NT, 3, HD]), ALU.mult))
                                if kv == 1:
                                    dve.wait_ge(S["ptr_done"], 3)
                                for j in range(2):
                                    last = nc.vector.tensor_tensor(res[:, :, :, j, :].rearrange("p t h d -> p (t h) d"),
                                                                   flat, sq_flat, ALU.add)
                                last.then_inc(S["prep_done"], 1)
                                for h in range(2):
                                    dve.wait_ge(S["hi_done"], 3 * kv + h + 1)
                                    nc.vector.scalar_tensor_tensor(out=q_l[:, 2 * kv + h, :], in0=back[kv][h],
                                                                   scalar=HD ** -0.5, in1=dst_h(kv, h), op0=ALU.mult,
                                                                   op1=ALU.subtract).then_inc(S["lo_done"], 1)
                                dve.wait_ge(S["hi_done"], 3 * kv + 3)
                                nc.vector.tensor_tensor(k_s[HD:P, kv, :], back[kv][2][HD:P, :], k_s[HD:P, kv, :],
                                                        ALU.subtract).then_inc(S["lo_done"], 1)
                    end_stage()
                    maps = [([lambda i, m=m: q_h[:, m, i * P:(i + 1) * P], lambda i, m=m: q_l[:, m, i * P:(i + 1) * P]],
                             [lambda x0, x1, m=m: k_s[:, m // 2, x0:x1]] * 2, v_s[:, m // 2]) for m in range(4)]
                    attention_stage("a", maps, [(0, NT, None)] * NT, lambda m: slice(m * HD, (m + 1) * HD), mix)

                with ExitStack() as cb:
                    cq_h = sb(cb, "cq_h", [P, 2, SEQ], F32R)
                    cq_l = sb(cb, "cq_l", [P, 2, SEQ], F32R)
                    ckv_h = sb(cb, "ckv_h", [P, 1, SEQ], F32R)
                    ckv_l = sb(cb, "ckv_l", [P, 1, SEQ], F32R)
                    k_h = sb(cb, "b_k_h", [P, 2, SEQ], F32R)
                    k_l = sb(cb, "b_k_l", [P, 2, SEQ], F32R)
                    R0, R1 = HD, HD + B_ROPE
                    with ExitStack() as c, nc.Block() as block:
                        ring = weight_ring(c, "b")
                        k_rope = sb(c, "k_rope", [P, SEQ])
                        cs = sb(c, "cos_sin", [P, SEQ])
                        u_sb = sb(c, "b_u", [P, 3, SEQ])
                        sq = sb(c, "b_sq", [P, 3, SEQ])
                        r_sb = sb(c, "b_r", [P, 2, SEQ])
                        g_col = sb(c, "b_g", [P, 3])
                        rt = sb(c, "b_rt", [P, SEQ])
                        u_ps = ps(c, "b_u_ps", [P, 2, SEQ])
                        r_ps = ps(c, "b_r_ps", [P, 2, SEQ])
                        w = a["w_in"][layer]

                        def cols(c0, n):
                            return w[:, c0:c0 + n].rearrange("(k p) n -> p k n", p=P)

                        half = B_ROPE // 2
                        kr = B0 + B_Q + B_KV
                        units = [full_unit(w[:, B0:B0 + P]),
                                 ([(lambda w_: w_[:, :, 0:HD], cols(B0 + P, HD)),
                                   (lambda w_: w_[:, :, R0:R1], cols(kr, B_ROPE)),
                                   (lambda w_: w_[:, :, R1:R1 + half], cols(kr + half, half)),
                                   (lambda w_: w_[:, :, R1 + half:P], cols(kr, half))], FULL),
                                 full_unit(w[:, B0 + B_Q:B0 + B_Q + P])]

                        @block.sync
                        def _(sp):
                            load_weights(sp, ring, units)
                            sp.dma_start(cs[HD:P, :], a["cos_sin_b"]).then_inc(S["const_landed"], 16)
                            col = lambda v: v.rearrange("a p -> p a")
                            sp.dma_start(g_col[:, 0:1], col(vec("b_cq_norm", 0, P))).then_inc(S["const_landed"], 16)
                            sp.dma_start(g_col[0:HD, 1:2], col(vec("b_cq_norm", P, B_Q))).then_inc(S["const_landed"], 16)
                            sp.dma_start(g_col[:, 2:3], col(vec("b_ckv_norm"))).then_inc(S["const_landed"], 16)

                        @block.gpsimd
                        def _(pool):
                            for u in range(3):
                                split_lo(pool, ring, units, u)

                        @block.tensor
                        def _(pe):
                            def sums(r):
                                rows_of = (((0, P), (1, HD)), ((2, P),))[r]
                                pe.wait_ge(S["square_done"], 2 + r)
                                for n in range(2):
                                    for j, (u, rows) in enumerate(rows_of):
                                        last = nc.tensor.matmul(r_ps[:, r, n * HALF:(n + 1) * HALF], ones[0:rows, :],
                                                                sq[0:rows, u, n * HALF:(n + 1) * HALF],
                                                                start=(j == 0), stop=(j == len(rows_of) - 1))
                                last.then_inc(S["pe_step"], 1)

                            for u in range(3):
                                if u == 2:
                                    pe.wait_ge(S["gemm_out"], 1)
                                    pe.wait_ge(S["square_done"], 1)
                                products(pe, u_ps[:, u % 2, :], ring, units, u, h_hi, h_lo,
                                         before={KT // 2: lambda: sums(0)} if u == 2 else {})
                            sums(1)

                        @block.scalar
                        def _(act):
                            def unit_out(u):
                                act.wait_ge(S["gemm_done"], u + 1)
                                nc.scalar.activation(u_sb[:, u, :], u_ps[:, u % 2, :], ACT.Copy).then_inc(S["gemm_out"], 1)
                                nc.scalar.activation(sq[:, u, :], u_ps[:, u % 2, :], ACT.Square) \
                                    .then_inc(S["square_done"], 1)

                            def mean_root(r, width):
                                act.wait_ge(S["pe_step"], r + 1)
                                nc.scalar.activation(r_sb[:, r, :], r_ps[:, r, :], ACT.Sqrt, scale=1.0 / width,
                                                     bias=eps_col[:, 0:1]).then_inc(S["root_done"], 1)

                            def high(j, dst):
                                act.wait_ge(S["norm_done"], j + 1)
                                nc.scalar.activation(dst, u_sb[0:dst.shape[0], j, :], ACT.Copy).then_inc(S["hi_done"], 1)

                            split_hi(act, ring, units, 0)
                            split_hi(act, ring, units, 1)
                            unit_out(0)
                            split_hi(act, ring, units, 2)
                            unit_out(1)
                            act.wait_ge(S["rope_done"], 1)
                            for e in range(2):
                                nc.scalar.activation(k_h[R0:R1, e, :], k_rope[R0:R1, :], ACT.Copy).then_inc(S["k_hi"], 1)
                            mean_root(0, B_Q)
                            unit_out(2)
                            mean_root(1, B_KV)
                            high(0, cq_h[:, 0, :])
                            high(1, cq_h[0:HD, 1, :])
                            high(2, ckv_h[:, 0, :])

                        @block.vector
                        def _(dve):
                            step = 0
                            dve.wait_ge(S["const_landed"], 64)
                            dve.wait_ge(S["gemm_out"], 2)
                            nc.vector.tensor_tensor(k_rope[R0:R1, :], u_sb[R0:R1, 1, :], cs[R0:R1, :],
                                                    ALU.mult).then_inc(S["prep_done"], 1)
                            nc.vector.tensor_tensor(rt[R0:R1, :], u_sb[R1:P, 1, :], cs[R1:P, :],
                                                    ALU.mult).then_inc(S["prep_done"], 1)
                            dve.wait_ge(S["prep_done"], 2)
                            nc.vector.tensor_tensor(k_rope[R0:R1, :], k_rope[R0:R1, :], rt[R0:R1, :], ALU.add) \
                                .then_inc(S["rope_done"], 1)
                            for e in range(2):
                                dve.wait_ge(S["k_hi"], e + 1)
                                nc.vector.tensor_tensor(k_l[R0:R1, e, :], k_rope[R0:R1, :], k_h[R0:R1, e, :],
                                                        ALU.subtract)
                            for r in range(2):
                                dve.wait_ge(S["root_done"], r + 1)
                                step = rstd(dve, r_sb[:, r, :], step)
                                for u, rows in (((0, P), (1, HD)) if r == 0 else ((2, P),)):
                                    nc.vector.scalar_tensor_tensor(out=u_sb[0:rows, u, :], in0=u_sb[0:rows, u, :],
                                                                   scalar=g_col[0:rows, u:u + 1], in1=r_sb[0:rows, r, :],
                                                                   op0=ALU.mult, op1=ALU.mult) \
                                        .then_inc(S["norm_done"], 1)
                            for j, (hi, lo) in enumerate(((cq_h[:, 0, :], cq_l[:, 0, :]),
                                                          (cq_h[0:HD, 1, :], cq_l[0:HD, 1, :]),
                                                          (ckv_h[:, 0, :], ckv_l[:, 0, :]))):
                                dve.wait_ge(S["hi_done"], j + 1)
                                nc.vector.tensor_tensor(lo, u_sb[0:hi.shape[0], j, :], hi, ALU.subtract)
                    end_stage()

                    with nc.Fori(0, 2) as pair, ExitStack() as ch:
                        q_h = sb(ch, "b_q_h", [P, 2, SEQ], F32R)
                        q_l = sb(ch, "b_q_l", [P, 2, SEQ], F32R)
                        v_s = sb(ch, "b_v_s", [P, 2, NT, P], F32R)
                        QK = HD + B_ROPE
                        with ExitStack() as c, nc.Block() as block:
                            ring = weight_ring(c, "bh", 2)
                            u_sb = sb(c, "bh_u", [P, 4, SEQ])
                            rt = sb(c, "bh_rt", [P, 2, SEQ])
                            cs = sb(c, "bh_cos_sin", [P, SEQ])
                            u_ps = ps(c, "bh_u_ps", [P, 2, SEQ])
                            t_ps = ps(c, "bh_t_ps", [P, 2, SEQ])
                            wq, wkv = a["b_w_uq"][layer], a["b_w_ukv"][layer]
                            half = B_ROPE // 2

                            def q_piece(e, k, rows, d0, d1, c0):
                                return (lambda w_: w_[0:rows, k, d0:d1],
                                        wq[k * P:k * P + rows, bass.ds(pair * (2 * QK) + (e * QK + c0), d1 - d0)])

                            units = []
                            for e in range(2):
                                units.append(([q_piece(e, k, rows, d0, d1, c0) for k, rows in ((0, P), (1, HD))
                                               for d0, d1, c0 in ((0, QK, 0), (QK, QK + half, HD + half),
                                                                  (QK + half, P, HD))],
                                              [(P, slice(0, 1)), (HD, slice(1, 2))]))
                                units.append(([(lambda w_: w_[:, 0, :], wkv[:, bass.ds(pair * (2 * P) + e * P, P)])],
                                              [(P, slice(0, 1))]))

                            def values_of(t):
                                return t.rearrange("p (t d) -> p t d", t=NT)[:, :, HD:P]

                            @block.sync
                            def _(sp):
                                load_weights(sp, ring, units)
                                sp.dma_start(cs[HD:P, :], a["cos_sin_b"]).then_inc(S["const_landed"], 16)

                            @block.gpsimd
                            def _(pool):
                                for u in range(4):
                                    split_lo(pool, ring, units, u)
                                    if u % 2:
                                        pool.wait_ge(S["w_lo"], u + 1)
                                        pool.wait_ge(S["const_landed"], 16)
                                        pool.wait_ge(S["gemm_out"], u)
                                        nc.gpsimd.tensor_tensor(rt[R0:R1, u // 2, :], u_sb[R1:P, u - 1, :], cs[R1:P, :],
                                                                ALU.mult).then_inc(S["swap_done"], 1)
                                        pool.wait_ge(S["swap_done"], u // 2 + 1)

                            @block.tensor
                            def _(pe):
                                for e in range(2):
                                    if e:
                                        pe.wait_ge(S["gemm_out"], 1)
                                    products(pe, u_ps[:, 0, :], ring, units, 2 * e, cq_h, cq_l)
                                    if e:
                                        pe.wait_ge(S["gemm_out"], 2)
                                        pe.wait_ge(S["k_lo"], 1)
                                    products(pe, u_ps[:, 1, :], ring, units, 2 * e + 1, ckv_h, ckv_l)
                                    pe.wait_ge(S["gemm_out"], 2 * e + 2)
                                    transposes(pe, t_ps[:, e, :], lambda t: u_sb[:, 2 * e + 1, t * P:(t + 1) * P]) \
                                        .then_inc(S["tt_done"], 1)

                            @block.scalar
                            def _(act):
                                def query_out(e):
                                    act.wait_ge(S["gemm_done"], 2 * e + 1)
                                    nc.scalar.activation(u_sb[:, 2 * e, :], u_ps[:, 0, :], ACT.Copy, scale=QK ** -0.5) \
                                        .then_inc(S["gemm_out"], 1)

                                def key_value_out(e):
                                    act.wait_ge(S["gemm_done"], 2 * e + 2)
                                    nc.scalar.activation(u_sb[:, 2 * e + 1, :], u_ps[:, 1, :], ACT.Copy) \
                                        .then_inc(S["gemm_out"], 1)
                                    nc.scalar.activation(k_h[0:HD, e, :], u_ps[0:HD, 1, :], ACT.Copy) \
                                        .then_inc(S["k_hi"], 1)

                                def value_hi(e):
                                    act.wait_ge(S["tt_done"], e + 1)
                                    nc.scalar.activation(v_s[:, e, :, 0:HD], values_of(t_ps[:, e, :]), ACT.Copy) \
                                        .then_inc(S["tt_hi"], 1)

                                def query_hi(e):
                                    act.wait_ge(S["rope_done"], e + 1)
                                    nc.scalar.activation(q_h[0:QK, e, :], u_sb[0:QK, 2 * e, :], ACT.Copy) \
                                        .then_inc(S["q_hi"], 1)

                                split_hi(act, ring, units, 0)
                                split_hi(act, ring, units, 1)
                                query_out(0)
                                split_hi(act, ring, units, 2)
                                key_value_out(0)
                                split_hi(act, ring, units, 3)
                                query_out(1)
                                value_hi(0)
                                query_hi(0)
                                key_value_out(1)
                                value_hi(1)
                                query_hi(1)

                            @block.vector
                            def _(dve):
                                def rope(e):
                                    dve.wait_ge(S["gemm_out"], 2 * e + 1)
                                    nc.vector.tensor_tensor(u_sb[R0:R1, 2 * e, :], u_sb[R0:R1, 2 * e, :], cs[R0:R1, :],
                                                            ALU.mult).then_inc(S["dve_step"], 1)
                                    dve.wait_ge(S["dve_step"], e + 1)
                                    dve.wait_ge(S["swap_done"], e + 1)
                                    nc.vector.tensor_tensor(u_sb[R0:R1, 2 * e, :], u_sb[R0:R1, 2 * e, :], rt[R0:R1, e, :],
                                                            ALU.add).then_inc(S["rope_done"], 1)

                                def key_lo(e):
                                    dve.wait_ge(S["k_hi"], e + 1)
                                    nc.vector.tensor_tensor(k_l[0:HD, e, :], u_ps[0:HD, 1, :], k_h[0:HD, e, :],
                                                            ALU.subtract).then_inc(S["k_lo"], 1)

                                def value_lo(e):
                                    dve.wait_ge(S["tt_hi"], e + 1)
                                    nc.vector.tensor_tensor(v_s[:, e, :, HD:P], values_of(t_ps[:, e, :]),
                                                            v_s[:, e, :, 0:HD], ALU.subtract)

                                def query_lo(e):
                                    dve.wait_ge(S["q_hi"], e + 1)
                                    nc.vector.tensor_tensor(q_l[0:QK, e, :], u_sb[0:QK, 2 * e, :], q_h[0:QK, e, :],
                                                            ALU.subtract)

                                dve.wait_ge(S["const_landed"], 16)
                                rope(0)
                                key_lo(0)
                                rope(1)
                                value_lo(0)
                                query_lo(0)
                                key_lo(1)
                                value_lo(1)
                                query_lo(1)
                        end_stage()

                        def b_map(e):
                            qh = lambda i: q_h[0:QK, e, i * P:(i + 1) * P]
                            ql = lambda i: q_l[0:QK, e, i * P:(i + 1) * P]
                            kh = lambda x0, x1: k_h[0:QK, e, x0:x1]
                            kl = lambda x0, x1: k_l[0:QK, e, x0:x1]
                            return ([qh, qh, ql], [kh, kl, kh], v_s[:, e])

                        attention_stage("b", [b_map(0), b_map(1)], [(0, NT, None)] * NT,
                                        lambda m: bass.ds(pair * P + (4 + m) * HD, HD), mix)

                def pair_stage(tag, c0, pair, scale, stack, v_s, extra_dma, extra_act, extra_dve):
                    with ExitStack() as c, nc.Block() as block:
                        ring = weight_ring(c, tag)
                        p_h = sb(c, f"{tag}_p_h", [P, 2, SEQ], F32R)
                        p_l = sb(c, f"{tag}_p_l", [P, 2, SEQ], F32R)
                        u_sb = sb(c, f"{tag}_u", [P, 1, SEQ])
                        u_ps = ps(c, f"{tag}_u_ps", [P, 3, SEQ])
                        t_ps = ps(c, f"{tag}_t_ps", [P, 1, SEQ])
                        w = a["w_in"][layer]
                        units = [full_unit(w[:, bass.ds(pair * P + (c0 + j * 4 * HD), P)]) for j in range(3)]

                        @block.sync
                        def _(sp):
                            load_weights(sp, ring, units)
                            extra_dma(sp)
                            sent = 0
                            for j in range(2):
                                sp.wait_ge(S["hi_done"], j + 1)
                                sp.wait_ge(S["lo_done"], j + 1)
                                copies = stack(p_h[:, j], p_l[:, j], j == 1)
                                sent += len(copies)
                                for dst, src in copies:
                                    sp.dma_start(dst.bitcast(F32), src.bitcast(F32)).then_inc(S["stack_landed"], 16)
                            sp.wait_ge(S["stack_landed"], 16 * sent)

                        @block.gpsimd
                        def _(pool):
                            for u in range(3):
                                split_lo(pool, ring, units, u)

                        @block.tensor
                        def _(pe):
                            for u in range(3):
                                products(pe, u_ps[:, u, :], ring, units, u, h_hi, h_lo)
                            pe.wait_ge(S["gemm_out"], 1)
                            turn_values(pe, t_ps, u_sb, 0).then_inc(S["tt_done"], 1)

                        @block.scalar
                        def _(act):
                            split_hi(act, ring, units, 0)
                            split_hi(act, ring, units, 1)
                            extra_act(act)
                            act.wait_ge(S["gemm_done"], 1)
                            nc.scalar.activation(p_h[:, 0, :], u_ps[:, 0, :], ACT.Copy, scale=scale) \
                                .then_inc(S["hi_done"], 1)
                            split_hi(act, ring, units, 2)
                            act.wait_ge(S["gemm_done"], 2)
                            nc.scalar.activation(p_h[:, 1, :], u_ps[:, 1, :], ACT.Copy).then_inc(S["hi_done"], 1)
                            act.wait_ge(S["gemm_done"], 3)
                            nc.scalar.activation(u_sb[:, 0, :], u_ps[:, 2, :], ACT.Copy).then_inc(S["gemm_out"], 1)
                            act.wait_ge(S["tt_done"], 1)
                            nc.scalar.activation(v_s[:, :, :, 0:HD],
                                                 t_ps[:, 0, :].rearrange("p (t h d) -> p t h d", t=NT, h=2),
                                                 ACT.Copy).then_inc(S["tt_hi"], 1)

                        @block.vector
                        def _(dve):
                            extra_dve[0](dve)
                            for j in range(2):
                                if j == 1:
                                    extra_dve[1](dve)
                                dve.wait_ge(S["hi_done"], j + 1)
                                nc.vector.scalar_tensor_tensor(out=p_l[:, j, :], in0=u_ps[:, j, :],
                                                               scalar=1.0 if j else scale, in1=p_h[:, j, :],
                                                               op0=ALU.mult, op1=ALU.subtract).then_inc(S["lo_done"], 1)
                            dve.wait_ge(S["tt_hi"], 1)
                            nc.vector.tensor_tensor(v_s[:, :, :, HD:P],
                                                    t_ps[:, 0, :].rearrange("p (t h d) -> p t h d", t=NT, h=2),
                                                    v_s[:, :, :, 0:HD], ALU.subtract)
                    end_stage()

                with ExitStack() as cc:
                    lam = sb(cc, "lam", [P, 1])
                    nd = sb(cc, "distance", [P, 2 * SEQ - P])
                    lv = sb(cc, "lam_vec", [P, 4, HD // 2])
                    lj = sb(cc, "lam_junk", [P, HD // 2])
                    ls = sb(cc, "lam_sum", [P, 2])
                    li = sb(cc, "lam_init", [P, 2])

                    with nc.Fori(0, 2) as pair, ExitStack() as ch:
                        qs = sb(ch, "c_q_s", [P, 4, SEQ], F32R)
                        ks = sb(ch, "c_k_s", [P, 4, SEQ], F32R)
                        v_s = sb(ch, "c_v_s", [P, NT, 2, P], F32R)
                        alibi = sb(ch, "alibi", [P, 2, 2 * SEQ - P])
                        slope = sb(ch, "slope", [P, 2])
                        W = HD // 2

                        def stack(hi, lo, is_k):
                            order = (hi, lo, hi, lo) if is_k else (hi, hi, lo, lo)
                            dst = ks if is_k else qs
                            return [(dst[r * W:(r + 1) * W, m, :], src[m * W:(m + 1) * W, :])
                                    for m in range(4) for r, src in enumerate(order)]

                        def extra_dma(sp):
                            sp.dma_start(nd[:, :], a["distance"]).then_inc(S["const_landed"], 16)
                            sp.dma_start(slope[:, :], row_vector(a["slopes"][:, bass.ds(pair * 2, 2)])) \
                                .then_inc(S["const_landed"], 16)
                            sp.dma_start(li[:, :], row_vector(vec("lambda_init"))).then_inc(S["gain_landed"], 16)
                            for j, name in enumerate(("c_lambda_q1", "c_lambda_k1", "c_lambda_q2", "c_lambda_k2")):
                                sp.dma_start(lv[:, j, :], row_vector(vec(name))).then_inc(S["gain_landed"], 16)

                        def biases(act):
                            act.wait_ge(S["const_landed"], 32)
                            for j in range(2):
                                nc.scalar.activation(alibi[:, j, :], nd[:, :], ACT.Copy, scale=slope[:, j:j + 1])
                            act.wait_ge(S["dve_step"], 2)
                            nc.scalar.activation(ls[:, :], ls[:, :], ACT.Exp).then_inc(S["exp_done"], 1)

                        def lambda_sums(dve):
                            dve.wait_ge(S["gain_landed"], 80)
                            for j in range(2):
                                nc.vector.tensor_tensor_reduce(out=lj[:, :], in0=lv[:, 2 * j, :], in1=lv[:, 2 * j + 1, :],
                                                               scale=1.0, scalar=0.0, op0=ALU.mult, op1=ALU.add,
                                                               accum_out=ls[:, j:j + 1]).then_inc(S["dve_step"], 1)
                                dve.wait_ge(S["dve_step"], j + 1)

                        def lambda_difference(dve):
                            dve.wait_ge(S["exp_done"], 1)
                            nc.vector.tensor_tensor(lam[:, :], ls[:, 1:2], ls[:, 0:1], ALU.subtract) \
                                .then_inc(S["dve_step"], 1)
                            dve.wait_ge(S["dve_step"], 3)
                            nc.vector.tensor_tensor(lam[:, :], lam[:, :], li[:, 0:1], ALU.subtract)

                        pair_stage("c", C0, pair, -W ** -0.5, stack, v_s, extra_dma, biases,
                                   (lambda_sums, lambda_difference))
                        maps = [([lambda i, m=m: qs[:, m, i * P:(i + 1) * P]],
                                 [lambda x0, x1, m=m: ks[:, m, x0:x1]], v_s[:, :, m // 2, :]) for m in range(4)]
                        tiles = [(0, NT, lambda m, i=i: alibi[:, m // 2, (SEQ - P) - i * P:(SEQ - P) - i * P + SEQ])
                                 for i in range(NT)]
                        attention_stage("c", maps, tiles, lambda j: bass.ds(pair * P + (8 * HD + j * HD), HD),
                                        mix, combine=lam[:, 0:1])

                with nc.Fori(0, 2) as pair, ExitStack() as ch:
                    if True:
                        qh = sb(ch, "d_q_h", [P, 2, SEQ], F32R)
                        ql = sb(ch, "d_q_l", [P, 2, SEQ], F32R)
                        ks = sb(ch, "d_k_s", [P, 2, SEQ], F32R)
                        v_s = sb(ch, "d_v_s", [P, NT, 2, P], F32R)
                        edge = sb(ch, "bias_edge", [P, 2, REL_R + 1, GRID_W])
                        inner = sb(ch, "bias_inner", [P, 2, 10, GRID_W])
                        cmask = sb(ch, "cmask", [P, GRID_W])
                        rmask = sb(ch, "rmask", [P, 10])

                        def load_bias(sp):
                            sp.dma_start(cmask[:, :], a["col_mask"]).then_inc(S["const_landed"], 16)
                            sp.dma_start(rmask[:, :], a["row_mask"]).then_inc(S["const_landed"], 16)
                            sp.wait_ge(skew_landed, 16 * DEPTH)
                            sp.wait_ge(S["dve_step"], 1)
                            for r in range(2):
                                for h in range(2):
                                    row = layer * (NHEAD * REL_R) + pair * (2 * REL_R) + h * REL_R
                                    src = bass.AP(skew.tensor, row * (GRID_W * SKEW) + (GRID_W - 1),
                                                  [[SKEW - 1, GRID_W], [GRID_W * SKEW, REL_R], [1, GRID_W]])
                                    sp.dma_start(edge[r * GRID_W:(r + 1) * GRID_W, h, r:r + REL_R, :], src) \
                                        .then_inc(S["copy_landed"], 16)

                        def clear_bias(dve):
                            nc.vector.memset(edge[:, :, :, :], NEG).then_inc(S["dve_step"], 1)

                        def mask_bias(dve):
                            dve.wait_ge(S["const_landed"], 32)
                            dve.wait_ge(S["copy_landed"], 16 * 4)
                            e = edge[:, :, :, :].rearrange("p h r k -> p (h r) k")
                            nc.vector.scalar_tensor_tensor(out=e, in0=e, scalar=-1.0, in1=cmask[:, :].unsqueeze(1)
                                                           .to_broadcast([P, 2 * (REL_R + 1), GRID_W]),
                                                           op0=ALU.mult, op1=ALU.add).then_inc(S["dve_step"], 1)
                            dve.wait_ge(S["dve_step"], 2)
                            for h in range(2):
                                nc.vector.tensor_tensor(inner[:, h], edge[:, h, 3:13, :],
                                                        rmask[:, :].unsqueeze(2).to_broadcast([P, 10, GRID_W]), ALU.add)

                        def stack(hi, lo, is_k):
                            out_ = []
                            for h in range(2):
                                s = slice(h * HD, (h + 1) * HD)
                                for r in range(2):
                                    d = slice(r * HD, (r + 1) * HD)
                                    if is_k:
                                        out_.append((ks[d, h, :], (lo if r else hi)[s, :]))
                                    else:
                                        out_ += [(qh[d, h, :], hi[s, :]), (ql[d, h, :], lo[s, :])]
                            return out_

                        pair_stage("d", D0, pair, -HD ** -0.5, stack, v_s, load_bias, lambda act: None,
                                   (clear_bias, mask_bias))

                        maps = [([lambda i, h=h: qh[:, h, i * P:(i + 1) * P], lambda i, h=h: ql[:, h, i * P:(i + 1) * P]],
                                 [lambda x0, x1, h=h: ks[:, h, x0:x1]] * 2, v_s[:, :, h, :]) for h in range(2)]

                        def bias(i):
                            r = {0: 7, 1: 5, 6: 3, 7: 1}.get(i)
                            if r is None:
                                return lambda m: inner[:, m].rearrange("p r k -> p (r k)")
                            return lambda m: edge[:, m, r:r + NA_R, :].rearrange("p r k -> p (r k)")

                        tiles = [((0 if i < 2 else 4 if i > 5 else i - 2), (5 if 2 <= i <= 5 else 4), bias(i))
                                 for i in range(NT)]
                        attention_stage("d", maps, tiles, lambda m: bass.ds(pair * P + (12 * HD + m * HD), HD), mix)

                with ExitStack() as c, nc.Block() as block:
                    sq = sb(c, "m_sq", [P, 2, D])
                    ss = sb(c, "m_ss", [P, NT, 4, 4])
                    sg = sb(c, "m_sg", [P, NT, 4])
                    hn = sb(c, "m_hn", [P, 2, D])
                    g = sb(c, "m_g", [P, D])
                    li = sb(c, "m_li", [P, 2])
                    hg = sb(c, "m_hg", [P, 2, D])
                    h_ps = ps(c, "m_ps", [P, 2, D])
                    GW = 4 * HD

                    @block.sync
                    def _(sp):
                        for j, name in ((0, "g_out_a"), (1, "g_out_b"), (3, "g_out_d")):
                            sp.dma_start(g[:, j * GW:(j + 1) * GW], row_vector(vec(name))).then_inc(S["gain_landed"], 16)
                        for h in range(4):
                            sp.dma_start(g[:, 2 * GW + h * HD:2 * GW + (h + 1) * HD], row_vector(vec("g_out_c"))) \
                                .then_inc(S["gain_landed"], 16)
                        sp.dma_start(li[:, :], row_vector(vec("lambda_init"))).then_inc(S["gain_landed"], 16)

                    @block.scalar
                    def _(act):
                        for t in range(NT):
                            if t >= 2:
                                act.wait_ge(S["mix_sq"], t - 1)
                            nc.scalar.activation(sq[:, t % 2, :], mix[:, t, :], ACT.Square).then_inc(S["square_done"], 1)
                        act.wait_ge(S["dve_step"], 4)
                        root(act, ss[:, :, :, :].rearrange("p t m h -> p (t m h)"), HD).then_inc(S["root_done"], 1)
                        for t in range(NT):
                            act.wait_ge(S["tr_done"], t + 1)
                            nc.scalar.activation(h_hi[:, :, t * P:(t + 1) * P],
                                                 h_ps[:, t % 2, :].rearrange("p (k n) -> p k n", k=KT),
                                                 ACT.Copy).then_inc(S["hi_done"], 1)

                    @block.vector
                    def _(dve):
                        step = [0]

                        def after(ins):
                            step[0] += 1
                            ins.then_inc(S["dve_step"], 1)
                            dve.wait_ge(S["dve_step"], step[0])

                        for t in range(NT):
                            dve.wait_ge(S["square_done"], t + 1)
                            nc.vector.tensor_reduce(ss[:, t].rearrange("p m h -> p (m h)"),
                                                    sq[:, t % 2, :].rearrange("p (h d) -> p h d", d=HD),
                                                    AX_X, ALU.add).then_inc(S["mix_sq"], 1)
                        dve.wait_ge(S["mix_sq"], NT)
                        after(nc.vector.tensor_reduce(sg[:, :, :].rearrange("p t m -> p (t m)"),
                                                      ss[:, :, :, :].rearrange("p t m h -> p (t m) h"), AX_X, ALU.add))
                        for m in (0, 1, 3):
                            after(nc.vector.tensor_scalar(ss[:, :, m, :], sg[:, :, m].unsqueeze(2)
                                                          .to_broadcast([P, NT, 4]), 0.25, None, ALU.mult))
                        dve.wait_ge(S["root_done"], 1)
                        after(nc.vector.reciprocal(ss[:, :, :, :], ss[:, :, :, :]))
                        dve.wait_ge(S["gain_landed"], 16 * 8)
                        after(nc.vector.tensor_scalar(g[:, 2 * GW:3 * GW], g[:, 2 * GW:3 * GW], li[:, 1:2], None, ALU.mult))
                        for t in range(NT + 2):
                            if t < NT:
                                if t >= 2:
                                    dve.wait_ge(S["gain_done"], t - 1)
                                nc.vector.tensor_tensor(
                                    hn[:, t % 2, :].rearrange("p (h d) -> p h d", d=HD),
                                    mix[:, t, :].rearrange("p (h d) -> p h d", d=HD),
                                    ss[:, t].rearrange("p m h -> p (m h)").unsqueeze(2).to_broadcast([P, 16, HD]),
                                    ALU.mult).then_inc(S["norm_done"], 1)
                            if t >= 2:
                                s = t - 2
                                dve.wait_ge(S["hi_done"], s + 1)
                                nc.vector.tensor_tensor(h_lo[:, :, s * P:(s + 1) * P],
                                                        h_ps[:, s % 2, :].rearrange("p (k n) -> p k n", k=KT),
                                                        h_hi[:, :, s * P:(s + 1) * P], ALU.subtract) \
                                    .then_inc(S["lo_done"], 1)

                    @block.gpsimd
                    def _(pool):
                        pool.wait_ge(S["dve_step"], 6)
                        for t in range(NT):
                            pool.wait_ge(S["norm_done"], t + 1)
                            if t >= 2:
                                pool.wait_ge(S["tr_done"], t - 1)
                            nc.gpsimd.tensor_tensor(hg[:, t % 2, :], hn[:, t % 2, :], g[:, :], ALU.mult) \
                                .then_inc(S["gain_done"], 1)

                    @block.tensor
                    def _(pe):
                        for t in range(NT):
                            pe.wait_ge(S["gain_done"], t + 1)
                            if t >= 2:
                                pe.wait_ge(S["lo_done"], t - 1)
                            transposes(pe, h_ps[:, t % 2, :], lambda k: hg[:, t % 2, k * P:(k + 1) * P]) \
                                .then_inc(S["tr_done"], 1)
                end_stage()

            with ExitStack() as co:
                ft = sb(co, "mix_out_t", [P, KT, SEQ])
                with ExitStack() as c, nc.Block() as block:
                    ring = weight_ring(c, "o")
                    u_ps = ps(c, "o_ps", [P, 2, SEQ])
                    w = a["w_out"][layer]
                    units = [full_unit(w[:, m * P:(m + 1) * P]) for m in range(KT)]

                    @block.sync
                    def _(sp):
                        load_weights(sp, ring, units)

                    @block.gpsimd
                    def _(pool):
                        for u in range(KT):
                            split_lo(pool, ring, units, u)

                    @block.scalar
                    def _(act):
                        for u in range(KT):
                            split_hi(act, ring, units, u)

                    @block.tensor
                    def _(pe):
                        for u in range(KT):
                            if u >= 2:
                                pe.wait_ge(S["gemm_out"], u - 1)
                            products(pe, u_ps[:, u % 2, :], ring, units, u, h_hi, h_lo)

                    @block.vector
                    def _(dve):
                        for u in range(KT):
                            dve.wait_ge(S["gemm_done"], u + 1)
                            nc.vector.tensor_copy(ft[:, u, :], u_ps[:, u % 2, :]).then_inc(S["gemm_out"], 1)
                end_stage()
                norm_stage("mlp_pre", ft, vec("norm_mix_post"), vec("norm_mlp_pre"))

            with ExitStack() as co:
                ft = sb(co, "mlp_out_t", [P, KT, SEQ])
                with ExitStack() as c, nc.Block() as block:
                    ring = weight_ring(c, "m")
                    up_h = sb(c, "up_h", [P, KT, SEQ], F32R)
                    up_l = sb(c, "up_l", [P, KT, SEQ], F32R)
                    r_sb = sb(c, "m_relu", [P, SEQ])
                    s_sb = sb(c, "m_square", [P, SEQ])
                    u_ps = ps(c, "u_ps", [P, 2, SEQ])
                    NU = 2 * KT
                    CHUNKS = FF // FF_CHUNK

                    def chunk_units(chunk):
                        wu = a["w_up"][layer]
                        wd = a["w_down"][layer][bass.ds(chunk * FF_CHUNK, FF_CHUNK), :]
                        return [full_unit(wu[:, bass.ds(chunk * FF_CHUNK + j * P, P)]) for j in range(KT)] + \
                               [full_unit(wd[:, m * P:(m + 1) * P]) for m in range(KT)]

                    shapes = chunk_units(0)

                    @block.sync
                    def _(sp):
                        with sp.Fori(0, CHUNKS) as chunk:
                            load_weights(sp, ring, chunk_units(chunk), chunk)

                    @block.gpsimd
                    def _(pool):
                        pool.sem_inc(S["w_lo"], 2)
                        with pool.Fori(0, CHUNKS) as chunk:
                            for u in range(NU):
                                split_lo(pool, ring, shapes, u, chunk)

                    @block.tensor
                    def _(pe):
                        pe.sem_inc(S["gemm_done"], 2)
                        with pe.Fori(0, CHUNKS) as chunk:
                            for u in range(NU):
                                if 2 <= u < KT + 2:
                                    pe.wait_ge(S["relu_done"], chunk * KT + (u - 1))
                                else:
                                    pe.wait_ge(S["acc_done"], chunk * KT + (u + 1 if u < 2 else u + 1 - KT))
                                if u < KT:
                                    products(pe, u_ps[:, u % 2, :], ring, shapes, u, h_hi, h_lo, chunk)
                                else:
                                    if u == KT:
                                        pe.wait_ge(S["up_lo"], chunk * KT + (KT - 1))
                                    products(pe, u_ps[:, u % 2, :], ring, shapes, u, up_h, up_l, chunk,
                                             {KT - 1: lambda: pe.wait_ge(S["up_lo"], chunk * KT + KT)})

                    @block.scalar
                    def _(act):
                        with act.Fori(0, CHUNKS) as chunk:
                            def hi(u):
                                split_hi(act, ring, shapes, u, chunk)

                            hi(0)
                            for u in range(NU):
                                if u + 1 < NU:
                                    hi(u + 1)
                                if u < KT:
                                    act.wait_ge(S["gemm_done"], chunk * NU + (u + 3))
                                    nc.scalar.activation(r_sb[:, :], u_ps[:, u % 2, :], ACT.Relu) \
                                        .then_inc(S["relu_done"], 1)
                                    act.wait_ge(S["sq_done"], chunk * KT + (u + 1))
                                    nc.scalar.activation(up_h[:, u, :], s_sb[:, :], ACT.Copy).then_inc(S["up_hi"], 1)

                    @block.vector
                    def _(dve):
                        dve.sem_inc(S["acc_done"], 2)
                        nc.vector.memset(ft[:, :, :], 0.0).then_inc(S["zero_done"], 1)
                        dve.wait_ge(S["zero_done"], 1)
                        with dve.Fori(0, CHUNKS) as chunk:
                            for u in range(NU):
                                if u < KT:
                                    dve.wait_ge(S["relu_done"], chunk * KT + (u + 1))
                                    nc.vector.tensor_tensor(s_sb[:, :], r_sb[:, :], r_sb[:, :], ALU.mult) \
                                        .then_inc(S["sq_done"], 1)
                                    dve.wait_ge(S["up_hi"], chunk * KT + (u + 1))
                                    nc.vector.tensor_tensor(up_l[:, u, :], s_sb[:, :], up_h[:, u, :], ALU.subtract) \
                                        .then_inc(S["up_lo"], 1)
                                    dve.wait_ge(S["up_lo"], chunk * KT + (u + 1))
                                else:
                                    m = u - KT
                                    dve.wait_ge(S["gemm_done"], chunk * NU + (u + 3))
                                    dve.wait_ge(S["acc_done"], chunk * KT + (m + 2))
                                    nc.vector.tensor_tensor(ft[:, m, :], ft[:, m, :], u_ps[:, u % 2, :], ALU.add) \
                                        .then_inc(S["acc_done"], 1)
                end_stage()
                norm_stage("mlp_post", ft, vec("norm_mlp_post"), None)


_INS = ["x", "norm_mix_pre", "norm_mix_post", "norm_mlp_pre", "norm_mlp_post", "w_in", "a_q_norm", "a_k_norm",
        "b_cq_norm", "b_ckv_norm", "b_w_uq", "b_w_ukv", "c_lambda_q1", "c_lambda_k1", "c_lambda_q2",
        "c_lambda_k2", "d_rel_bias", "g_out_a", "g_out_b", "g_out_c", "g_out_d", "w_out", "w_up", "w_down"]


def kernel(**inputs):
    import concourse.bacc as _bacc
    from concourse.bass_utils import run_bass_kernel_spmd as _run

    nc = _bacc.Bacc("TRN2", target_bir_lowering=False, num_devices=1)
    arrays = {}
    for name in _INS:
        v = np.ascontiguousarray(inputs[name])
        if name == "x":
            v = v.reshape(SEQ, D)
        if name == "d_rel_bias":
            v = v.reshape(DEPTH, REL_N)
        arrays[name] = v
    arrays.update(shape_constants())
    aps = {n: nc.dram_tensor(f"in_{n}", v.shape, F32, kind="ExternalInput").ap() for n, v in arrays.items()}
    out = nc.dram_tensor("out_x", (SEQ, D), F32, kind="ExternalOutput").ap()
    build(nc, aps, out)
    r = _run(nc, [{f"in_{n}": v for n, v in arrays.items()}], core_ids=[0])
    return r.results[0]["out_x"].reshape(1, SEQ, D)
```

```python
from contextlib import ExitStack
import math

import numpy as np
import concourse.bass as bass
from concourse import mybir

ALU = mybir.AluOpType
ACT = mybir.ActivationFunctionType
AX_X = mybir.AxisListType.X
F32 = mybir.dt.float32
F32R = mybir.dt.float32r

P = 128
SEQ, D, DEPTH = 1024, 1024, 2
NT = SEQ // P
KT = D // P
HALF = 512
HD = 64
GRID_W = 64
NHEAD = 4
B_Q, B_KV, B_ROPE = 3 * HD, 2 * HD, HD // 2
A0 = 0
B0 = A0 + 8 * HD
C0 = B0 + B_Q + B_KV + B_ROPE
D0 = C0 + 12 * HD
FF = 4 * D
FF_CHUNK = 1024
NA_R, NA_C = 8, 16
REL_C = 2 * NA_C - 1
REL_R = 2 * NA_R - 1
REL_N = NHEAD * REL_R * REL_C
EPS = 1e-6
NEG = -1e30
MIN_START = 3.0e38
REL_PAD = 64
REL_ROW = REL_N + 2 * REL_PAD
SKEW = 2 * GRID_W - 1


def shape_constants():
    t = np.arange(SEQ)

    def angles(pos, dim):
        inv = np.float32(10000.0) ** (-np.arange(0, dim, 2, dtype=np.float32) / np.float32(dim))
        return pos.astype(np.float32)[:, None] * inv[None, :].astype(np.float32)

    def both(ang):
        c, s = np.cos(ang), np.sin(ang)
        return np.concatenate([c, c], 1), np.concatenate([-s, s], 1)

    cr, sr = both(angles(t // GRID_W, HD // 2))
    cc, sc = both(angles(t % GRID_W, HD // 2))
    cb, sb = both(angles(t, B_ROPE))
    col = np.arange(GRID_W)
    first = np.clip(col - NA_C // 2, 0, GRID_W - NA_C)
    seen = (col[None, :] >= first[:, None]) & (col[None, :] < first[:, None] + NA_C)
    col_mask = np.where(seen, 0.0, -NEG)
    row_mask = np.zeros((2, 10))
    row_mask[0, 8:] = -NEG
    row_mask[1, 0] = -NEG
    row_mask[1, 9] = -NEG
    p, m = np.arange(P)[:, None], np.arange(2 * SEQ - P)[None, :]
    li = [0.8 - 0.6 * math.exp(-0.3 * l) for l in range(DEPTH)]
    tables = {
        "cos_a": np.concatenate([cr, cc], 1), "sin_a": np.concatenate([sr, sc], 1),
        "cos_sin_b": np.concatenate([cb.T, sb.T], 0),
        "col_mask": np.concatenate([col_mask, col_mask], 0),
        "row_mask": np.repeat(row_mask, GRID_W, 0),
        "distance": np.abs(p + (SEQ - P) - m),
        "slopes": np.array([[2.0 ** (-8.0 * (h + 1) / NHEAD) for h in range(NHEAD)]]),
        "lambda_init": np.array([[v, 1.0 - v] for v in li]),
    }
    return {k: np.ascontiguousarray(v, dtype=np.float32) for k, v in tables.items()}


SEMS = """w_landed_head w_landed0 w_landed1 w_hi w_lo gemm_done gemm_out tt_done tt_hi tt_lo x_landed0
 x_landed1 x_landed2 x_landed3 x_landed4 x_landed5 x_landed6 x_landed7 gain_landed x_stored
 square_done norm_done gain_done hi_done lo_done tr_done ytr_done ysq_done ynorm_done xadd_done
 zero_done dve_step pool_step pe_step const_landed scores_done max_done exp_done ptr_done pt_hi pt_lo
 pv_done ot_done o_done map_done stack_landed root_done yroot_done relu_done sq_done up_hi up_lo
 acc_done q_hi k_hi k_lo rope_done swap_done copy_landed prep_done mix_sq""".split()


class Sems:

    def __init__(self, ctx, nc):
        handles = [ctx.enter_context(nc.semaphore(n)) for n in SEMS]
        self.by_name = dict(zip(SEMS, handles))
        nums = [h.num for h in handles]
        self.range = range(min(nums), max(nums) + 1)

    def __getitem__(self, name):
        return self.by_name[name]


def build(nc, a, out):
    with ExitStack() as ctx:
        S = Sems(ctx, nc)
        x_copied = ctx.enter_context(nc.semaphore("x_copied"))
        skew_landed = ctx.enter_context(nc.semaphore("skew_landed"))

        def sb(c, name, shape, dt=F32):
            return c.enter_context(nc.sbuf_tensor(name, shape, dt))

        def ps(c, name, shape, dt=F32):
            return c.enter_context(nc.psum_tensor(name, shape, dt))

        def end_stage():
            nc.all_engine_barrier(sems_to_clear=S.range)

        ident = sb(ctx, "ident", [P, P])
        fold = sb(ctx, "fold", [P, HD])
        ones = sb(ctx, "ones", [P, P])
        h_hi = sb(ctx, "h_hi", [P, KT, SEQ], F32R)
        h_lo = sb(ctx, "h_lo", [P, KT, SEQ], F32R)
        eps_col = sb(ctx, "eps_col", [P, 1])
        rel_scratch = nc.dram_tensor("rel_scratch", (DEPTH, REL_ROW), F32).ap()
        skew = nc.dram_tensor("skew", (DEPTH, NHEAD * REL_R, GRID_W, SKEW), F32).ap()

        with ExitStack() as c, nc.Block() as block:
            zero = sb(c, "zero", [DEPTH, REL_PAD])

            @block.scalar
            def _(act):
                act.wait_ge(S["const_landed"], 1)
                for at in (0, REL_PAD + REL_N):
                    act.dma_start(rel_scratch[:, at:at + REL_PAD], zero[:, :]).then_inc(S["copy_landed"], 16)
                act.dma_start(rel_scratch[:, REL_PAD:REL_PAD + REL_N], a["d_rel_bias"]).then_inc(S["copy_landed"], 16)
                act.wait_ge(S["copy_landed"], 48)

            @block.vector
            def _(dve):
                nc.vector.memset(zero[:, :], 0.0).then_inc(S["const_landed"], 1)
                nc.vector.memset(ones[:, :], 1.0)
                nc.vector.memset(eps_col[:, :], EPS)

            @block.gpsimd
            def _(pool):
                nc.gpsimd.memset(ident[:, :], 0.0).then_inc(S["pool_step"], 1)
                nc.gpsimd.memset(fold[:, :], 0.0).then_inc(S["pool_step"], 1)
                pool.wait_ge(S["pool_step"], 2)
                nc.gpsimd.affine_select(out=ident[:, :], in_=ident[:, :], compare_op=ALU.not_equal, fill=1.0,
                                        base=0, pattern=[[-1, P]], channel_multiplier=1)
                nc.gpsimd.affine_select(out=fold[:, :], in_=fold[:, :], compare_op=ALU.not_equal, fill=1.0,
                                        base=0, pattern=[[-1, HD]], channel_multiplier=1).then_inc(S["pool_step"], 1)
                pool.wait_ge(S["pool_step"], 3)
                nc.gpsimd.affine_select(out=fold[:, :], in_=fold[:, :], compare_op=ALU.not_equal, fill=1.0,
                                        base=-HD, pattern=[[-1, HD]], channel_multiplier=1)
        end_stage()

        def weight_ring(c, tag):
            return (sb(c, f"w_raw_{tag}", [P, 2, KT, P]), sb(c, f"w_h_{tag}", [P, 2, KT, P], F32R),
                    sb(c, f"w_l_{tag}", [P, 2, KT, P], F32R))

        HEAD = 2

        def parts(units, u):
            shape = units[u][1]
            if u == 0 and shape == FULL:
                return [[(P, slice(0, HEAD))], [(P, slice(HEAD, KT))]]
            return [shape]

        def parts_done(units, n, rnd=None):
            count = sum(len(parts(units, u)) for u in range(n))
            return count if rnd is None else rnd * sum(len(parts(units, u)) for u in range(len(units))) + count

        def load_weights(sp, ring, units, rnd=None):
            raw = ring[0]
            for u, (pieces, _) in enumerate(units):
                if rnd is not None:
                    sp.wait_ge(S["w_lo"], parts_done(units, u - 1, rnd) + 2 if u >= 1
                               else rnd * parts_done(units, len(units)) + 1)
                elif u >= 2:
                    sp.wait_ge(S["w_lo"], parts_done(units, u - 1))
                for dst, src in pieces:
                    d = dst(raw[:, u % 2])
                    if len(parts(units, u)) > 1:
                        sp.dma_start(d[:, 0:HEAD], src[:, 0:HEAD]).then_inc(S["w_landed_head"], 16)
                        d, src = d[:, HEAD:], src[:, HEAD:]
                    sp.dma_start(d, src).then_inc(S[f"w_landed{u % 2}"], 16)

        def landed(units, u, rnd=None):
            count = 16 * sum(len(units[v][0]) for v in range(u % 2, u + 1, 2))
            return count if rnd is None else rnd * (16 * sum(len(units[v][0]) for v in range(u % 2, len(units), 2))) + count

        def split_hi(act, ring, units, u, rnd=None):
            raw, hi, _ = ring
            if rnd is not None:
                act.wait_ge(S["gemm_done"], rnd * len(units) + (u + 1))
            elif u >= 2:
                act.wait_ge(S["gemm_done"], u - 1)
            part_list = parts(units, u)
            for j, part in enumerate(part_list):
                if j < len(part_list) - 1:
                    act.wait_ge(S["w_landed_head"], 16 if rnd is None else rnd * 16 + 16)
                else:
                    act.wait_ge(S[f"w_landed{u % 2}"], landed(units, u, rnd))
                for rows, cols in part:
                    last = nc.scalar.activation(hi[0:rows, u % 2, cols, :], raw[0:rows, u % 2, cols, :], ACT.Copy)
                last.then_inc(S["w_hi"], 1)

        def split_lo(pool, ring, units, u, rnd=None):
            raw, hi, lo = ring
            for j, part in enumerate(parts(units, u)):
                pool.wait_ge(S["w_hi"], parts_done(units, u, rnd) + (j + 1))
                for rows, cols in part:
                    last = nc.gpsimd.tensor_tensor(lo[0:rows, u % 2, cols, :], raw[0:rows, u % 2, cols, :],
                                                   hi[0:rows, u % 2, cols, :], ALU.subtract)
                last.then_inc(S["w_lo"], 1)

        def part_products(dst, w_hi, w_lo, x_hi, x_lo, first, last):
            for n in range(2):
                o, tok = dst[:, n * HALF:(n + 1) * HALF], slice(n * HALF, (n + 1) * HALF)
                nc.tensor.matmul(o, w_hi, x_hi[:, tok], start=first, stop=False)
                nc.tensor.matmul(o, w_hi, x_lo[:, tok], start=False, stop=False)
            for n in range(2):
                o, tok = dst[:, n * HALF:(n + 1) * HALF], slice(n * HALF, (n + 1) * HALF)
                ins = nc.tensor.matmul(o, w_lo, x_hi[:, tok], start=False, stop=last)
            return ins

        def products(pe, dst, ring, units, u, x_hi, x_lo, rnd=None, before={}):
            _, hi, lo = ring
            rows_of = [rows for rows, cols in units[u][1] for _ in range(cols.start, cols.stop)]
            starts = [part[0][1].start for part in parts(units, u)]
            for k, rows in enumerate(rows_of):
                if k in starts:
                    pe.wait_ge(S["w_lo"], parts_done(units, u, rnd) + (starts.index(k) + 1 + (0 if rnd is None else 2)))
                if k in before:
                    before[k]()
                last = part_products(dst, hi[0:rows, u % 2, k, :], lo[0:rows, u % 2, k, :], x_hi[0:rows, k, :],
                                     x_lo[0:rows, k, :], k == 0, k == len(rows_of) - 1)
            last.then_inc(S["gemm_done"], 1)

        def half_products(pe, dst, ring, units, u, x_hi, x_lo, n, before={}):
            _, hi, lo = ring
            pe.wait_ge(S["w_lo"], parts_done(units, u + 1))
            o, tok = dst[:, n * HALF:(n + 1) * HALF], slice(n * HALF, (n + 1) * HALF)
            for k in range(KT):
                if k in before:
                    before[k]()
                nc.tensor.matmul(o, hi[:, u % 2, k, :], x_hi[:, k, tok], start=(k == 0), stop=False)
                nc.tensor.matmul(o, hi[:, u % 2, k, :], x_lo[:, k, tok], start=False, stop=False)
                last = nc.tensor.matmul(o, lo[:, u % 2, k, :], x_hi[:, k, tok], start=False, stop=(k == KT - 1))
            last.then_inc(S["gemm_done"], 1)

        FULL = [(P, slice(0, KT))]

        def full_unit(src):
            return ([(lambda w: w, src.rearrange("(k p) n -> p k n", p=P))], FULL)

        def transposes(pe, dst, src_of, n=8):
            for i in range(n):
                last = nc.tensor.transpose(dst[:, i * P:(i + 1) * P], src_of(i), ident[:, :])
            return last

        def row_vector(src):
            return src.partition_broadcast(P)

        def root(act, ss, width):
            return nc.scalar.activation(ss, ss, ACT.Sqrt, scale=1.0 / width, bias=eps_col[:, 0:1])

        def rstd(dve, ss, step):
            nc.vector.reciprocal(ss, ss).then_inc(S["dve_step"], 1)
            dve.wait_ge(S["dve_step"], step + 1)
            return step + 1

        def norm_stage(tag, ft, post_gain, pre_gain, x_dram=out, after_loads=None):
            post, pre = ft is not None, pre_gain is not None
            lag = 2 if post else 0
            with ExitStack() as c, nc.Block() as block:
                x = sb(c, f"x_{tag}", [P, NT, D])
                junk = sb(c, f"junk_{tag}", [P, D])
                stat = sb(c, f"stat_{tag}", [P, 2, NT])
                if post:
                    g_post = sb(c, f"g_post_{tag}", [P, D])
                    y = sb(c, f"y_{tag}", [P, 2, D])
                    y_ps = ps(c, f"y_ps_{tag}", [P, 2, D])
                if pre:
                    g_pre = sb(c, f"g_pre_{tag}", [P, D])
                    hn = sb(c, f"hn_{tag}", [P, 2, D])
                    h_ps = ps(c, f"h_ps_{tag}", [P, 2, D])
                gains = 16 * (post + pre)
                rounds = NT + (lag + 1 if pre else 0)

                @block.sync
                def _(sp):
                    if post:
                        sp.wait_ge(x_copied, 16)
                    for t in range(NT):
                        sp.dma_start(x[:, t, :], x_dram[t * P:(t + 1) * P, :]).then_inc(S[f"x_landed{t}"], 16)
                        if t == 0:
                            if post:
                                sp.dma_start(g_post[:, :], row_vector(post_gain)).then_inc(S["gain_landed"], 16)
                            if pre:
                                sp.dma_start(g_pre[:, :], row_vector(pre_gain)).then_inc(S["gain_landed"], 16)
                    if after_loads:
                        after_loads(sp)
                    if post:
                        for t in range(NT):
                            sp.wait_ge(S["xadd_done"], t + 1)
                            sp.dma_start(out[t * P:(t + 1) * P, :], x[:, t, :]).then_inc(S["x_stored"], 16)
                        sp.wait_ge(S["x_stored"], 16 * NT)

                @block.gpsimd
                def _(pool):
                    if post:
                        for t in range(NT):
                            pool.wait_ge(S[f"x_landed{t}"], 16)
                            pool.wait_ge(S["ynorm_done"], t + 1)
                            nc.gpsimd.tensor_tensor(x[:, t, :], x[:, t, :], y[:, t % 2, :],
                                                    ALU.add).then_inc(S["xadd_done"], 1)

                @block.tensor
                def _(pe):
                    for t in range(rounds):
                        if post and t < NT:
                            if t >= 2:
                                pe.wait_ge(S["ynorm_done"], t - 1)
                            transposes(pe, y_ps[:, t % 2, :], lambda m, t=t: ft[:, m, t * P:(t + 1) * P]) \
                                .then_inc(S["ytr_done"], 1)
                        s = t - lag - 1
                        if pre and s >= 0:
                            pe.wait_ge(S["norm_done"], s + 1)
                            if s >= 2:
                                pe.wait_ge(S["lo_done"], s - 1)
                            transposes(pe, h_ps[:, s % 2, :], lambda k, s=s: hn[:, s % 2, k * P:(k + 1) * P]) \
                                .then_inc(S["tr_done"], 1)

                @block.scalar
                def _(act):
                    for t in range(rounds):
                        if post and t < NT:
                            act.wait_ge(S["ytr_done"], t + 1)
                            nc.scalar.activation(junk[:, :], y_ps[:, t % 2, :], ACT.Square,
                                                 accum_out=stat[:, 0, t:t + 1]).then_inc(S["ysq_done"], 1)
                            act.wait_ge(S["ysq_done"], t + 1)
                            root(act, stat[:, 0, t:t + 1], D).then_inc(S["yroot_done"], 1)
                        s = t - lag
                        if pre and 0 <= s < NT:
                            act.wait_ge(*((S["xadd_done"], s + 1) if post else (S[f"x_landed{s}"], 16)))
                            nc.scalar.activation(junk[:, :], x[:, s, :], ACT.Square,
                                                 accum_out=stat[:, 1, s:s + 1]).then_inc(S["square_done"], 1)
                            act.wait_ge(S["square_done"], s + 1)
                            root(act, stat[:, 1, s:s + 1], D).then_inc(S["root_done"], 1)
                        s -= 1
                        if pre and s >= 0:
                            act.wait_ge(S["tr_done"], s + 1)
                            nc.scalar.activation(h_hi[:, :, s * P:(s + 1) * P],
                                                 h_ps[:, s % 2, :].rearrange("p (k n) -> p k n", k=KT),
                                                 ACT.Copy).then_inc(S["hi_done"], 1)

                @block.vector
                def _(dve):
                    step = 0
                    dve.wait_ge(S["gain_landed"], gains)
                    for t in range(rounds):
                        if post and t < NT:
                            dve.wait_ge(S["yroot_done"], t + 1)
                            step = rstd(dve, stat[:, 0, t:t + 1], step)
                            if t >= 2:
                                dve.wait_ge(S["xadd_done"], t - 1)
                            nc.vector.scalar_tensor_tensor(out=y[:, t % 2, :], in0=y_ps[:, t % 2, :],
                                                           scalar=stat[:, 0, t:t + 1], in1=g_post[:, :],
                                                           op0=ALU.mult, op1=ALU.mult).then_inc(S["ynorm_done"], 1)
                        s = t - lag
                        if pre and 0 <= s < NT:
                            dve.wait_ge(S["root_done"], s + 1)
                            step = rstd(dve, stat[:, 1, s:s + 1], step)
                            if s >= 2:
                                dve.wait_ge(S["tr_done"], s - 1)
                            nc.vector.scalar_tensor_tensor(out=hn[:, s % 2, :], in0=x[:, s, :],
                                                           scalar=stat[:, 1, s:s + 1], in1=g_pre[:, :],
                                                           op0=ALU.mult, op1=ALU.mult).then_inc(S["norm_done"], 1)
                        s -= 1
                        if pre and s >= 0:
                            dve.wait_ge(S["hi_done"], s + 1)
                            nc.vector.tensor_tensor(h_lo[:, :, s * P:(s + 1) * P],
                                                    h_ps[:, s % 2, :].rearrange("p (k n) -> p k n", k=KT),
                                                    h_hi[:, :, s * P:(s + 1) * P], ALU.subtract) \
                                .then_inc(S["lo_done"], 1)
            end_stage()

        def attention_stage(tag, maps, tiles, mix_cols, mix, combine=None):
            n_all = len(maps) * NT
            n_groups = n_all // 2
            kmax = max(t[1] for t in tiles)
            base_of = [min(tiles[i][0], tiles[i + 1][0]) for i in range(0, NT, 2)]
            value_steps = []
            for i in range(0, NT, 2):
                (f0, c0), (f1, c1) = tiles[i][0:2], tiles[i + 1][0:2]
                both = range(max(f0, f1), min(f0 + c0, f1 + c1))
                value_steps.append([(k, slice(0, 2 * P)) for k in both]
                                   + [(k, slice(0, P)) for k in range(f0, f0 + c0) if k not in both]
                                   + [(k, slice(P, 2 * P)) for k in range(f1, f1 + c1) if k not in both])
            kslots = max(k - b + 1 for b, steps in zip(base_of, value_steps) for k, _ in steps)
            with ExitStack() as c, nc.Block() as block:
                prob = sb(c, f"prob_{tag}", [P, 2, kmax * P])
                pt_h = sb(c, f"pt_h_{tag}", [P, 2, kslots, 2 * P], F32R)
                pt_l = sb(c, f"pt_l_{tag}", [P, 2, kslots, 2 * P], F32R)
                ot = sb(c, f"ot_{tag}", [P, 2, 2 * P])
                nmax = sb(c, f"nmax_{tag}", [P, n_all])
                z = sb(c, f"z_{tag}", [P, n_all])
                if combine is not None:
                    part = sb(c, f"part_{tag}", [P, 2, NT, HD])
                s_ps = ps(c, f"s_ps_{tag}", [P, 2, 2 * HALF])
                t_ps = ps(c, f"t_ps_{tag}", [P, 2, HALF])
                ot_ps = ps(c, f"ot_ps_{tag}", [P, HALF])
                o_ps = ps(c, f"o_ps_{tag}", [P, NT, HD])

                def seq(n):
                    return n // NT, n % NT

                piece_end = [0]
                for n in range(n_all):
                    piece_end.append(piece_end[-1] + -(-tiles[n % NT][1] // 4))

                def pieces(n):
                    cnt = tiles[n % NT][1]
                    return [(piece_end[n] + b, 4 * b, min(cnt, 4 * b + 4)) for b in range(-(-cnt // 4))]

                def turned(p, k0, k1):
                    return t_ps[:, p % 2, 0:(k1 - k0) * P].rearrange("p (k n) -> p k n", k=k1 - k0)

                @block.tensor
                def _(pe):
                    def scores(n):
                        m, i = seq(n)
                        first, cnt = tiles[i][0:2]
                        if n >= 2:
                            pe.wait_ge(S["exp_done"], n - 1)
                        q_of, k_of = maps[m][0], maps[m][1]
                        for at in range(0, cnt * P, HALF):
                            w = min(HALF, cnt * P - at)
                            for j, (q, k) in enumerate(zip(q_of, k_of)):
                                last = nc.tensor.matmul(s_ps[:, n % 2, at:at + w], q(i),
                                                        k(first * P + at, first * P + at + w),
                                                        start=(j == 0), stop=(j == len(q_of) - 1))
                        last.then_inc(S["scores_done"], 1)

                    def turn(n):
                        m, i = seq(n)
                        pe.wait_ge(S["exp_done"], n + 1)
                        for p, k0, k1 in pieces(n):
                            if p >= 2:
                                pe.wait_ge(S["pt_lo"], p - 1)
                            transposes(pe, t_ps[:, p % 2, :],
                                       lambda k: prob[:, n % 2, (k0 + k) * P:(k0 + k + 1) * P], k1 - k0) \
                                .then_inc(S["ptr_done"], 1)

                    def values(g, half):
                        m, i = seq(2 * g)
                        if half == 0:
                            pe.wait_ge(S["pt_lo"], piece_end[2 * g + 2])
                            if g >= 1:
                                pe.wait_ge(S["ot_done"], g)
                        v, steps = maps[m][2], value_steps[i // 2]
                        cut = (len(steps) + 1) // 2
                        for at in range(0, cut) if half == 0 else range(cut, len(steps)):
                            k, cols = steps[at]
                            for j, pt in enumerate((pt_h, pt_l)):
                                last = nc.tensor.matmul(ot_ps[:, cols], v[:, k, :],
                                                        pt[:, g % 2, k - base_of[i // 2], cols],
                                                        start=(at == 0 and j == 0),
                                                        stop=(at == len(steps) - 1 and j == 1))
                        if half == 1:
                            last.then_inc(S["pv_done"], 1)

                    def finish(g):
                        m, i = seq(2 * g)
                        pe.wait_ge(S["ot_done"], g + 1)
                        if m >= 1 and i == 0:
                            pe.wait_ge(S["map_done"], m)
                        for j in range(2):
                            last = nc.tensor.matmul(o_ps[:, i + j, :], ot[:, g % 2, j * P:(j + 1) * P],
                                                    fold[:, :], start=True, stop=True)
                        last.then_inc(S["o_done"], 1)

                    scores(0)
                    scores(1)
                    for n in range(n_all + 3):
                        if n + 2 < n_all:
                            scores(n + 2)
                        if n < n_all:
                            turn(n)
                        if 0 <= n // 2 - 1 < n_groups:
                            values(n // 2 - 1, n % 2)
                        if n >= 4 and n % 2 == 0:
                            finish(n // 2 - 2)

                @block.scalar
                def _(act):
                    def split(n):
                        m, i = seq(n)
                        g, j = n // 2, n % 2
                        off = tiles[i][0] - base_of[i // 2]
                        if j == 0 and g >= 2:
                            act.wait_ge(S["pv_done"], g - 1)
                        for p, k0, k1 in pieces(n):
                            act.wait_ge(S["ptr_done"], p + 1)
                            nc.scalar.activation(pt_h[:, g % 2, off + k0:off + k1, j * P:(j + 1) * P],
                                                 turned(p, k0, k1),
                                                 ACT.Copy).then_inc(S["pt_hi"], 1)

                    def lift(g):
                        act.wait_ge(S["pv_done"], g + 1)
                        if g >= 2:
                            act.wait_ge(S["o_done"], g - 1)
                        nc.scalar.activation(ot[:, g % 2, :], ot_ps[:, 0:2 * P], ACT.Copy) \
                            .then_inc(S["ot_done"], 1)

                    def exponential(n):
                        cnt = tiles[n % NT][1]
                        act.wait_ge(S["max_done"], n + 1)
                        if n >= 2:
                            act.wait_ge(S["ptr_done"], piece_end[n - 1])
                        nc.scalar.activation(prob[:, n % 2, 0:cnt * P], s_ps[:, n % 2, 0:cnt * P], ACT.Exp,
                                             scale=1.0 if tiles[n % NT][2] is None else -1.0, bias=nmax[:, n:n + 1], accum_out=z[:, n:n + 1]) \
                            .then_inc(S["exp_done"], 1)

                    exponential(0)
                    for n in range(n_all + 2):
                        if n + 1 < n_all:
                            exponential(n + 1)
                        if n < n_all:
                            split(n)
                        if n >= 3 and n % 2 == 1:
                            lift(n // 2 - 1)

                @block.vector
                def _(dve):
                    step = [0]

                    def after(ins):
                        step[0] += 1
                        ins.then_inc(S["dve_step"], 1)
                        dve.wait_ge(S["dve_step"], step[0])

                    def maximum(n):
                        m, i = seq(n)
                        first, cnt, bias = tiles[i]
                        dve.wait_ge(S["scores_done"], n + 1)
                        s = s_ps[:, n % 2, 0:cnt * P]
                        if bias is None:
                            nc.vector.tensor_reduce(nmax[:, n:n + 1], s, AX_X, ALU.max, negate=True) \
                                .then_inc(S["max_done"], 1)
                        else:
                            nc.vector.tensor_tensor_reduce(out=s, in0=s, in1=bias(m), scale=1.0,
                                                           scalar=MIN_START, op0=ALU.add, op1=ALU.min,
                                                           accum_out=nmax[:, n:n + 1]).then_inc(S["max_done"], 1)

                    def split(n):
                        m, i = seq(n)
                        g, j = n // 2, n % 2
                        off = tiles[i][0] - base_of[i // 2]
                        for p, k0, k1 in pieces(n):
                            dve.wait_ge(S["pt_hi"], p + 1)
                            at = (slice(None), g % 2, slice(off + k0, off + k1), slice(j * P, (j + 1) * P))
                            nc.vector.tensor_tensor(pt_l[at], turned(p, k0, k1), pt_h[at], ALU.subtract) \
                                .then_inc(S["pt_lo"], 1)

                    def divide(m):
                        zm = z[:, m * NT:(m + 1) * NT]
                        after(nc.vector.reciprocal(zm, zm))
                        dve.wait_ge(S["o_done"], (m + 1) * NT // 2)
                        zb = zm.unsqueeze(2).to_broadcast([P, NT, HD])
                        if combine is None:
                            nc.vector.tensor_tensor(mix[:, :, mix_cols(m)], o_ps[:, :, :], zb, ALU.mult) \
                                .then_inc(S["map_done"], 1)
                        else:
                            after(nc.vector.tensor_tensor(part[:, m % 2], o_ps[:, :, :], zb, ALU.mult))
                            if m % 2:
                                nc.vector.scalar_tensor_tensor(out=mix[:, :, mix_cols(m // 2)], in0=part[:, 1],
                                                               scalar=combine, in1=part[:, 0],
                                                               op0=ALU.mult, op1=ALU.add) \
                                    .then_inc(S["map_done"], 1)
                            else:
                                dve.sem_inc(S["map_done"], 1)

                    maximum(0)
                    maximum(1)
                    for n in range(n_all + 4):
                        if n + 2 < n_all:
                            maximum(n + 2)
                        if n < n_all:
                            split(n)
                        if n >= NT + 3 and (n - 3) % NT == 0:
                            divide((n - 3) // NT - 1)
            end_stage()

        def turn_values(pe, t_ps, u_sb, slot):
            return transposes(pe, t_ps[:, slot, :], lambda t: u_sb[:, slot, t * P:(t + 1) * P])

        def background_copy(sp):
            sp.dma_start(out, a["x"]).then_inc(x_copied, 16)

        norm_stage("mix_pre", None, None, a["norm_mix_pre"][0:1, :], a["x"], background_copy)

        with nc.Fori(0, DEPTH) as layer:
            def vec(name, lo=None, hi=None):
                v = a[name][bass.ds(layer, 1), :]
                return v if lo is None else v[:, lo:hi]

            with ExitStack() as cm:
                mix = sb(cm, "mix", [P, NT, D])

                with ExitStack() as ca:
                    q_h = sb(ca, "a_q_h", [P, 4, SEQ], F32R)
                    q_l = sb(ca, "a_q_l", [P, 4, SEQ], F32R)
                    k_s = sb(ca, "a_k_s", [P, 2, SEQ], F32R)
                    v_s = sb(ca, "a_v_s", [P, 2, NT, P], F32R)
                    with ExitStack() as c, nc.Block() as block:
                        ring = weight_ring(c, "a")
                        u_sb = sb(c, "a_u", [P, 2, SEQ])
                        tok = sb(c, "a_tok", [P, NT, 3, HD])
                        sq = sb(c, "a_sq", [P, NT, 3, HD])
                        rot = sq
                        res = sb(c, "a_res", [P, NT, 3, 2, HD])
                        ss = sb(c, "a_ss", [P, 2, NT * 3])
                        gain = sb(c, "a_gain", [P, 3, HD])
                        cos = sb(c, "a_cos", [P, NT, HD])
                        sin = sb(c, "a_sin", [P, NT, HD])
                        u_ps = ps(c, "a_u_ps", [P, 2, SEQ])
                        t_ps = ps(c, "a_t_ps", [P, 2, SEQ])
                        w = a["w_in"][layer]
                        units = []
                        for kv in range(2):
                            units.append(full_unit(w[:, A0 + kv * P:A0 + (kv + 1) * P]))
                            units.append(([(lambda w_, j=j: w_[:, :, j * HD:(j + 1) * HD],
                                            w[:, A0 + (4 + 2 * j + kv) * HD:A0 + (5 + 2 * j + kv) * HD]
                                            .rearrange("(k p) n -> p k n", p=P)) for j in range(2)], FULL))
                        back = [[t_ps[:, 0, :], t_ps[:, 1, :], u_ps[:, 0, :]],
                                [u_ps[:, 0, :], u_ps[:, 1, :], t_ps[:, 0, :]]]

                        def dst_h(kv, h):
                            return q_h[:, 2 * kv + h, :] if h < 2 else k_s[:, kv, :]

                        def v_part(t):
                            return t.rearrange("p (t d) -> p t d", t=NT)

                        @block.sync
                        def _(sp):
                            load_weights(sp, ring, units)
                            for dst, name in ((cos, "cos_a"), (sin, "sin_a")):
                                sp.dma_start(dst[:, :, :], a[name].rearrange("(t p) d -> p t d", p=P)) \
                                    .then_inc(S["const_landed"], 16)
                            for h in range(3):
                                sp.dma_start(gain[:, h, :], row_vector(vec("a_k_norm" if h == 2 else "a_q_norm"))) \
                                    .then_inc(S["const_landed"], 16)
                            src = bass.AP(rel_scratch.tensor, layer * REL_ROW + (REL_PAD + NA_C - GRID_W),
                                          [[REL_C, NHEAD * REL_R], [0, GRID_W], [1, SKEW]])
                            sp.dma_start(skew[layer], src).then_inc(skew_landed, 16)

                        @block.gpsimd
                        def _(pool):
                            for u in range(4):
                                split_lo(pool, ring, units, u)

                        @block.tensor
                        def _(pe):
                            def turn(u):
                                pe.wait_ge(S["gemm_out"], u + 1)
                                if u >= 2:
                                    pe.wait_ge(S["lo_done"], u - 1)
                                turn_values(pe, t_ps, u_sb, u % 2).then_inc(S["tt_done"], 1)

                            def turn_back(kv):
                                pe.wait_ge(S["prep_done"], 3 * kv + 1)
                                pe.wait_ge(S["gemm_out"], 3 + kv)
                                if kv == 1:
                                    pe.wait_ge(S["lo_done"], 3)
                                for h in range(3):
                                    pe.wait_ge(S["prep_done"], 3 * kv + h + 1)
                                    transposes(pe, back[kv][h], lambda t: res[:, t, h].rearrange("p a d -> p (a d)")) \
                                        .then_inc(S["ptr_done"], 1)

                            def product(u, before):
                                if u >= 2:
                                    pe.wait_ge(S["gemm_out"], u - 1)
                                products(pe, u_ps[:, u % 2, :], ring, units, u, h_hi, h_lo, before=before)

                            product(0, {})
                            product(1, {HEAD: lambda: turn(0)})
                            product(2, {HEAD: lambda: turn(1)})
                            product(3, {KT - 1: lambda: turn_back(0)})
                            turn(2)
                            turn(3)
                            turn_back(1)

                        @block.scalar
                        def _(act):
                            def unit_out(u):
                                act.wait_ge(S["gemm_done"], u + 1)
                                if u >= 2:
                                    act.wait_ge(S["tt_done"], u - 1)
                                nc.scalar.activation(u_sb[:, u % 2, :], u_ps[:, u % 2, :], ACT.Copy) \
                                    .then_inc(S["gemm_out"], 1)

                            def value_hi(kv):
                                act.wait_ge(S["tt_done"], 2 * kv + 2)
                                nc.scalar.activation(v_s[:, kv, :, 0:HD], v_part(t_ps[:, 1, :])[:, :, HD:P],
                                                     ACT.Copy).then_inc(S["tt_hi"], 1)

                            def mean_root(kv):
                                act.wait_ge(S["square_done"], kv + 1)
                                root(act, ss[:, kv, :], HD).then_inc(S["root_done"], 1)

                            def back_hi(kv):
                                for h in range(3):
                                    act.wait_ge(S["ptr_done"], 3 * kv + h + 1)
                                    nc.scalar.activation(dst_h(kv, h), back[kv][h], ACT.Copy,
                                                         scale=HD ** -0.5 if h < 2 else 1.0).then_inc(S["hi_done"], 1)

                            split_hi(act, ring, units, 0)
                            split_hi(act, ring, units, 1)
                            unit_out(0)
                            split_hi(act, ring, units, 2)
                            unit_out(1)
                            split_hi(act, ring, units, 3)
                            value_hi(0)
                            mean_root(0)
                            unit_out(2)
                            back_hi(0)
                            unit_out(3)
                            value_hi(1)
                            mean_root(1)
                            back_hi(1)

                        @block.vector
                        def _(dve):
                            step = [0]

                            def after(ins):
                                step[0] += 1
                                ins.then_inc(S["dve_step"], 1)
                                dve.wait_ge(S["dve_step"], step[0])

                            flat = tok[:, :, :, :].rearrange("p t h d -> p (t h) d")
                            by_token = tok[:, :, :, :].rearrange("p t h d -> p t (h d)")
                            sq_flat = sq[:, :, :, :].rearrange("p t h d -> p (t h) d")

                            for kv in range(2):
                                dve.wait_ge(S["tt_done"], 2 * kv + 1)
                                nc.vector.tensor_copy(tok[:, :, 0:2, :].rearrange("p t h d -> p t (h d)"),
                                                      v_part(t_ps[:, 0, :])).then_inc(S["dve_step"], 1)
                                dve.wait_ge(S["tt_hi"], kv + 1)
                                nc.vector.tensor_copy(tok[:, :, 2, :], v_part(t_ps[:, 1, :])[:, :, 0:HD]) \
                                    .then_inc(S["dve_step"], 1)
                                nc.vector.tensor_tensor(v_s[:, kv, :, HD:P], v_part(t_ps[:, 1, :])[:, :, HD:P],
                                                        v_s[:, kv, :, 0:HD], ALU.subtract)
                                step[0] += 2
                                dve.wait_ge(S["dve_step"], step[0])
                                after(nc.vector.tensor_tensor(sq_flat, flat, flat, ALU.mult))
                                nc.vector.tensor_reduce(ss[:, kv, :], sq_flat, AX_X, ALU.add).then_inc(S["square_done"], 1)
                                dve.wait_ge(S["square_done"], kv + 1)
                                dve.wait_ge(S["const_landed"], 80)
                                gb = gain[:, :, :].rearrange("p h d -> p (h d)").unsqueeze(1).to_broadcast([P, NT, 3 * HD])
                                after(nc.vector.tensor_tensor(by_token, by_token, gb, ALU.mult))
                                dve.wait_ge(S["root_done"], kv + 1)
                                step[0] = rstd(dve, ss[:, kv, :], step[0])
                                after(nc.vector.tensor_tensor(flat, flat, ss[:, kv, :].unsqueeze(2)
                                                              .to_broadcast([P, NT * 3, HD]), ALU.mult))
                                q4 = HD // 4
                                for d0 in range(0, HD, 2 * q4):
                                    for f, g in ((d0, d0 + q4), (d0 + q4, d0)):
                                        nc.vector.tensor_tensor(
                                            rot[:, :, :, f:f + q4], tok[:, :, :, g:g + q4],
                                            sin[:, :, f:f + q4].unsqueeze(2).to_broadcast([P, NT, 3, q4]), ALU.mult) \
                                            .then_inc(S["dve_step"], 1)
                                        step[0] += 1
                                dve.wait_ge(S["dve_step"], step[0])
                                after(nc.vector.tensor_tensor(tok[:, :, :, :], tok[:, :, :, :],
                                                              cos[:, :, :].unsqueeze(2).to_broadcast([P, NT, 3, HD]), ALU.mult))
                                if kv == 1:
                                    dve.wait_ge(S["ptr_done"], 3)
                                for h in range(3):
                                    for j in range(2):
                                        last = nc.vector.tensor_tensor(res[:, :, h, j, :], tok[:, :, h, :],
                                                                       rot[:, :, h, :], ALU.add)
                                    last.then_inc(S["prep_done"], 1)
                                for h in range(2):
                                    dve.wait_ge(S["hi_done"], 3 * kv + h + 1)
                                    nc.vector.scalar_tensor_tensor(out=q_l[:, 2 * kv + h, :], in0=back[kv][h],
                                                                   scalar=HD ** -0.5, in1=dst_h(kv, h), op0=ALU.mult,
                                                                   op1=ALU.subtract).then_inc(S["lo_done"], 1)
                                dve.wait_ge(S["hi_done"], 3 * kv + 3)
                                nc.vector.tensor_tensor(k_s[HD:P, kv, :], back[kv][2][HD:P, :], k_s[HD:P, kv, :],
                                                        ALU.subtract).then_inc(S["lo_done"], 1)
                    end_stage()
                    maps = [([lambda i, m=m: q_h[:, m, i * P:(i + 1) * P], lambda i, m=m: q_l[:, m, i * P:(i + 1) * P]],
                             [lambda x0, x1, m=m: k_s[:, m // 2, x0:x1]] * 2, v_s[:, m // 2]) for m in range(4)]
                    attention_stage("a", maps, [(0, NT, None)] * NT, lambda m: slice(m * HD, (m + 1) * HD), mix)

                def pair_stage(tag, c0, pair, scale, stack, v_s, extra_dma, extra_act, extra_dve):
                    with ExitStack() as c, nc.Block() as block:
                        ring = weight_ring(c, tag)
                        p_h = sb(c, f"{tag}_p_h", [P, 2, SEQ], F32R)
                        p_l = sb(c, f"{tag}_p_l", [P, 2, SEQ], F32R)
                        u_sb = sb(c, f"{tag}_u", [P, 2, HALF])
                        u_ps = ps(c, f"{tag}_u_ps", [P, 3, SEQ])
                        t_ps = ps(c, f"{tag}_t_ps", [P, 2, HALF])

                        def v_half(n, d0, d1):
                            return v_s[:, n * (NT // 2):(n + 1) * (NT // 2), :, d0:d1]

                        def turned(n):
                            return t_ps[:, n, :].rearrange("p (t h d) -> p t h d", t=NT // 2, h=2)

                        w = a["w_in"][layer]
                        units = [full_unit(w[:, bass.ds(pair * P + (c0 + j * 4 * HD), P)]) for j in range(3)]

                        @block.sync
                        def _(sp):
                            load_weights(sp, ring, units)
                            extra_dma(sp)
                            sent = 0
                            for j in range(2):
                                copies = stack(p_h[:, j], p_l[:, j], j == 1)
                                copies.sort(key=lambda copy: copy[2])
                                sent += len(copies)
                                sp.wait_ge(S["hi_done"], j + 1)
                                for i, (dst, src, is_lo) in enumerate(copies):
                                    if is_lo and not copies[i - 1][2]:
                                        sp.wait_ge(S["lo_done"], j + 1)
                                    sp.dma_start(dst.bitcast(F32), src.bitcast(F32)).then_inc(S["stack_landed"], 16)
                            sp.wait_ge(S["stack_landed"], 16 * sent)

                        @block.gpsimd
                        def _(pool):
                            for u in range(3):
                                split_lo(pool, ring, units, u)

                        @block.tensor
                        def _(pe):
                            def turn(n):
                                pe.wait_ge(S["gemm_out"], n + 1)
                                transposes(pe, t_ps[:, n, :], lambda t: u_sb[:, n, t * P:(t + 1) * P], NT // 2) \
                                    .then_inc(S["tt_done"], 1)

                            for u in range(2):
                                products(pe, u_ps[:, u, :], ring, units, u, h_hi, h_lo)
                            half_products(pe, u_ps[:, 2, :], ring, units, 2, h_hi, h_lo, 0)
                            half_products(pe, u_ps[:, 2, :], ring, units, 2, h_hi, h_lo, 1, {KT // 2: lambda: turn(0)})
                            turn(1)

                        @block.scalar
                        def _(act):
                            split_hi(act, ring, units, 0)
                            split_hi(act, ring, units, 1)
                            extra_act(act)
                            act.wait_ge(S["gemm_done"], 1)
                            nc.scalar.activation(p_h[:, 0, :], u_ps[:, 0, :], ACT.Copy, scale=scale) \
                                .then_inc(S["hi_done"], 1)
                            split_hi(act, ring, units, 2)
                            act.wait_ge(S["gemm_done"], 2)
                            nc.scalar.activation(p_h[:, 1, :], u_ps[:, 1, :], ACT.Copy).then_inc(S["hi_done"], 1)
                            for n in range(2):
                                act.wait_ge(S["gemm_done"], 3 + n)
                                nc.scalar.activation(u_sb[:, n, :], u_ps[:, 2, n * HALF:(n + 1) * HALF], ACT.Copy) \
                                    .then_inc(S["gemm_out"], 1)
                                act.wait_ge(S["tt_done"], n + 1)
                                nc.scalar.activation(v_half(n, 0, HD), turned(n), ACT.Copy).then_inc(S["tt_hi"], 1)

                        @block.vector
                        def _(dve):
                            extra_dve[0](dve)
                            for j in range(2):
                                if j == 1:
                                    extra_dve[1](dve)
                                dve.wait_ge(S["hi_done"], j + 1)
                                nc.vector.scalar_tensor_tensor(out=p_l[:, j, :], in0=u_ps[:, j, :],
                                                               scalar=1.0 if j else scale, in1=p_h[:, j, :],
                                                               op0=ALU.mult, op1=ALU.subtract).then_inc(S["lo_done"], 1)
                            for n in range(2):
                                dve.wait_ge(S["tt_hi"], n + 1)
                                nc.vector.tensor_tensor(v_half(n, HD, P), turned(n), v_half(n, 0, HD), ALU.subtract)
                    end_stage()

                with ExitStack() as cc:
                    lam = sb(cc, "lam", [P, 1])
                    nd = sb(cc, "distance", [P, 2 * SEQ - P])
                    lv = sb(cc, "lam_vec", [P, 4, HD // 2])
                    lj = sb(cc, "lam_junk", [P, HD // 2])
                    ls = sb(cc, "lam_sum", [P, 2])
                    li = sb(cc, "lam_init", [P, 2])

                    with nc.Fori(0, 2) as pair, ExitStack() as ch:
                        qs = sb(ch, "c_q_s", [P, 4, SEQ], F32R)
                        ks = sb(ch, "c_k_s", [P, 4, SEQ], F32R)
                        v_s = sb(ch, "c_v_s", [P, NT, 2, P], F32R)
                        alibi = sb(ch, "alibi", [P, 2, 2 * SEQ - P])
                        slope = sb(ch, "slope", [P, 2])
                        W = HD // 2

                        def stack(hi, lo, is_k):
                            order = (0, 1, 0, 1) if is_k else (0, 0, 1, 1)
                            dst = ks if is_k else qs
                            return [(dst[r * W:(r + 1) * W, m, :], (hi, lo)[is_lo][m * W:(m + 1) * W, :], is_lo)
                                    for m in range(4) for r, is_lo in enumerate(order)]

                        def extra_dma(sp):
                            sp.dma_start(nd[:, :], a["distance"]).then_inc(S["const_landed"], 16)
                            sp.dma_start(slope[:, :], row_vector(a["slopes"][:, bass.ds(pair * 2, 2)])) \
                                .then_inc(S["const_landed"], 16)
                            sp.dma_start(li[:, :], row_vector(vec("lambda_init"))).then_inc(S["gain_landed"], 16)
                            for j, name in enumerate(("c_lambda_q1", "c_lambda_k1", "c_lambda_q2", "c_lambda_k2")):
                                sp.dma_start(lv[:, j, :], row_vector(vec(name))).then_inc(S["gain_landed"], 16)

                        def biases(act):
                            act.wait_ge(S["const_landed"], 32)
                            for j in range(2):
                                nc.scalar.activation(alibi[:, j, :], nd[:, :], ACT.Copy, scale=slope[:, j:j + 1])
                            act.wait_ge(S["dve_step"], 2)
                            nc.scalar.activation(ls[:, :], ls[:, :], ACT.Exp).then_inc(S["exp_done"], 1)

                        def lambda_sums(dve):
                            dve.wait_ge(S["gain_landed"], 80)
                            for j in range(2):
                                nc.vector.tensor_tensor_reduce(out=lj[:, :], in0=lv[:, 2 * j, :], in1=lv[:, 2 * j + 1, :],
                                                               scale=1.0, scalar=0.0, op0=ALU.mult, op1=ALU.add,
                                                               accum_out=ls[:, j:j + 1]).then_inc(S["dve_step"], 1)
                                dve.wait_ge(S["dve_step"], j + 1)

                        def lambda_difference(dve):
                            dve.wait_ge(S["exp_done"], 1)
                            nc.vector.tensor_tensor(lam[:, :], ls[:, 1:2], ls[:, 0:1], ALU.subtract) \
                                .then_inc(S["dve_step"], 1)
                            dve.wait_ge(S["dve_step"], 3)
                            nc.vector.tensor_tensor(lam[:, :], lam[:, :], li[:, 0:1], ALU.subtract)

                        pair_stage("c", C0, pair, -W ** -0.5, stack, v_s, extra_dma, biases,
                                   (lambda_sums, lambda_difference))
                        maps = [([lambda i, m=m: qs[:, m, i * P:(i + 1) * P]],
                                 [lambda x0, x1, m=m: ks[:, m, x0:x1]], v_s[:, :, m // 2, :]) for m in range(4)]
                        tiles = [(0, NT, lambda m, i=i: alibi[:, m // 2, (SEQ - P) - i * P:(SEQ - P) - i * P + SEQ])
                                 for i in range(NT)]
                        attention_stage("c", maps, tiles, lambda j: bass.ds(pair * P + (8 * HD + j * HD), HD),
                                        mix, combine=lam[:, 0:1])

                with nc.Fori(0, 2) as pair, ExitStack() as ch:
                    qh = sb(ch, "d_q_h", [P, 2, SEQ], F32R)
                    ql = sb(ch, "d_q_l", [P, 2, SEQ], F32R)
                    ks = sb(ch, "d_k_s", [P, 2, SEQ], F32R)
                    v_s = sb(ch, "d_v_s", [P, NT, 2, P], F32R)
                    edge = sb(ch, "bias_edge", [P, 2, REL_R + 1, GRID_W])
                    inner = sb(ch, "bias_inner", [P, 2, 10, GRID_W])
                    cmask = sb(ch, "cmask", [P, GRID_W])
                    rmask = sb(ch, "rmask", [P, 10])

                    def load_bias(sp):
                        sp.dma_start(cmask[:, :], a["col_mask"]).then_inc(S["const_landed"], 16)
                        sp.dma_start(rmask[:, :], a["row_mask"]).then_inc(S["const_landed"], 16)
                        sp.wait_ge(skew_landed, layer * 16 + 16)
                        sp.wait_ge(S["dve_step"], 1)
                        for r in range(2):
                            for h in range(2):
                                row = layer * (NHEAD * REL_R) + pair * (2 * REL_R) + h * REL_R
                                src = bass.AP(skew.tensor, row * (GRID_W * SKEW) + (GRID_W - 1),
                                              [[SKEW - 1, GRID_W], [GRID_W * SKEW, REL_R], [1, GRID_W]])
                                sp.dma_start(edge[r * GRID_W:(r + 1) * GRID_W, h, r:r + REL_R, :], src) \
                                    .then_inc(S["copy_landed"], 16)

                    def clear_bias(dve):
                        nc.vector.memset(edge[:, :, :, :], NEG).then_inc(S["dve_step"], 1)

                    def mask_bias(dve):
                        dve.wait_ge(S["const_landed"], 32)
                        dve.wait_ge(S["copy_landed"], 16 * 4)
                        e = edge[:, :, :, :].rearrange("p h r k -> p (h r) k")
                        nc.vector.scalar_tensor_tensor(out=e, in0=e, scalar=-1.0, in1=cmask[:, :].unsqueeze(1)
                                                       .to_broadcast([P, 2 * (REL_R + 1), GRID_W]),
                                                       op0=ALU.mult, op1=ALU.add).then_inc(S["dve_step"], 1)
                        dve.wait_ge(S["dve_step"], 2)
                        for h in range(2):
                            nc.vector.tensor_tensor(inner[:, h], edge[:, h, 3:13, :],
                                                    rmask[:, :].unsqueeze(2).to_broadcast([P, 10, GRID_W]), ALU.add)

                    def stack(hi, lo, is_k):
                        out_ = []
                        for h in range(2):
                            s = slice(h * HD, (h + 1) * HD)
                            for r in range(2):
                                d = slice(r * HD, (r + 1) * HD)
                                if is_k:
                                    out_.append((ks[d, h, :], (hi, lo)[r][s, :], r))
                                else:
                                    out_ += [(qh[d, h, :], hi[s, :], 0), (ql[d, h, :], lo[s, :], 1)]
                        return out_

                    pair_stage("d", D0, pair, -HD ** -0.5, stack, v_s, load_bias, lambda act: None,
                               (clear_bias, mask_bias))

                    maps = [([lambda i, h=h: qh[:, h, i * P:(i + 1) * P], lambda i, h=h: ql[:, h, i * P:(i + 1) * P]],
                             [lambda x0, x1, h=h: ks[:, h, x0:x1]] * 2, v_s[:, :, h, :]) for h in range(2)]

                    def bias(i):
                        r = {0: 7, 1: 5, 6: 3, 7: 1}.get(i)
                        if r is None:
                            return lambda m: inner[:, m].rearrange("p r k -> p (r k)")
                        return lambda m: edge[:, m, r:r + NA_R, :].rearrange("p r k -> p (r k)")

                    tiles = [((0 if i < 2 else 4 if i > 5 else i - 2), (5 if 2 <= i <= 5 else 4), bias(i))
                             for i in range(NT)]
                    attention_stage("d", maps, tiles, lambda m: bass.ds(pair * P + (12 * HD + m * HD), HD), mix)

                with ExitStack() as cb:
                    cq_h = sb(cb, "cq_h", [P, 2, SEQ], F32R)
                    cq_l = sb(cb, "cq_l", [P, 2, SEQ], F32R)
                    ckv_h = sb(cb, "ckv_h", [P, 1, SEQ], F32R)
                    ckv_l = sb(cb, "ckv_l", [P, 1, SEQ], F32R)
                    kr_h = sb(cb, "b_kr_h", [P, SEQ], F32R)
                    kr_l = sb(cb, "b_kr_l", [P, SEQ], F32R)
                    R0, R1 = HD, HD + B_ROPE
                    raw = sb(cb, "bh_w_raw", [P, 3, NHEAD, P])
                    w_h = sb(cb, "bh_w_h", [P, 3, NHEAD, P], F32R)
                    w_l = sb(cb, "bh_w_l", [P, 3, NHEAD, P], F32R)
                    w_rows = (P, HD, P)
                    wq = a["b_w_uq"][layer].rearrange("r (e q) -> r e q", e=NHEAD)
                    wkv = a["b_w_ukv"][layer].rearrange("r (e q) -> r e q", e=NHEAD)
                    QK = HD + B_ROPE
                    with ExitStack() as c, nc.Block() as block:
                        ring = weight_ring(c, "b")
                        k_rope = sb(c, "k_rope", [P, SEQ])
                        cs = sb(c, "cos_sin", [P, SEQ])
                        u_sb = sb(c, "b_u", [P, 3, SEQ])
                        sq = sb(c, "b_sq", [P, 3, SEQ])
                        r_tok = sb(c, "b_r", [P, 2, NT])
                        g_col = sb(c, "b_g", [P, 3])
                        rt = sb(c, "b_rt", [P, SEQ])
                        u_ps = ps(c, "b_u_ps", [P, 2, SEQ])
                        sum_ps = ps(c, "b_sum_ps", [P, 2, NT])
                        r_ps = ps(c, "b_r_ps", [P, SEQ])
                        w = a["w_in"][layer]

                        def cols(c0, n):
                            return w[:, c0:c0 + n].rearrange("(k p) n -> p k n", p=P)

                        half = B_ROPE // 2
                        kr = B0 + B_Q + B_KV
                        units = [full_unit(w[:, B0:B0 + P]),
                                 ([(lambda w_: w_[:, :, 0:HD], cols(B0 + P, HD)),
                                   (lambda w_: w_[:, :, R0:R1], cols(kr, B_ROPE)),
                                   (lambda w_: w_[:, :, R1:R1 + half], cols(kr + half, half)),
                                   (lambda w_: w_[:, :, R1 + half:P], cols(kr, half))], FULL),
                                 full_unit(w[:, B0 + B_Q:B0 + B_Q + P])]

                        @block.sync
                        def _(sp):
                            load_weights(sp, ring, units)
                            for k, rows in enumerate(w_rows[0:2]):
                                for d0, d1, c0 in ((0, QK, 0), (QK, QK + half, HD + half), (QK + half, P, HD)):
                                    sp.dma_start(raw[0:rows, k, :, d0:d1], wq[k * P:k * P + rows, :, c0:c0 + d1 - d0]) \
                                        .then_inc(S["copy_landed"], 16)
                            sp.dma_start(raw[:, 2, :, :], wkv).then_inc(S["copy_landed"], 16)
                            sp.dma_start(cs[HD:P, :], a["cos_sin_b"]).then_inc(S["const_landed"], 16)
                            col = lambda v: v.rearrange("a p -> p a")
                            sp.dma_start(g_col[:, 0:1], col(vec("b_cq_norm", 0, P))).then_inc(S["const_landed"], 16)
                            sp.dma_start(g_col[0:HD, 1:2], col(vec("b_cq_norm", P, B_Q))).then_inc(S["const_landed"], 16)
                            sp.dma_start(g_col[:, 2:3], col(vec("b_ckv_norm"))).then_inc(S["const_landed"], 16)

                        @block.gpsimd
                        def _(pool):
                            for u in range(3):
                                split_lo(pool, ring, units, u)
                            for k, rows in enumerate(w_rows):
                                pool.wait_ge(S["q_hi"], k + 1)
                                nc.gpsimd.tensor_tensor(w_l[0:rows, k, :, :], raw[0:rows, k, :, :],
                                                        w_h[0:rows, k, :, :], ALU.subtract)

                        @block.tensor
                        def _(pe):
                            def sums(r):
                                rows_of = (((0, P), (1, HD)), ((2, P),))[r]
                                pe.wait_ge(S["square_done"], 2 + r)
                                for t in range(NT):
                                    for j, (u, rows) in enumerate(rows_of):
                                        last = nc.tensor.matmul(sum_ps[:, r, t:t + 1], sq[0:rows, u, t * P:(t + 1) * P],
                                                                ones[0:rows, 0:1], start=(j == 0),
                                                                stop=(j == len(rows_of) - 1))
                                last.then_inc(S["pe_step"], 1)

                            def spread(r):
                                pe.wait_ge(S["yroot_done"], r + 1)
                                if r:
                                    pe.wait_ge(S["norm_done"], 2)
                                transposes(pe, r_ps, lambda t: r_tok[:, r, t:t + 1].to_broadcast([P, P])) \
                                    .then_inc(S["tr_done"], 1)

                            for u in range(3):
                                if u == 2:
                                    pe.wait_ge(S["gemm_out"], 1)
                                    pe.wait_ge(S["square_done"], 1)
                                products(pe, u_ps[:, u % 2, :], ring, units, u, h_hi, h_lo,
                                         before={KT // 2: lambda: sums(0), KT - 2: lambda: spread(0)} if u == 2 else {})
                            sums(1)
                            spread(1)

                        @block.scalar
                        def _(act):
                            def unit_out(u):
                                act.wait_ge(S["gemm_done"], u + 1)
                                nc.scalar.activation(u_sb[:, u, :], u_ps[:, u % 2, :], ACT.Copy).then_inc(S["gemm_out"], 1)
                                nc.scalar.activation(sq[:, u, :], u_ps[:, u % 2, :], ACT.Square) \
                                    .then_inc(S["square_done"], 1)

                            def mean_root(r, width):
                                act.wait_ge(S["pe_step"], r + 1)
                                nc.scalar.activation(r_tok[:, r, :], sum_ps[:, r, :], ACT.Sqrt, scale=1.0 / width,
                                                     bias=eps_col[:, 0:1]).then_inc(S["root_done"], 1)

                            def high(j, dst):
                                act.wait_ge(S["norm_done"], j + 1)
                                nc.scalar.activation(dst, u_sb[0:dst.shape[0], j, :], ACT.Copy).then_inc(S["hi_done"], 1)

                            split_hi(act, ring, units, 0)
                            split_hi(act, ring, units, 1)
                            unit_out(0)
                            split_hi(act, ring, units, 2)
                            act.wait_ge(S["copy_landed"], 16 * 7)
                            for k, rows in enumerate(w_rows):
                                nc.scalar.activation(w_h[0:rows, k, :, :], raw[0:rows, k, :, :], ACT.Copy) \
                                    .then_inc(S["q_hi"], 1)
                            unit_out(1)
                            act.wait_ge(S["rope_done"], 1)
                            nc.scalar.activation(kr_h[R0:R1, :], k_rope[R0:R1, :], ACT.Copy).then_inc(S["k_hi"], 1)
                            mean_root(0, B_Q)
                            unit_out(2)
                            mean_root(1, B_KV)
                            high(0, cq_h[:, 0, :])
                            high(1, cq_h[0:HD, 1, :])
                            high(2, ckv_h[:, 0, :])

                        @block.vector
                        def _(dve):
                            dve.wait_ge(S["const_landed"], 64)
                            dve.wait_ge(S["gemm_out"], 2)
                            nc.vector.tensor_tensor(k_rope[R0:R1, :], u_sb[R0:R1, 1, :], cs[R0:R1, :],
                                                    ALU.mult).then_inc(S["prep_done"], 1)
                            nc.vector.tensor_tensor(rt[R0:R1, :], u_sb[R1:P, 1, :], cs[R1:P, :],
                                                    ALU.mult).then_inc(S["prep_done"], 1)
                            dve.wait_ge(S["prep_done"], 2)
                            nc.vector.tensor_tensor(k_rope[R0:R1, :], k_rope[R0:R1, :], rt[R0:R1, :], ALU.add) \
                                .then_inc(S["rope_done"], 1)
                            dve.wait_ge(S["k_hi"], 1)
                            nc.vector.tensor_tensor(kr_l[R0:R1, :], k_rope[R0:R1, :], kr_h[R0:R1, :], ALU.subtract)
                            for r in range(2):
                                dve.wait_ge(S["root_done"], r + 1)
                                nc.vector.reciprocal(r_tok[:, r, :], r_tok[:, r, :]).then_inc(S["yroot_done"], 1)
                                dve.wait_ge(S["tr_done"], r + 1)
                                for u, rows in (((0, P), (1, HD)) if r == 0 else ((2, P),)):
                                    nc.vector.scalar_tensor_tensor(out=u_sb[0:rows, u, :], in0=u_sb[0:rows, u, :],
                                                                   scalar=g_col[0:rows, u:u + 1], in1=r_ps[0:rows, :],
                                                                   op0=ALU.mult, op1=ALU.mult) \
                                        .then_inc(S["norm_done"], 1)
                            for j, (hi, lo) in enumerate(((cq_h[:, 0, :], cq_l[:, 0, :]),
                                                          (cq_h[0:HD, 1, :], cq_l[0:HD, 1, :]),
                                                          (ckv_h[:, 0, :], ckv_l[:, 0, :]))):
                                dve.wait_ge(S["hi_done"], j + 1)
                                nc.vector.tensor_tensor(lo, u_sb[0:hi.shape[0], j, :], hi, ALU.subtract)
                    end_stage()

                    with ExitStack() as ch:
                        q_h, k_h = h_hi[:, 0:NHEAD, :], h_hi[:, NHEAD:2 * NHEAD, :]
                        q_l, k_l = h_lo[:, 0:NHEAD, :], h_lo[:, NHEAD:2 * NHEAD, :]
                        v_s = sb(ch, "b_v_s", [P, NHEAD, NT, P], F32R)
                        with ExitStack() as c, nc.Block() as block:
                            u_sb = sb(c, "bh_u", [P, 2 * NHEAD, SEQ])
                            rt = sb(c, "bh_rt", [P, 2, SEQ])
                            cs = sb(c, "bh_cos_sin", [P, SEQ])
                            u_ps = ps(c, "bh_u_ps", [P, 2, SEQ])
                            t_ps = ps(c, "bh_t_ps", [P, 2, SEQ])

                            def values_of(t):
                                return t.rearrange("p (t d) -> p t d", t=NT)[:, :, HD:P]

                            @block.sync
                            def _(sp):
                                sp.dma_start(cs[HD:P, :], a["cos_sin_b"]).then_inc(S["const_landed"], 16)
                                for e in range(NHEAD):
                                    for dst, src in ((k_h, kr_h), (k_l, kr_l)):
                                        sp.dma_start(dst[R0:R1, e, :].bitcast(F32), src[R0:R1, :].bitcast(F32)) \
                                            .then_inc(S["stack_landed"], 16)
                                sp.wait_ge(S["stack_landed"], 16 * 2 * NHEAD)

                            @block.gpsimd
                            def _(pool):
                                pool.wait_ge(S["const_landed"], 16)
                                for e in range(NHEAD):
                                    pool.wait_ge(S["gemm_out"], 2 * e + 1)
                                    if e >= 1:
                                        pool.wait_ge(S["swap_done"], e)
                                    if e >= 2:
                                        pool.wait_ge(S["rope_done"], e - 1)
                                    nc.gpsimd.tensor_tensor(rt[R0:R1, e % 2, :], u_sb[R1:P, 2 * e, :], cs[R1:P, :],
                                                            ALU.mult).then_inc(S["swap_done"], 1)

                            @block.tensor
                            def _(pe):
                                def turn(e):
                                    pe.wait_ge(S["gemm_out"], 2 * e + 2)
                                    if e >= 2:
                                        pe.wait_ge(S["tt_lo"], e - 1)
                                    transposes(pe, t_ps[:, e % 2, :], lambda t: u_sb[:, 2 * e + 1, t * P:(t + 1) * P]) \
                                        .then_inc(S["tt_done"], 1)

                                for e in range(NHEAD):
                                    if e:
                                        pe.wait_ge(S["gemm_out"], 2 * e - 1)
                                    for k in range(2):
                                        rows = w_rows[k]
                                        last = part_products(u_ps[:, 0, :], w_h[0:rows, k, e, :], w_l[0:rows, k, e, :],
                                                             cq_h[0:rows, k, :], cq_l[0:rows, k, :], k == 0, k == 1)
                                    last.then_inc(S["gemm_done"], 1)
                                    if e:
                                        turn(e - 1)
                                        pe.wait_ge(S["k_lo"], e)
                                    part_products(u_ps[:, 1, :], w_h[:, 2, e, :], w_l[:, 2, e, :], ckv_h[:, 0, :],
                                                  ckv_l[:, 0, :], True, True).then_inc(S["gemm_done"], 1)
                                turn(NHEAD - 1)

                            @block.scalar
                            def _(act):
                                def query_out(e):
                                    act.wait_ge(S["gemm_done"], 2 * e + 1)
                                    nc.scalar.activation(u_sb[:, 2 * e, :], u_ps[:, 0, :], ACT.Copy, scale=QK ** -0.5) \
                                        .then_inc(S["gemm_out"], 1)

                                def key_value_out(e):
                                    act.wait_ge(S["gemm_done"], 2 * e + 2)
                                    nc.scalar.activation(u_sb[:, 2 * e + 1, :], u_ps[:, 1, :], ACT.Copy) \
                                        .then_inc(S["gemm_out"], 1)
                                    nc.scalar.activation(k_h[0:HD, e, :], u_ps[0:HD, 1, :], ACT.Copy) \
                                        .then_inc(S["k_hi"], 1)

                                def value_hi(e):
                                    act.wait_ge(S["tt_done"], e + 1)
                                    nc.scalar.activation(v_s[:, e, :, 0:HD], values_of(t_ps[:, e % 2, :]), ACT.Copy) \
                                        .then_inc(S["tt_hi"], 1)

                                def query_hi(e):
                                    act.wait_ge(S["rope_done"], e + 1)
                                    nc.scalar.activation(q_h[0:QK, e, :], u_sb[0:QK, 2 * e, :], ACT.Copy) \
                                        .then_inc(S["q_hi"], 1)

                                for e in range(NHEAD + 1):
                                    if e < NHEAD:
                                        query_out(e)
                                        key_value_out(e)
                                    if e:
                                        value_hi(e - 1)
                                        query_hi(e - 1)

                            @block.vector
                            def _(dve):
                                def rope(e):
                                    dve.wait_ge(S["gemm_out"], 2 * e + 1)
                                    nc.vector.tensor_tensor(u_sb[R0:R1, 2 * e, :], u_sb[R0:R1, 2 * e, :], cs[R0:R1, :],
                                                            ALU.mult).then_inc(S["dve_step"], 1)
                                    dve.wait_ge(S["dve_step"], e + 1)
                                    dve.wait_ge(S["swap_done"], e + 1)
                                    nc.vector.tensor_tensor(u_sb[R0:R1, 2 * e, :], u_sb[R0:R1, 2 * e, :], rt[R0:R1, e % 2, :],
                                                            ALU.add).then_inc(S["rope_done"], 1)

                                def key_lo(e):
                                    dve.wait_ge(S["k_hi"], e + 1)
                                    nc.vector.tensor_tensor(k_l[0:HD, e, :], u_ps[0:HD, 1, :], k_h[0:HD, e, :],
                                                            ALU.subtract).then_inc(S["k_lo"], 1)

                                def value_lo(e):
                                    dve.wait_ge(S["tt_hi"], e + 1)
                                    nc.vector.tensor_tensor(v_s[:, e, :, HD:P], values_of(t_ps[:, e % 2, :]),
                                                            v_s[:, e, :, 0:HD], ALU.subtract).then_inc(S["tt_lo"], 1)

                                def query_lo(e):
                                    dve.wait_ge(S["q_hi"], e + 1)
                                    nc.vector.tensor_tensor(q_l[0:QK, e, :], u_sb[0:QK, 2 * e, :], q_h[0:QK, e, :],
                                                            ALU.subtract)

                                dve.wait_ge(S["const_landed"], 16)
                                for e in range(NHEAD + 1):
                                    if e < NHEAD:
                                        rope(e)
                                        key_lo(e)
                                    if e:
                                        value_lo(e - 1)
                                        query_lo(e - 1)
                        end_stage()

                        def b_map(e):
                            qh = lambda i: q_h[0:QK, e, i * P:(i + 1) * P]
                            ql = lambda i: q_l[0:QK, e, i * P:(i + 1) * P]
                            kh = lambda x0, x1: k_h[0:QK, e, x0:x1]
                            kl = lambda x0, x1: k_l[0:QK, e, x0:x1]
                            return ([qh, qh, ql], [kh, kl, kh], v_s[:, e])

                        attention_stage("b", [b_map(e) for e in range(NHEAD)], [(0, NT, None)] * NT,
                                        lambda m: slice((4 + m) * HD, (5 + m) * HD), mix)

                with ExitStack() as c, nc.Block() as block:
                    sq = sb(c, "m_sq", [P, 2, D])
                    ss = sb(c, "m_ss", [P, NT, 4, 4])
                    sg = sb(c, "m_sg", [P, NT, 4])
                    hn = sb(c, "m_hn", [P, 2, D])
                    g = sb(c, "m_g", [P, D])
                    li = sb(c, "m_li", [P, 2])
                    hg = sb(c, "m_hg", [P, 2, D])
                    h_ps = ps(c, "m_ps", [P, 2, D])
                    GW = 4 * HD

                    @block.sync
                    def _(sp):
                        for j, name in ((0, "g_out_a"), (1, "g_out_b"), (3, "g_out_d")):
                            sp.dma_start(g[:, j * GW:(j + 1) * GW], row_vector(vec(name))).then_inc(S["gain_landed"], 16)
                        for h in range(4):
                            sp.dma_start(g[:, 2 * GW + h * HD:2 * GW + (h + 1) * HD], row_vector(vec("g_out_c"))) \
                                .then_inc(S["gain_landed"], 16)
                        sp.dma_start(li[:, :], row_vector(vec("lambda_init"))).then_inc(S["gain_landed"], 16)

                    @block.scalar
                    def _(act):
                        for t in range(NT):
                            if t >= 2:
                                act.wait_ge(S["mix_sq"], t - 1)
                            nc.scalar.activation(sq[:, t % 2, :], mix[:, t, :], ACT.Square).then_inc(S["square_done"], 1)
                        act.wait_ge(S["dve_step"], 4)
                        root(act, ss[:, :, :, :].rearrange("p t m h -> p (t m h)"), HD).then_inc(S["root_done"], 1)
                        for t in range(NT):
                            act.wait_ge(S["tr_done"], t + 1)
                            nc.scalar.activation(h_hi[:, :, t * P:(t + 1) * P],
                                                 h_ps[:, t % 2, :].rearrange("p (k n) -> p k n", k=KT),
                                                 ACT.Copy).then_inc(S["hi_done"], 1)

                    @block.vector
                    def _(dve):
                        step = [0]

                        def after(ins):
                            step[0] += 1
                            ins.then_inc(S["dve_step"], 1)
                            dve.wait_ge(S["dve_step"], step[0])

                        for t in range(NT):
                            dve.wait_ge(S["square_done"], t + 1)
                            nc.vector.tensor_reduce(ss[:, t].rearrange("p m h -> p (m h)"),
                                                    sq[:, t % 2, :].rearrange("p (h d) -> p h d", d=HD),
                                                    AX_X, ALU.add).then_inc(S["mix_sq"], 1)
                        dve.wait_ge(S["mix_sq"], NT)
                        after(nc.vector.tensor_reduce(sg[:, :, :].rearrange("p t m -> p (t m)"),
                                                      ss[:, :, :, :].rearrange("p t m h -> p (t m) h"), AX_X, ALU.add))
                        for m in (0, 1, 3):
                            after(nc.vector.tensor_scalar(ss[:, :, m, :], sg[:, :, m].unsqueeze(2)
                                                          .to_broadcast([P, NT, 4]), 0.25, None, ALU.mult))
                        dve.wait_ge(S["root_done"], 1)
                        after(nc.vector.reciprocal(ss[:, :, :, :], ss[:, :, :, :]))
                        dve.wait_ge(S["gain_landed"], 16 * 8)
                        after(nc.vector.tensor_scalar(g[:, 2 * GW:3 * GW], g[:, 2 * GW:3 * GW], li[:, 1:2], None, ALU.mult))
                        for t in range(NT + 2):
                            if t < NT:
                                if t >= 2:
                                    dve.wait_ge(S["gain_done"], t - 1)
                                nc.vector.tensor_tensor(
                                    hn[:, t % 2, :].rearrange("p (h d) -> p h d", d=HD),
                                    mix[:, t, :].rearrange("p (h d) -> p h d", d=HD),
                                    ss[:, t].rearrange("p m h -> p (m h)").unsqueeze(2).to_broadcast([P, 16, HD]),
                                    ALU.mult).then_inc(S["norm_done"], 1)
                            if t >= 2:
                                s = t - 2
                                dve.wait_ge(S["hi_done"], s + 1)
                                nc.vector.tensor_tensor(h_lo[:, :, s * P:(s + 1) * P],
                                                        h_ps[:, s % 2, :].rearrange("p (k n) -> p k n", k=KT),
                                                        h_hi[:, :, s * P:(s + 1) * P], ALU.subtract) \
                                    .then_inc(S["lo_done"], 1)

                    @block.gpsimd
                    def _(pool):
                        pool.wait_ge(S["dve_step"], 6)
                        for t in range(NT):
                            pool.wait_ge(S["norm_done"], t + 1)
                            if t >= 2:
                                pool.wait_ge(S["tr_done"], t - 1)
                            nc.gpsimd.tensor_tensor(hg[:, t % 2, :], hn[:, t % 2, :], g[:, :], ALU.mult) \
                                .then_inc(S["gain_done"], 1)

                    @block.tensor
                    def _(pe):
                        for t in range(NT):
                            pe.wait_ge(S["gain_done"], t + 1)
                            if t >= 2:
                                pe.wait_ge(S["lo_done"], t - 1)
                            transposes(pe, h_ps[:, t % 2, :], lambda k: hg[:, t % 2, k * P:(k + 1) * P]) \
                                .then_inc(S["tr_done"], 1)
                end_stage()

            with ExitStack() as co:
                ft = sb(co, "mix_out_t", [P, KT, SEQ])
                with ExitStack() as c, nc.Block() as block:
                    ring = weight_ring(c, "o")
                    u_ps = ps(c, "o_ps", [P, 2, SEQ])
                    w = a["w_out"][layer]
                    units = [full_unit(w[:, m * P:(m + 1) * P]) for m in range(KT)]

                    @block.sync
                    def _(sp):
                        load_weights(sp, ring, units)

                    @block.gpsimd
                    def _(pool):
                        for u in range(KT):
                            split_lo(pool, ring, units, u)

                    @block.scalar
                    def _(act):
                        for u in range(KT):
                            split_hi(act, ring, units, u)

                    @block.tensor
                    def _(pe):
                        for u in range(KT):
                            if u >= 2:
                                pe.wait_ge(S["gemm_out"], u - 1)
                            products(pe, u_ps[:, u % 2, :], ring, units, u, h_hi, h_lo)

                    @block.vector
                    def _(dve):
                        for u in range(KT):
                            dve.wait_ge(S["gemm_done"], u + 1)
                            nc.vector.tensor_copy(ft[:, u, :], u_ps[:, u % 2, :]).then_inc(S["gemm_out"], 1)
                end_stage()
                norm_stage("mlp_pre", ft, vec("norm_mix_post"), vec("norm_mlp_pre"))

            with ExitStack() as co:
                ft = sb(co, "mlp_out_t", [P, KT, SEQ])
                with ExitStack() as c, nc.Block() as block:
                    ring = weight_ring(c, "m")
                    up_h = sb(c, "up_h", [P, KT, SEQ], F32R)
                    up_l = sb(c, "up_l", [P, KT, SEQ], F32R)
                    r_sb = sb(c, "m_relu", [P, SEQ])
                    s_sb = sb(c, "m_square", [P, SEQ])
                    u_ps = ps(c, "u_ps", [P, 2, SEQ])
                    NU = 2 * KT
                    CHUNKS = FF // FF_CHUNK

                    def chunk_units(chunk):
                        wu = a["w_up"][layer]
                        wd = a["w_down"][layer][bass.ds(chunk * FF_CHUNK, FF_CHUNK), :]
                        return [full_unit(wu[:, bass.ds(chunk * FF_CHUNK + j * P, P)]) for j in range(KT)] + \
                               [full_unit(wd[:, m * P:(m + 1) * P]) for m in range(KT)]

                    shapes = chunk_units(0)

                    @block.sync
                    def _(sp):
                        with sp.Fori(0, CHUNKS) as chunk:
                            load_weights(sp, ring, chunk_units(chunk), chunk)

                    @block.gpsimd
                    def _(pool):
                        pool.sem_inc(S["w_lo"], 2)
                        with pool.Fori(0, CHUNKS) as chunk:
                            for u in range(NU):
                                split_lo(pool, ring, shapes, u, chunk)

                    @block.tensor
                    def _(pe):
                        pe.sem_inc(S["gemm_done"], 2)
                        with pe.Fori(0, CHUNKS) as chunk:
                            for u in range(NU):
                                if 2 <= u < KT + 2:
                                    pe.wait_ge(S["relu_done"], chunk * KT + (u - 1))
                                else:
                                    pe.wait_ge(S["acc_done"], chunk * KT + (u + 1 if u < 2 else u + 1 - KT))
                                if u < KT:
                                    products(pe, u_ps[:, u % 2, :], ring, shapes, u, h_hi, h_lo, chunk)
                                else:
                                    if u == KT:
                                        pe.wait_ge(S["up_lo"], chunk * KT + (KT - 1))
                                    products(pe, u_ps[:, u % 2, :], ring, shapes, u, up_h, up_l, chunk,
                                             {KT - 1: lambda: pe.wait_ge(S["up_lo"], chunk * KT + KT)})

                    @block.scalar
                    def _(act):
                        with act.Fori(0, CHUNKS) as chunk:
                            def hi(u):
                                split_hi(act, ring, shapes, u, chunk)

                            hi(0)
                            for u in range(NU):
                                if u + 1 < NU:
                                    hi(u + 1)
                                if u < KT:
                                    act.wait_ge(S["gemm_done"], chunk * NU + (u + 3))
                                    nc.scalar.activation(r_sb[:, :], u_ps[:, u % 2, :], ACT.Relu) \
                                        .then_inc(S["relu_done"], 1)
                                    act.wait_ge(S["sq_done"], chunk * KT + (u + 1))
                                    nc.scalar.activation(up_h[:, u, :], s_sb[:, :], ACT.Copy).then_inc(S["up_hi"], 1)

                    @block.vector
                    def _(dve):
                        dve.sem_inc(S["acc_done"], 2)
                        nc.vector.memset(ft[:, :, :], 0.0).then_inc(S["zero_done"], 1)
                        dve.wait_ge(S["zero_done"], 1)
                        with dve.Fori(0, CHUNKS) as chunk:
                            for u in range(NU):
                                if u < KT:
                                    dve.wait_ge(S["relu_done"], chunk * KT + (u + 1))
                                    nc.vector.tensor_tensor(s_sb[:, :], r_sb[:, :], r_sb[:, :], ALU.mult) \
                                        .then_inc(S["sq_done"], 1)
                                    dve.wait_ge(S["up_hi"], chunk * KT + (u + 1))
                                    nc.vector.tensor_tensor(up_l[:, u, :], s_sb[:, :], up_h[:, u, :], ALU.subtract) \
                                        .then_inc(S["up_lo"], 1)
                                    dve.wait_ge(S["up_lo"], chunk * KT + (u + 1))
                                else:
                                    m = u - KT
                                    dve.wait_ge(S["gemm_done"], chunk * NU + (u + 3))
                                    dve.wait_ge(S["acc_done"], chunk * KT + (m + 2))
                                    nc.vector.tensor_tensor(ft[:, m, :], ft[:, m, :], u_ps[:, u % 2, :], ALU.add) \
                                        .then_inc(S["acc_done"], 1)
                end_stage()
                norm_stage("mlp_post", ft, vec("norm_mlp_post"), vec("norm_mix_next"))


_INS = ["x", "norm_mix_pre", "norm_mix_post", "norm_mlp_pre", "norm_mlp_post", "w_in", "a_q_norm", "a_k_norm",
        "b_cq_norm", "b_ckv_norm", "b_w_uq", "b_w_ukv", "c_lambda_q1", "c_lambda_k1", "c_lambda_q2",
        "c_lambda_k2", "d_rel_bias", "g_out_a", "g_out_b", "g_out_c", "g_out_d", "w_out", "w_up", "w_down"]


def kernel(**inputs):
    import concourse.bacc as _bacc
    from concourse.bass_utils import run_bass_kernel_spmd as _run

    nc = _bacc.Bacc("TRN2", target_bir_lowering=False, num_devices=1)
    arrays = {}
    for name in _INS:
        v = np.ascontiguousarray(inputs[name])
        if name == "x":
            v = v.reshape(SEQ, D)
        if name == "d_rel_bias":
            v = v.reshape(DEPTH, REL_N)
        arrays[name] = v
    arrays["norm_mix_next"] = np.ascontiguousarray(np.roll(arrays["norm_mix_pre"], -1, axis=0))
    arrays.update(shape_constants())
    aps = {n: nc.dram_tensor(f"in_{n}", v.shape, F32, kind="ExternalInput").ap() for n, v in arrays.items()}
    out = nc.dram_tensor("out_x", (SEQ, D), F32, kind="ExternalOutput").ap()
    build(nc, aps, out)
    r = _run(nc, [{f"in_{n}": v for n, v in arrays.items()}], core_ids=[0])
    return r.results[0]["out_x"].reshape(1, SEQ, D)
```
